# Optimizing a Trainium2 kernel written in Bass

```python
import jax, jax.numpy as jnp
from jax import lax
import numpy as np

D_MODEL = 1024
BATCH = 1
SEQ = 512
DEPTH = 2

CONV_WIDTH = 3
HEAD_DIM = 64
N_HEADS = D_MODEL // HEAD_DIM
N_KV_GROUPS = 4
HEADS_PER_GROUP = N_HEADS // N_KV_GROUPS
N_BRANCH = 3
N_KV_SLOTS = 2 * N_BRANCH
CMP_BLOCK = 32
CMP_STRIDE = 16
CMP_HIDDEN = 256
SLC_BLOCK = 64
N_SELECT = 16
WINDOW = 512
Q_BLOCK = 128
FORCE_BONUS = 1000.0
ROPE_THETA = 10000.0
N_GROUPS = 4
EXPERTS_PER_GROUP = 8
N_EXPERTS = N_GROUPS * EXPERTS_PER_GROUP
TOP_K_INNER = 2
D_EXPERT = D_MODEL // 2
DISPATCH_ROWS = 256
RMS_EPS = 1e-6

kernel_name = 'hybrid_shortconv_nsa_hmoe'

def rmsnorm(x, g):
    xf = x.astype(jnp.float32)
    y = xf * lax.rsqrt(jnp.mean(xf * xf, axis=-1, keepdims=True) + RMS_EPS)
    return (y * g.astype(jnp.float32)).astype(x.dtype)

def rope(t, positions):
    half = HEAD_DIM // 2
    inv = ROPE_THETA ** (-jnp.arange(half, dtype=jnp.float32) / half)
    ang = positions.astype(jnp.float32)[..., None] * inv
    cos = jnp.cos(ang)[:, :, None, :]
    sin = jnp.sin(ang)[:, :, None, :]
    t1 = t[..., :half].astype(jnp.float32)
    t2 = t[..., half:].astype(jnp.float32)
    return jnp.concatenate([t1 * cos - t2 * sin, t2 * cos + t1 * sin], axis=-1).astype(t.dtype)

def masked_softmax(s, mask):
    s = jnp.where(mask, s.astype(jnp.float32), -jnp.inf)
    m = jnp.max(s, axis=-1, keepdims=True)
    m = jnp.where(jnp.isfinite(m), m, 0.0)
    e = jnp.exp(s - m)
    d = jnp.sum(e, axis=-1, keepdims=True)
    return e / jnp.maximum(d, jnp.float32(1e-30))

def short_conv_mixer(h, w_in, conv_w, w_out):
    d = h.shape[-1]
    proj = h @ w_in
    b_gate, c_gate, v = jnp.split(proj, 3, axis=-1)
    u = c_gate * v
    y = lax.conv_general_dilated(
        u, conv_w.astype(u.dtype)[:, None, :], window_strides=(1,),
        padding=[(CONV_WIDTH - 1, 0)], dimension_numbers=('NWC', 'WIO', 'NWC'),
        feature_group_count=d)
    return (b_gate * y) @ w_out

def nsa_shared_kv(h, positions, w_kv, cmp_pos_k, cmp_w1_k, cmp_w2_k, cmp_pos_v, cmp_w1_v, cmp_w2_v):
    b, s, _ = h.shape
    kv = (h @ w_kv).reshape(b, s, N_KV_SLOTS, N_KV_GROUPS, HEAD_DIM)
    k_c, v_c, k_s, v_s, k_w, v_w = [kv[:, :, i] for i in range(N_KV_SLOTS)]
    k_s = rope(k_s, positions)
    k_w = rope(k_w, positions)
    n_cmp = (s - CMP_BLOCK) // CMP_STRIDE + 1
    idx = jnp.arange(n_cmp)[:, None] * CMP_STRIDE + jnp.arange(CMP_BLOCK)[None, :]

    def compress(t, pos, w1, w2):
        blk = t[:, idx] + pos[None, None, :, None, :]
        blk = blk.transpose(0, 1, 3, 2, 4).reshape(b, n_cmp, N_KV_GROUPS, CMP_BLOCK * HEAD_DIM)
        return jax.nn.gelu(blk @ w1) @ w2

    k_cmp = compress(k_c, cmp_pos_k, cmp_w1_k, cmp_w2_k)
    v_cmp = compress(v_c, cmp_pos_v, cmp_w1_v, cmp_w2_v)
    n_slc = s // SLC_BLOCK
    k_slc = k_s.reshape(b, n_slc, SLC_BLOCK, N_KV_GROUPS, HEAD_DIM).transpose(0, 3, 1, 2, 4)
    v_slc = v_s.reshape(b, n_slc, SLC_BLOCK, N_KV_GROUPS, HEAD_DIM).transpose(0, 3, 1, 2, 4)
    pad = ((0, 0), (WINDOW, 0), (0, 0), (0, 0))
    k_win = jnp.pad(k_w, pad)
    v_win = jnp.pad(v_w, pad)
    return k_cmp, v_cmp, k_slc, v_slc, k_win, v_win

def selection_map(n_cmp, n_slc):
    c0 = jnp.arange(n_cmp) * CMP_STRIDE
    j0 = jnp.arange(n_slc) * SLC_BLOCK
    ov = jnp.minimum(c0[:, None] + CMP_BLOCK, j0[None, :] + SLC_BLOCK) - jnp.maximum(c0[:, None], j0[None, :])
    return jnp.clip(ov, 0).astype(jnp.float32) / CMP_BLOCK

def nsa_attention(h, positions, w_in, w_out, k_cmp, v_cmp, k_slc, v_slc, k_win, v_win):
    b, s, _ = h.shape
    dtype = h.dtype
    qd = N_HEADS * HEAD_DIM
    proj = h @ w_in
    q = proj[..., :qd].reshape(b, s, N_HEADS, HEAD_DIM)
    gates = jax.nn.sigmoid(proj[..., qd:].astype(jnp.float32)).reshape(
        b, s, N_KV_GROUPS, HEADS_PER_GROUP, N_BRANCH)
    scale = HEAD_DIM ** -0.5
    q_rot = (rope(q, positions) * scale).reshape(b, s, N_KV_GROUPS, HEADS_PER_GROUP, HEAD_DIM)
    q_cmp = (q * scale).reshape(b, s, N_KV_GROUPS, HEADS_PER_GROUP, HEAD_DIM)
    n_cmp = k_cmp.shape[1]
    n_slc = k_slc.shape[2]
    n_sel = min(N_SELECT, n_slc)
    cmp_end = jnp.arange(n_cmp) * CMP_STRIDE + CMP_BLOCK - 1
    slc_map = selection_map(n_cmp, n_slc)
    blk_ids = jnp.arange(n_slc)
    bi = jnp.arange(b)[:, None, None, None]
    gi = jnp.arange(N_KV_GROUPS)[None, None, :, None]

    def one_block(i):
        qs = i * Q_BLOCK
        t = qs + jnp.arange(Q_BLOCK)
        qc = lax.dynamic_slice_in_dim(q_cmp, qs, Q_BLOCK, axis=1)
        qr = lax.dynamic_slice_in_dim(q_rot, qs, Q_BLOCK, axis=1)
        gt = lax.dynamic_slice_in_dim(gates, qs, Q_BLOCK, axis=1)
        s_c = jnp.einsum('bqghd,bcgd->bqghc', qc, k_cmp)
        m_c = (cmp_end[None, :] <= t[:, None])[None, :, None, None, :]
        p_c = masked_softmax(s_c, m_c)
        o_c = jnp.einsum('bqghc,bcgd->bqghd', p_c.astype(dtype), v_cmp)
        imp = jnp.einsum('bqghc,cj->bqgj', p_c, slc_map)
        cur = t // SLC_BLOCK
        valid = blk_ids[None, :] * SLC_BLOCK <= t[:, None]
        forced = (blk_ids[None, :] == 0) | (blk_ids[None, :] == cur[:, None]) | (blk_ids[None, :] == cur[:, None] - 1)
        score = jnp.where(valid[None, :, None, :],
                          imp + jnp.where(forced, FORCE_BONUS, 0.0)[None, :, None, :], -1.0)
        _, sel = lax.top_k(score, n_sel)
        k_g = k_slc[bi, gi, sel]
        v_g = v_slc[bi, gi, sel]
        kpos = sel[..., None] * SLC_BLOCK + jnp.arange(SLC_BLOCK)
        s_s = jnp.einsum('bqghd,bqgnkd->bqghnk', qr, k_g).reshape(
            b, Q_BLOCK, N_KV_GROUPS, HEADS_PER_GROUP, n_sel * SLC_BLOCK)
        m_s = (kpos <= t[None, :, None, None, None]).reshape(b, Q_BLOCK, N_KV_GROUPS, 1, n_sel * SLC_BLOCK)
        p_s = masked_softmax(s_s, m_s).reshape(b, Q_BLOCK, N_KV_GROUPS, HEADS_PER_GROUP, n_sel, SLC_BLOCK)
        o_s = jnp.einsum('bqghnk,bqgnkd->bqghd', p_s.astype(dtype), v_g)
        kw = lax.dynamic_slice_in_dim(k_win, qs, Q_BLOCK + WINDOW, axis=1)
        vw = lax.dynamic_slice_in_dim(v_win, qs, Q_BLOCK + WINDOW, axis=1)
        wpos = qs - WINDOW + jnp.arange(Q_BLOCK + WINDOW)
        diff = t[:, None] - wpos[None, :]
        m_w = ((diff >= 0) & (diff < WINDOW) & (wpos[None, :] >= 0))[None, :, None, None, :]
        s_w = jnp.einsum('bqghd,bkgd->bqghk', qr, kw)
        p_w = masked_softmax(s_w, m_w)
        o_w = jnp.einsum('bqghk,bkgd->bqghd', p_w.astype(dtype), vw)
        o = (gt[..., 0:1] * o_c.astype(jnp.float32) + gt[..., 1:2] * o_s.astype(jnp.float32)
             + gt[..., 2:3] * o_w.astype(jnp.float32))
        return o.astype(dtype).reshape(b, Q_BLOCK, qd)

    out = lax.map(one_block, jnp.arange(s // Q_BLOCK))
    out = out.transpose(1, 0, 2, 3).reshape(b, s, qd)
    return out @ w_out

def hier_moe(h, w_rg, b_rg, w_re, b_re, w_gate, w_up, w_down):
    b, s, d = h.shape
    n_tok = b * s
    xf = h.reshape(n_tok, d)
    g_logits = (xf @ w_rg).astype(jnp.float32) + b_rg.astype(jnp.float32)
    g_prob = jax.nn.softmax(g_logits, axis=-1)
    g_top = jnp.argmax(g_logits, axis=-1)
    p_g = jnp.take_along_axis(g_prob, g_top[:, None], axis=1)[:, 0]
    e_logits = ((xf @ w_re).astype(jnp.float32) + b_re.astype(jnp.float32)).reshape(
        n_tok, N_GROUPS, EXPERTS_PER_GROUP)
    chosen = jnp.take_along_axis(e_logits, g_top[:, None, None], axis=1)[:, 0]
    top_vals, top_idx = lax.top_k(chosen, TOP_K_INNER)
    weights = p_g[:, None] * jax.nn.softmax(top_vals, axis=-1)
    expert = g_top[:, None] * EXPERTS_PER_GROUP + top_idx
    a_exp = expert.reshape(-1)
    a_tok = jnp.repeat(jnp.arange(n_tok), TOP_K_INNER)
    a_w = weights.reshape(-1)
    n_asg = n_tok * TOP_K_INNER
    onehot = jax.nn.one_hot(a_exp, N_EXPERTS, dtype=jnp.int32)
    rank = jnp.take_along_axis(jnp.cumsum(onehot, axis=0), a_exp[:, None], axis=1)[:, 0] - 1
    counts = jnp.sum(onehot, axis=0)
    padded = (counts + DISPATCH_ROWS - 1) // DISPATCH_ROWS * DISPATCH_ROWS
    pend = jnp.cumsum(padded)
    pstart = pend - padded
    dest = pstart[a_exp] + rank
    n_chunks = -(-n_asg // DISPATCH_ROWS) + N_EXPERTS
    n_rows = n_chunks * DISPATCH_ROWS
    row_tok = jnp.zeros((n_rows,), jnp.int32).at[dest].set(a_tok)
    row_w = jnp.zeros((n_rows,), jnp.float32).at[dest].set(a_w)
    chunk_exp = jnp.clip(jnp.searchsorted(pend, jnp.arange(n_chunks) * DISPATCH_ROWS, side='right'),
                         0, N_EXPERTS - 1)
    xs = xf[row_tok].reshape(n_chunks, DISPATCH_ROWS, d)

    def run_chunk(args):
        xc, e = args
        return (jax.nn.silu(xc @ w_gate[e]) * (xc @ w_up[e])) @ w_down[e]

    ys = lax.map(run_chunk, (xs, chunk_exp)).reshape(n_rows, d)
    out = jax.ops.segment_sum(ys * row_w[:, None].astype(ys.dtype), row_tok, num_segments=n_tok)
    return out.reshape(b, s, d).astype(h.dtype)

def setup_inputs(seed: int = 0) -> dict:
    key = jax.random.key(seed)
    ks = iter(jax.random.split(key, 32))
    f32 = jnp.float32

    def nrm(shape, scale):
        return jax.random.normal(next(ks), shape, f32) * scale

    d = D_MODEL
    n_a = DEPTH // 2
    n_b = DEPTH - n_a
    gd = N_KV_GROUPS * HEAD_DIM
    qd = N_HEADS * HEAD_DIM
    cin = CMP_BLOCK * HEAD_DIM
    return {
        'x': nrm((BATCH, SEQ, d), 1.0),
        'positions': jnp.tile(jnp.arange(SEQ, dtype=jnp.int32)[None, :], (BATCH, 1)),
        'norm_mix': 1.0 + nrm((DEPTH, d), 0.02),
        'norm_ffn': 1.0 + nrm((DEPTH, d), 0.02),
        'conv_w_in': nrm((n_a, d, 3 * d), d ** -0.5),
        'conv_w': nrm((n_a, CONV_WIDTH, d), CONV_WIDTH ** -0.5),
        'conv_w_out': nrm((n_a, d, d), d ** -0.5),
        'norm_kv': 1.0 + nrm((d,), 0.02),
        'w_kv': nrm((d, N_KV_SLOTS * gd), d ** -0.5),
        'cmp_pos_k': nrm((CMP_BLOCK, HEAD_DIM), 0.1),
        'cmp_w1_k': nrm((cin, CMP_HIDDEN), cin ** -0.5),
        'cmp_w2_k': nrm((CMP_HIDDEN, HEAD_DIM), CMP_HIDDEN ** -0.5),
        'cmp_pos_v': nrm((CMP_BLOCK, HEAD_DIM), 0.1),
        'cmp_w1_v': nrm((cin, CMP_HIDDEN), cin ** -0.5),
        'cmp_w2_v': nrm((CMP_HIDDEN, HEAD_DIM), CMP_HIDDEN ** -0.5),
        'attn_w_in': nrm((n_b, d, qd + N_BRANCH * N_HEADS), d ** -0.5),
        'attn_w_out': nrm((n_b, qd, d), qd ** -0.5),
        'router_group_w': nrm((DEPTH, d, N_GROUPS), d ** -0.5),
        'router_group_b': nrm((DEPTH, N_GROUPS), 0.01),
        'router_expert_w': nrm((DEPTH, d, N_EXPERTS), d ** -0.5),
        'router_expert_b': nrm((DEPTH, N_EXPERTS), 0.01),
        'expert_w_gate': nrm((DEPTH, N_EXPERTS, d, D_EXPERT), d ** -0.5),
        'expert_w_up': nrm((DEPTH, N_EXPERTS, d, D_EXPERT), d ** -0.5),
        'expert_w_down': nrm((DEPTH, N_EXPERTS, D_EXPERT, d), D_EXPERT ** -0.5),
        'norm_final': 1.0 + nrm((d,), 0.02),
    }

def reference(x, positions, norm_mix, norm_ffn, conv_w_in, conv_w, conv_w_out, norm_kv, w_kv,
              cmp_pos_k, cmp_w1_k, cmp_w2_k, cmp_pos_v, cmp_w1_v, cmp_w2_v, attn_w_in, attn_w_out,
              router_group_w, router_group_b, router_expert_w, router_expert_b,
              expert_w_gate, expert_w_up, expert_w_down, norm_final):
    n_a = DEPTH // 2
    shared = None
    for l in range(DEPTH):
        if l < n_a:
            h = rmsnorm(x, norm_mix[l])
            x = x + short_conv_mixer(h, conv_w_in[l], conv_w[l], conv_w_out[l])
        else:
            if shared is None:
                shared = nsa_shared_kv(rmsnorm(x, norm_kv), positions, w_kv, cmp_pos_k, cmp_w1_k, cmp_w2_k,
                                       cmp_pos_v, cmp_w1_v, cmp_w2_v)
            h = rmsnorm(x, norm_mix[l])
            x = x + nsa_attention(h, positions, attn_w_in[l - n_a], attn_w_out[l - n_a], *shared)
        x = x + hier_moe(rmsnorm(x, norm_ffn[l]), router_group_w[l], router_group_b[l],
                         router_expert_w[l], router_expert_b[l],
                         expert_w_gate[l], expert_w_up[l], expert_w_down[l])
    return rmsnorm(x, norm_final)


_drawn_inputs = setup_inputs


def setup_inputs(seed=0):
    import zlib

    import numpy as np

    out = dict(_drawn_inputs(seed))
    spreads = {}
    factors = {'norm_kv': 6.137,
     'cmp_pos_k': 6.974,
     'router_group_b': 24.514,
     'norm_final': 8.478,
     'cmp_pos_v': 6.065}
    for name, (base, spread) in spreads.items():
        noise = np.random.default_rng([zlib.crc32(name.encode()), seed]).standard_normal(out[name].shape)
        drawn = base * np.exp(spread * noise) if base else spread * noise
        out[name] = __import__('jax').numpy.asarray(drawn.astype(out[name].dtype))
    for name, factor in factors.items():
        out[name] = (out[name] * factor).astype(out[name].dtype)
    return out
```

```python
from contextlib import ExitStack

import concourse.bass as bass
from concourse import mybir

ALU = mybir.AluOpType
ACT = mybir.ActivationFunctionType
AX = mybir.AxisListType
F32 = mybir.dt.float32
F32R = mybir.dt.float32r
BF16 = mybir.dt.bfloat16
I32 = mybir.dt.int32
U32 = mybir.dt.uint32

P = 128
S = 512
D = 1024
NT = S // P
NK = D // P
EPS = 1e-6
NEG = -1e30

HD = 64
NH = 16
NG = 4
HPG = NH // NG
NBR = 3
CMP = 32
STRIDE = 16
NCMP = (S - CMP) // STRIDE + 1
HID = 256
SCALE = HD ** -0.5
MAGIC = 12582912.0
PI = 3.141592653589793
PI32 = 3.1415925
TWO_PI = (6.28125, 0.0019354820251464844, -1.7484556025237907e-07)

G = 4
EPG = 8
E = G * EPG
F = D // 2
KF = F // P
C = 64
N_OVF = 2 * S // C
ROWS = (E + N_OVF + 2) * C
NPIECE = 6
PIECE = 2048


class Chain:

    def __init__(self, eng, sem, base=0):
        self.eng, self.sem, self.n, self.base = eng, sem, 0, base

    def step(self, ins):
        self.n += 1
        ins.then_inc(self.sem, 1)
        self.eng.wait_ge(self.sem, self.base + self.n)


class Mem:
    pass


def program(nc, a, out):
    with ExitStack() as ctx:
        m = Mem()
        m.a, m.out = a, out

        def sb(name, shape, dt=F32):
            return ctx.enter_context(nc.sbuf_tensor(name, shape, dt))

        def sem(name):
            return ctx.enter_context(nc.semaphore(name))

        m.stage_sems = []

        def stage_sem(name):
            m.stage_sems.append(nc.alloc_semaphore(name=name))
            return m.stage_sems[-1]

        m.sem = stage_sem
        m.x = sb("x_res", [P, NT, D])
        m.raw = sb("raw", [P, NPIECE, PIECE])
        m.ident = sb("ident", [P, P])
        m.identb = sb("identb", [P, P], BF16)
        m.before = sb("before", [P, P], BF16)
        m.ones = sb("ones", [P, P], BF16)
        m.iota = sb("iota", [P, 48])
        m.ss = sb("ss", [P, 8])
        m.rstd = sb("rstd", [P, 5, NT])
        m.idx = sb("idx", [P, NT, 2], U32)
        m.wts = sb("wts", [P, NT, 2])
        m.novf = sb("novf", [1, 1], I32)
        m.ovf_e = sb("ovf_e", [1, N_OVF + 1], I32)
        m.ps = [ctx.enter_context(nc.psum_tensor(f"ps{i}", [P, 512], F32)) for i in range(8)]
        m.slots_x = nc.dram_tensor("slots_x", (ROWS, D), F32, kind="Internal").ap()
        m.slots_y = nc.dram_tensor("slots_y", (ROWS, D), F32, kind="Internal").ap()
        m.ready = sem("constants_ready")
        m.load = [[sem(f"load{L}_{q}") for q in range(NPIECE)] for L in range(2)]

        setup(nc, m)
        conv_mixer(nc, m)
        router(nc, m, 0)
        experts(nc, m, 0)
        combine(nc, m, 0)
        recycle_semaphores(nc, m)
        with ExitStack() as kvctx:
            shared_kv(nc, m, kvctx)
            attention(nc, m)
        router(nc, m, 1)
        experts(nc, m, 1)
        combine(nc, m, 1)
        final_norm(nc, m)


def recycle_semaphores(nc, m):
    nc.clear_and_free_semaphores(m.stage_sems)
    m.stage_sems = []
    nc.all_engine_barrier()


def setup(nc, m):
    x_in, filled = m.sem("x_in"), m.sem("const_filled")
    with nc.Block() as block:

        @block.sync
        def _(sp):
            sp.dma_start(m.x[:], m.a["x"].rearrange("b (t p) d -> p (b t) d", p=P)).then_inc(x_in, 16)
            sp.wait_ge(x_in, 16)

        @block.gpsimd
        def _(pool):
            pool.memset(m.ident[:], 0.0).then_inc(filled, 1)
            pool.memset(m.ones[:], 1.0).then_inc(filled, 1)
            pool.iota(m.iota[:], [[1, 48]], base=0, channel_multiplier=0,
                      allow_small_or_imprecise_dtypes=True).then_inc(filled, 1)
            pool.wait_ge(filled, 3)
            pool.affine_select(out=m.ident[:], in_=m.ident[:], compare_op=ALU.not_equal, fill=1.0, base=0,
                               pattern=[[-1, P]], channel_multiplier=1).then_inc(filled, 1)
            pool.affine_select(out=m.before[:], in_=m.ones[:], compare_op=ALU.is_gt, fill=0.0, base=0,
                               pattern=[[1, P]], channel_multiplier=-1).then_inc(filled, 1)
            pool.wait_ge(filled, 5)
            pool.tensor_copy(m.identb[:], m.ident[:]).then_inc(m.ready, 1)
            pool.wait_ge(m.ready, 1)


class Norm:

    def __init__(self, m, name, n):
        self.m, self.n = m, n
        self.sq, self.ms, self.rt = m.sem(name + "_squares"), m.sem(name + "_mean"), m.sem(name + "_root")
        self.own, self.xn = m.sem(name + "_own"), m.sem(name + "_normed")
        self.tr, self.ev = m.sem(name + "_transposed"), [m.sem(name + "_hT_act"), m.sem(name + "_hT_dve")]

    def scalar_stats(self, act, junk):
        m = self.m
        for t in range(NT):
            if t:
                act.wait_ge(self.sq, t)
            act.activation(junk, m.x[:, t, :], ACT.Square, accum_out=m.ss[:, t:t + 1]).then_inc(self.sq, 1)
        act.wait_ge(self.ms, 1)
        act.activation(m.rstd[:, self.n, :], m.ss[:, 4:8], ACT.Sqrt).then_inc(self.rt, 1)

    def vector_stats(self, dve, tmp):
        m, own = self.m, Chain(dve, self.own)
        dve.wait_ge(self.sq, NT)
        dve.tensor_scalar(m.ss[:, 4:8], m.ss[:, 0:4], 1.0 / D, EPS, ALU.mult, ALU.add).then_inc(self.ms, 1)
        dve.wait_ge(self.rt, 1)
        r = m.rstd[:, self.n, :]
        own.step(dve.reciprocal(r, r))
        own.step(dve.tensor_tensor(tmp, r, r, ALU.mult))
        own.step(dve.tensor_tensor(tmp, tmp, m.ss[:, 4:8], ALU.mult))
        own.step(dve.tensor_scalar(tmp, tmp, -0.5, 1.5, ALU.mult, ALU.add))
        own.step(dve.tensor_tensor(r, r, tmp, ALU.mult))

    def vector_normed(self, dve, xn):
        for t in range(NT):
            dve.tensor_scalar(xn[:, t, :], self.m.x[:, t, :], self.m.rstd[:, self.n, t:t + 1], None,
                              ALU.mult).then_inc(self.xn, 1)

    def tensor(self, pe, xn):
        pe.wait_ge(self.xn, NT)
        for k in range(NK):
            for t in range(NT):
                tr = pe.transpose(self.m.ps[k][:, t * P:(t + 1) * P], xn[:, t, k::NK], self.m.ident[:])
            tr.then_inc(self.tr, 1)

    def evacuate(self, eng, dve, outs):
        for k in range(dve, NK, 2):
            eng.wait_ge(self.tr, k + 1)
            for hT, gain in outs:
                src, g = self.m.ps[k][:], None if gain is None else gain[:, k:k + 1]
                if dve:
                    i = eng.tensor_copy(hT[:, k, :], src) if g is None else \
                        eng.tensor_scalar(hT[:, k, :], src, g, None, ALU.mult)
                else:
                    i = eng.activation(hT[:, k, :], src, ACT.Copy, scale=1.0 if g is None else g)
            i.then_inc(self.ev[dve], 1)

    def wait_hT(self, pe):
        pe.wait_ge(self.ev[0], NK // 2)
        pe.wait_ge(self.ev[1], NK // 2)


def conv_mixer(nc, m):
    a = m.a
    CW = 256
    NCH = D // CW
    with ExitStack() as ctx:
        def sb(name, shape, dt=F32):
            return ctx.enter_context(nc.sbuf_tensor(name, shape, dt))

        hT = sb("c_hT", [P, NK, S])
        gain = sb("c_gain", [P, NK])
        cw = sb("c_cw", [P, 3, NK])
        win = sb("c_win", [P, 2, NK, 3, CW])
        wout = sb("c_wout", [P, NK, D])
        gated = sb("c_gated", [P, NK, S])
        xn = gated.rearrange("p k s -> p (k s)").rearrange("p (t d) -> p t d", t=NT)
        u = sb("c_u", [P, 2, S + 2])
        csb = sb("c_csb", [P, 2, S])
        y = sb("c_y", [P, 2, S])
        tmp = sb("c_tmp", [P, NT])
        zero = sb("c_zero", [P, D])
        s_zero, s_blank = m.sem("c_zero_set"), m.sem("c_blank_rows")
        nrm = Norm(m, "c", 0)
        s_gain, s_cw, s_wout = m.sem("c_gain_in"), m.sem("c_cw_in"), m.sem("c_wout_in")
        s_win = [m.sem(f"c_win{i}") for i in range(2)]
        s_proj, s_cc, s_own = m.sem("c_projected"), m.sem("c_copied"), m.sem("c_own2")
        s_u, s_gated, s_o, s_res = m.sem("c_u_done"), m.sem("c_gated_done"), m.sem("c_out"), m.sem("c_res")
        block = ctx.enter_context(nc.Block())
        w_in = a["conv_w_in"][0].rearrange("(p k) (c n w) -> n c p k w", k=NK, c=3, w=CW)

        @block.sync
        def _(sp):
            with nc.allow_non_contiguous_dma(reason="small vectors"):
                sp.dma_start(gain[:], a["norm_mix"][0].rearrange("(p k) -> p k", k=NK)).then_inc(s_gain, 16)
                sp.dma_start(cw[:], a["conv_w"][0].rearrange("w (j p) -> p w j", p=P)).then_inc(s_cw, 16)
            for n in range(NCH):
                if n >= 2:
                    sp.wait_ge(s_proj, 6 * (n - 1))
                for c in range(3):
                    sp.dma_start(win[:, n % 2, :, c, :], w_in[n, c]).then_inc(s_win[n % 2], 16)
            sp.dma_start(wout[:], a["conv_w_out"][0].rearrange("(j p) n -> p j n", p=P)).then_inc(s_wout, 16)
            prefetch(sp, m, 0)
            sp.wait_ge(s_zero, 1)
            blank = [m.slots_x[i * P:(i + 1) * P, :] for i in range(ROWS // P)]
            blank += [m.slots_y[i * P:(i + 1) * P, :] for i in range(E * C // P, ROWS // P)]
            for rows in blank:
                sp.dma_start(rows, zero[:]).then_inc(s_blank, 16)
            sp.wait_ge(s_blank, 16 * len(blank))

        @block.scalar
        def _(act):
            nrm.scalar_stats(act, y[:].rearrange("p b s -> p (b s)"))
            act.wait_ge(s_gain, 16)
            nrm.evacuate(act, 0, [(hT, gain)])
            for j in range(NK):
                act.wait_ge(s_proj, 3 * j + 1)
                if j >= 2:
                    act.wait_ge(s_u, j - 1)
                act.activation(csb[:, j % 2, :], m.ps[3 * (j % 2)][:], ACT.Copy).then_inc(s_cc, 1)

        @block.vector
        def _(dve):
            own = Chain(dve, s_own)
            dve.memset(zero[:], 0.0).then_inc(s_zero, 1)
            for b in range(2):
                own.step(dve.memset(u[:, b, 0:2], 0.0))
            nrm.vector_stats(dve, tmp[:])
            nrm.vector_normed(dve, xn)
            dve.wait_ge(s_gain, 16)
            nrm.evacuate(dve, 1, [(hT, gain)])
            dve.wait_ge(s_cw, 16)
            for j in range(NK):
                b = j % 2
                dve.wait_ge(s_cc, j + 1)
                dve.wait_ge(s_proj, 3 * j + 2)
                dve.tensor_tensor(u[:, b, 2:], csb[:, b, :], m.ps[3 * b + 1][:], ALU.mult).then_inc(s_u, 1)
                dve.wait_ge(s_u, j + 1)
                own.step(dve.tensor_scalar(y[:, b, :], u[:, b, 0:S], cw[:, 0, j:j + 1], None, ALU.mult))
                for w in (1, 2):
                    own.step(dve.scalar_tensor_tensor(out=y[:, b, :], in0=u[:, b, w:w + S],
                                                      scalar=cw[:, w, j:j + 1], in1=y[:, b, :],
                                                      op0=ALU.mult, op1=ALU.add))
                dve.wait_ge(s_proj, 3 * j + 3)
                dve.tensor_tensor(gated[:, j, :], y[:, b, :], m.ps[3 * b + 2][:], ALU.mult).then_inc(s_gated, 1)
            add_residual(dve, m, s_o, s_res)

        @block.tensor
        def _(pe):
            nrm.tensor(pe, xn)
            nrm.wait_hT(pe)
            for j in range(NK):
                n = j // 2
                pe.wait_ge(s_win[n % 2], 48 * (n // 2 + 1))
                if j >= 2:
                    pe.wait_ge(s_gated, j - 1)
                for i, c in enumerate((1, 2, 0)):
                    for k in range(NK):
                        mm = pe.matmul(m.ps[3 * (j % 2) + i][:],
                                       win[:, n % 2, k, c, (j % 2) * P:(j % 2 + 1) * P], hT[:, k, :],
                                       start=(k == 0), stop=(k == NK - 1))
                    mm.then_inc(s_proj, 1)
            pe.wait_ge(s_wout, 16)
            pe.wait_ge(s_gated, NK)
            project_out(pe, m, gated, wout, s_o)


def project_out(pe, m, feats, w, s_o):
    for t in range(NT):
        for h in range(2):
            for k in range(NK):
                mm = pe.matmul(m.ps[2 * t + h][:], feats[:, k, t * P:(t + 1) * P], w[:, k, h * 512:(h + 1) * 512],
                               start=(k == 0), stop=(k == NK - 1))
            mm.then_inc(s_o, 1)


def add_residual(dve, m, s_o, s_res):
    for i in range(2 * NT):
        dve.wait_ge(s_o, i + 1)
        x = m.x[:, i // 2, (i % 2) * 512:(i % 2 + 1) * 512]
        dve.tensor_tensor(x, x, m.ps[i][:], ALU.add).then_inc(s_res, 1)


def piece_src(m, L, q, e):
    name = ("expert_w_gate", "expert_w_up", "expert_w_down")[q // 2]
    w = m.a[name][L]
    if q < 4:
        w = w.rearrange("e (p h k) n -> h e p (k n)", p=P, h=2)[q % 2]
    else:
        w = w.rearrange("e (h p k) n -> h e p (k n)", h=2, p=P)[q % 2]
    return w[e] if isinstance(e, int) else w[bass.ds(e, 1)].rearrange("e p n -> (e p) n")


def prefetch(sp, m, L):
    for slot, q in ((0, 0), (1, 1), (4, 2), (5, 3), (2, 4), (3, 5)):
        sp.dma_start(m.raw[:, slot, :], piece_src(m, L, q, 0)).then_inc(m.load[L][slot], 16)


def router(nc, m, L):
    a = m.a
    with ExitStack() as ctx:
        def sb(name, shape, dt=F32):
            return ctx.enter_context(nc.sbuf_tensor(f"r{L}_{name}", shape, dt))

        def sem(name):
            return m.sem(f"r{L}_{name}")

        NL = G + E
        xn = sb("xn", [P, NT, D])
        hT = sb("hT", [P, NK, S])
        gb = sb("gb", [P, D])
        wr = sb("wr", [P, NK, NL])
        bias = sb("bias", [P, NL])
        lg = sb("lg", [P, NT, NL])
        t4 = [sb(f"t4_{i}", [P, NT, G]) for i in range(3)]
        el = sb("el", [P, NT, E])
        t32 = sb("t32", [P, NT, E])
        oh = [sb(f"oh{i}", [P, NT, E]) for i in range(2)]
        both = sb("both", [P, NT, E], BF16)
        c1 = [sb(f"c1_{i}", [P, NT]) for i in range(6)]
        rank = sb("rank", [P, NT, E])
        slot = sb("slot", [P, NT, E])
        late = sb("late", [P, NT, E])
        cnt = sb("cnt", [P, E])
        t28 = sb("t28", [P, E, 8])
        ovn = sb("ovn", [P, E])
        inc = sb("inc", [P, E])
        onef = sb("onef", [P, E])
        base = sb("base", [P, 2, E])
        slotf = sb("slotf", [P, NT, 2])
        tab = sb("tab", [1, N_OVF, E])
        tabf = sb("tabf", [1, N_OVF + 1])
        tmp = sb("tmp", [P, NT])
        nrm = Norm(m, f"r{L}", 1 + 2 * L)
        s_w, s_gb = sem("weights_in"), sem("gain_in")
        s_lg, s_one, s_rank = sem("logits"), sem("onehot"), sem("ranks")
        s_ge, s_e, s_own = sem("exp_ready"), sem("exp_done"), sem("own2")
        s_slots, s_rows = sem("slots_ready"), sem("rows_out")
        block = ctx.enter_context(nc.Block())
        AXX = AX.X

        @block.sync
        def _(sp):
            sp.dma_start(gb[:], a["norm_ffn"][L:L + 1, :].broadcast_to([P, D])).then_inc(s_gb, 16)
            with nc.allow_non_contiguous_dma(reason="router weights are 1% of the bytes"):
                sp.dma_start(wr[:, :, 0:G], a["router_group_w"][L].rearrange("(p k) g -> p k g", k=NK)).then_inc(s_w, 16)
                sp.dma_start(wr[:, :, G:], a["router_expert_w"][L].rearrange("(p k) g -> p k g", k=NK)).then_inc(s_w, 16)
                sp.dma_start(bias[:, 0:G], a["router_group_b"][L:L + 1, :].broadcast_to([P, G])).then_inc(s_w, 16)
                sp.dma_start(bias[:, G:], a["router_expert_b"][L:L + 1, :].broadcast_to([P, E])).then_inc(s_w, 16)

        @block.scalar
        def _(act):
            nrm.scalar_stats(act, xn[:, 0, :])
            nrm.evacuate(act, 0, [(hT, None)])
            act.wait_ge(s_ge, 1)
            act.activation(t4[1][:], t4[0][:], ACT.Exp).then_inc(s_e, 1)
            act.wait_ge(s_ge, 2)
            act.activation(c1[3][:], c1[2][:], ACT.Exp).then_inc(s_e, 1)

        @block.tensor
        def _(pe):
            nrm.tensor(pe, xn)
            nrm.wait_hT(pe)
            pe.wait_ge(s_w, 64)
            for t in range(NT):
                for k in range(NK):
                    mm = pe.matmul(m.ps[0][:, t * NL:(t + 1) * NL], hT[:, k, t * P:(t + 1) * P], wr[:, k, :],
                                   start=(k == 0), stop=(k == NK - 1))
            mm.then_inc(s_lg, 1)
            pe.wait_ge(s_one, 1)
            for t in range(NT):
                for t2 in range(t + 1):
                    mm = pe.matmul(m.ps[1][:, t * E:(t + 1) * E], (m.before if t2 == t else m.ones)[:],
                                   both[:, t2, :], start=(t2 == 0), stop=(t2 == t))
            for t in range(NT):
                mm = pe.matmul(m.ps[1][:, NT * E:(NT + 1) * E], m.ones[:], both[:, t, :],
                               start=(t == 0), stop=(t == NT - 1))
            mm.then_inc(s_rank, 1)

        @block.vector
        def _(dve):
            own = Chain(dve, s_own)
            nrm.vector_stats(dve, tmp[:])
            dve.wait_ge(s_gb, 16)
            for t in range(NT):
                dve.scalar_tensor_tensor(out=xn[:, t, :], in0=m.x[:, t, :], scalar=m.rstd[:, nrm.n, t:t + 1],
                                         in1=gb[:], op0=ALU.mult, op1=ALU.mult).then_inc(nrm.xn, 1)
            nrm.evacuate(dve, 1, [(hT, None)])
            dve.wait_ge(s_w, 64)
            dve.wait_ge(s_lg, 1)

            def bc(x, n):
                return x.unsqueeze(2).broadcast_to([P, NT, n])

            own.step(dve.tensor_tensor(lg[:], m.ps[0][:, 0:NT * NL].rearrange("p (t n) -> p t n", t=NT),
                                       bias[:].unsqueeze(1).broadcast_to([P, NT, NL]), ALU.add))

            def first_max(vals, n, top, onehot, scratch):
                own.step(dve.tensor_reduce(top, vals, AXX, ALU.max))
                own.step(dve.tensor_tensor(scratch, vals, bc(top, n), ALU.is_equal))
                own.step(dve.tensor_tensor(scratch, scratch, down(n), ALU.mult))
                own.step(dve.tensor_reduce(c1[5][:], scratch, AXX, ALU.max))
                own.step(dve.tensor_tensor(onehot, scratch, bc(c1[5][:], n), ALU.is_equal))

            own.step(dve.tensor_scalar(onef[:], m.iota[:, 0:E], -1.0, 64.0, ALU.mult, ALU.add))

            def down(n):
                return onef[:, 0:n].unsqueeze(1).broadcast_to([P, NT, n])

            gl = lg[:, :, 0:G]
            first_max(gl, G, c1[0][:], t4[2][:], t4[0][:])
            dve.tensor_tensor(t4[0][:], gl, bc(c1[0][:], G), ALU.subtract).then_inc(s_ge, 1)
            elv = el[:].rearrange("p t (g e) -> p t g e", g=G)
            gsel = t4[2][:].unsqueeze(3).broadcast_to([P, NT, G, EPG])
            own.step(dve.tensor_tensor(elv, lg[:, :, G:].rearrange("p t (g e) -> p t g e", g=G), gsel, ALU.mult))
            own.step(dve.tensor_scalar(t4[2][:], t4[2][:], -1.0, -NEG, ALU.add, ALU.mult))
            own.step(dve.tensor_tensor(elv, elv, gsel, ALU.add))
            first_max(el[:], E, c1[0][:], oh[0][:], t32[:])
            own.step(dve.scalar_tensor_tensor(out=el[:], in0=oh[0][:], scalar=NEG, in1=el[:],
                                              op0=ALU.mult, op1=ALU.add))
            first_max(el[:], E, c1[1][:], oh[1][:], t32[:])
            dve.tensor_tensor(both[:], oh[0][:], oh[1][:], ALU.add).then_inc(s_one, 1)
            dve.tensor_tensor(c1[2][:], c1[1][:], c1[0][:], ALU.subtract).then_inc(s_ge, 1)
            dve.wait_ge(s_e, 1)
            own.step(dve.tensor_reduce(c1[4][:], t4[1][:], AXX, ALU.add))
            dve.wait_ge(s_e, 2)
            own.step(dve.tensor_scalar(c1[5][:], c1[3][:], 1.0, None, ALU.add))
            own.step(dve.tensor_tensor(c1[4][:], c1[4][:], c1[5][:], ALU.mult))
            own.step(dve.reciprocal(m.wts[:, :, 0], c1[4][:]))
            own.step(dve.tensor_tensor(m.wts[:, :, 1], m.wts[:, :, 0], c1[3][:], ALU.mult))

            dve.wait_ge(s_rank, 1)
            own.step(dve.tensor_copy(rank[:], m.ps[1][:, 0:NT * E].rearrange("p (t e) -> p t e", t=NT)))
            own.step(dve.tensor_copy(cnt[:], m.ps[1][:, NT * E:(NT + 1) * E]))
            own.step(dve.tensor_scalar(t28[:], m.iota[:, 0:8].unsqueeze(1).broadcast_to([P, E, 8]),
                                       1.0, float(C), ALU.add, ALU.mult))
            own.step(dve.tensor_tensor(t28[:], cnt[:].unsqueeze(2).broadcast_to([P, E, 8]), t28[:], ALU.is_gt))
            own.step(dve.tensor_reduce(ovn[:], t28[:], AXX, ALU.add))
            own.step(dve.memset(onef[:], 1.0))
            own.step(dve.tensor_tensor_scan(inc[:], onef[:], ovn[:], 0.0, ALU.mult, ALU.add))
            own.step(dve.tensor_scalar(base[:, 0, :], m.iota[:, 0:E], float(C), None, ALU.mult))
            own.step(dve.tensor_tensor(base[:, 1, :], inc[:], ovn[:], ALU.subtract))
            own.step(dve.tensor_scalar(base[:, 1, :], base[:, 1, :], float(C), float(C * E - C), ALU.mult, ALU.add))
            own.step(dve.tensor_tensor(base[:, 1, :], base[:, 1, :], base[:, 0, :], ALU.subtract))
            own.step(dve.tensor_scalar(late[:], rank[:], float(C) - 0.5, None, ALU.is_gt))
            own.step(dve.tensor_tensor(late[:], late[:], base[:, 1, :].unsqueeze(1).broadcast_to([P, NT, E]), ALU.mult))
            own.step(dve.tensor_tensor(slot[:], rank[:], base[:, 0, :].unsqueeze(1).broadcast_to([P, NT, E]), ALU.add))
            own.step(dve.tensor_tensor(slot[:], slot[:], late[:], ALU.add))
            for k in range(2):
                own.step(dve.tensor_tensor(t32[:], slot[:], oh[k][:], ALU.mult))
                own.step(dve.tensor_reduce(slotf[:, :, k], t32[:], AXX, ALU.add))
            dve.tensor_copy(m.idx[:], slotf[:]).then_inc(s_slots, 1)
            own.step(dve.tensor_tensor(tab[:], inc[0:1, :].unsqueeze(1).broadcast_to([1, N_OVF, E]),
                                       m.iota[0:1, 0:N_OVF].unsqueeze(2).broadcast_to([1, N_OVF, E]), ALU.is_le))
            own.step(dve.memset(tabf[:, 0:1], float(E - 1)))
            own.step(dve.tensor_reduce(tabf[:, 1:], tab[:], AXX, ALU.add))
            own.step(dve.tensor_scalar(tabf[:], tabf[:], float(E - 1), None, ALU.min))
            own.step(dve.tensor_copy(m.ovf_e[:], tabf[:]))
            own.step(dve.tensor_copy(m.novf[:], inc[0:1, E - 1:E]))

        @block.gpsimd
        def _(pool):
            pool.wait_ge(s_slots, 1)
            pool.wait_ge(nrm.xn, NT)
            for t in range(NT):
                for k in range(2):
                    pool.indirect_dma_start(out=m.slots_x[:, :],
                                            out_offset=bass.IndirectOffsetOnAxis(ap=m.idx[:, t, k:k + 1], axis=0),
                                            in_=xn[:, t, :], in_offset=None).then_inc(s_rows, 16)
            pool.wait_ge(s_rows, 16 * 2 * NT)


def experts(nc, m, L):
    with ExitStack() as ctx:
        def sb(name, shape, dt=F32):
            return ctx.enter_context(nc.sbuf_tensor(f"e{L}_{name}", shape, dt))

        def sem(name):
            return m.sem(f"e{L}_{name}")

        H = 2 * C
        FH = F // 2
        xrow = sb("xrow", [P, D])
        xst = sb("xst", [P, 2, NK, H], F32R)
        w_hi = sb("w_hi", [P, NPIECE, PIECE], F32R)
        w_lo = sb("w_lo", [P, NPIECE, PIECE], F32R)
        part = sb("part", [P, 2, FH])
        gate = sb("gate", [P, FH])
        up = sb("up", [P, FH])
        act_g = sb("act_g", [P, FH])
        hid = sb("hid", [P, FH])
        hst = sb("hst", [P, 2, 2, H], F32R)
        ypart = sb("ypart", [C, D])
        yrow = sb("yrow", [C, D])
        s_xl, s_st = sem("x_in"), sem("y_out")
        s_xt, s_xhi, s_xlo = sem("x_transposed"), sem("x_hi"), sem("x_lo")
        s_hi = {"act": sem("w_hi_act"), "dve": sem("w_hi_dve")}
        s_lo = {"dve": sem("w_lo_dve"), "pool": sem("w_lo_pool")}
        s_used = sem("piece_used")
        s_part = [sem("gate_part"), sem("up_part")]
        s_sum = [sem("gate_sum"), sem("up_sum")]
        s_sg, s_h = sem("silu"), sem("hidden")
        s_ht, s_hhi, s_hlo = sem("h_transposed"), sem("h_hi"), sem("h_lo")
        s_yp, s_y = sem("y_part"), sem("y_sum")
        ps_x, ps_gu, ps_h, ps_y = m.ps[0:2], m.ps[2:4], m.ps[4], m.ps[5:7]
        GATE, DOWN, UP = (0, 1), (2, 3), (4, 5)
        HI = ("act", "act", "act", "act", "act", "dve")
        LO = ("dve", "dve", "pool", "pool", "dve", "dve")

        def wait(eng, s, v):
            if not isinstance(v, int) or v > 0:
                eng.wait_ge(s, v)

        def made(eng, table, sems, c, k, last=False):
            who = table[k]
            down = sum(table[q] == who for q in DOWN)
            before = [q for q in range(k) if not (last and q in GATE) and not (isinstance(c, int) and c == 0 and q in DOWN)]
            first = 0 if isinstance(c, int) and c == 0 else c * table.count(who) - down
            wait(eng, sems[who], first + sum(table[q] == who for q in before) + 1)

        def used(eng, c, k, last=False):
            if isinstance(c, int) and c < 0 or isinstance(c, int) and c == 0 and k in DOWN:
                return
            if isinstance(c, int) and c == 0:
                eng.wait_ge(s_used, {0: 1, 1: 2, 4: 3, 5: 4}[k])
            else:
                eng.wait_ge(s_used, c * NPIECE - 2 + k + 1 - (2 if last else 0))

        def loaded(eng, c, k):
            wait(eng, m.load[L][k], (c if k in DOWN else c + 1) * 16)

        def pe_rows(pe, i):
            wait(pe, s_xl, i * 16 + 16)
            wait(pe, s_xlo, i * 2)
            for k in range(NK):
                mm = pe.transpose(ps_x[k // 4][:, (k % 4) * P:(k % 4 + 1) * P], xrow[:, k::NK], m.ident[:])
            mm.then_inc(s_xt, 1)

        def pe_gate_up(pe, c, u, i, pieces):
            wait(pe, s_xlo, c + 1)
            for b, k in enumerate(pieces):
                made(pe, LO, s_lo, c, k)
                if b == 0:
                    wait(pe, s_sum[i], c)
                for kk in range(4):
                    for w in (w_hi, w_lo):
                        mm = pe.matmul(ps_gu[i][:], xst[:, u, 4 * b + kk, :], w[:, k, kk * F:(kk + 1) * F],
                                       start=(b == 0 and kk == 0 and w is w_hi),
                                       stop=(b == 1 and kk == 3 and w is w_lo))
                mm.then_inc(s_used, 1)

        def pe_down(pe, c, last=False):
            wait(pe, s_h, c)
            wait(pe, s_hlo, c - 1)
            for k in range(2):
                mm = pe.transpose(ps_h[:, k * P:(k + 1) * P], hid[:, k::2], m.ident[:])
            mm.then_inc(s_ht, 1)
            wait(pe, s_hlo, c)
            wait(pe, s_y, c - 1)
            for h, k in enumerate(DOWN):
                made(pe, LO, s_lo, c, k, last)
                for kk in range(2):
                    for w in (w_hi, w_lo):
                        for n in range(2):
                            mm = pe.matmul(ps_y[n][:], hst[:, kk, h, :],
                                           w[:, k, kk * D + n * 512:kk * D + (n + 1) * 512],
                                           start=(h == 0 and kk == 0 and w is w_hi),
                                           stop=(h == 1 and kk == 1 and w is w_lo))
                mm.then_inc(s_used, 1)

        def pe_step(pe, c, u):
            if isinstance(c, int) and c == 0:
                pe_rows(pe, 0)
            pe_gate_up(pe, c, u, 0, GATE)
            if u == 1:
                pe_rows(pe, (c + 1) // 2 if isinstance(c, int) else (c + 1) >> 1)
            if not (isinstance(c, int) and c == 0):
                pe_down(pe, c)
            pe_gate_up(pe, c, u, 1, UP)

        def act_rows_in(act, i):
            wait(act, s_xt, i)
            act.dma_start(xrow[:], m.slots_x[bass.ds(i * H, H), :]).then_inc(s_xl, 16)

        def act_hi(act, c, k, last=False):
            if HI[k] == "act":
                loaded(act, c, k)
                used(act, c - 1, k)
                act.activation(w_hi[:, k, :], m.raw[:, k, :], ACT.Copy).then_inc(s_hi["act"], 1)

        def act_part(act, c, i, at, k, last=False):
            used(act, at, k)
            wait(act, s_sum[i], c)
            act.activation(part[0:C, i, :], ps_gu[i][C:H, 0:FH], ACT.Copy)
            act.activation(part[C:H, i, :], ps_gu[i][0:C, FH:F], ACT.Copy).then_inc(s_part[i], 1)

        def act_h_hi(act, c):
            wait(act, s_ht, c)
            used(act, c - 1, DOWN[1])
            act.activation(hst[:, :, :, 0:C], ps_h[:, 0:2 * P].rearrange("p (k h c) -> p k h c", k=2, h=2),
                           ACT.Copy).then_inc(s_hhi, 1)

        def act_y(act, c, last=False):
            used(act, c, DOWN[1], last)
            wait(act, s_y, c - 1)
            for n in range(2):
                act.activation(ypart[:, n * 512:(n + 1) * 512], ps_y[n][C:H, :], ACT.Copy).then_inc(s_yp, 1)
            wait(act, s_y, c)
            act.dma_start(m.slots_y[bass.ds(c * C - C, C), :], yrow[:]).then_inc(s_st, 16)

        def rows_view(c, u):
            return [(b, ps_x[b][:].rearrange("p (k u c) -> p k u c", k=4, u=2)[:, :, u, :],
                     xst[:, u, 4 * b:4 * b + 4, :]) for b in range(2)]

        def act_x_hi(act, c, u):
            wait(act, s_xt, (c // 2 if isinstance(c, int) else c >> 1) + 1)
            used(act, c - 2, UP[1])
            for b, src, dst in rows_view(c, u):
                act.activation(dst[:, :, 0:C], src, ACT.Copy).then_inc(s_xhi, 1)

        def act_step(act, c, u):
            start = isinstance(c, int) and c == 0
            if start:
                act_rows_in(act, 0)
                act_x_hi(act, 0, 0)
            if u == 0:
                act_rows_in(act, c // 2 + 1 if isinstance(c, int) else (c >> 1) + 1)
            for k in GATE:
                act_hi(act, c, k)
            if not start:
                if not (isinstance(c, int) and c == 1):
                    act_y(act, c - 1)
                act_part(act, c - 1, 1, c - 1, UP[1])
                for k in DOWN:
                    act_hi(act, c, k)
                act_h_hi(act, c)
            act_hi(act, c, UP[0])
            act_part(act, c, 0, c, GATE[1])
            wait(act, s_sum[0], c + 1)
            wait(act, s_h, c)
            act.activation(act_g[:], gate[:], ACT.Silu).then_inc(s_sg, 1)
            act_hi(act, c, UP[1])
            act_x_hi(act, c + 1, 1 - u)

        def act_tail(act, c):
            act_y(act, c - 1)
            act_part(act, c - 1, 1, c - 1, UP[1])
            for k in DOWN:
                act_hi(act, c, k, True)
            act_h_hi(act, c)
            act_y(act, c, True)

        def split(eng, who, c, k, last=False):
            if HI[k] == who:
                loaded(eng, c, k)
                used(eng, c - 1, k)
                eng.tensor_copy(w_hi[:, k, :], m.raw[:, k, :]).then_inc(s_hi[who], 1)
            if LO[k] == who:
                made(eng, HI, s_hi, c, k, last)
                used(eng, c - 1, k)
                eng.tensor_tensor(w_lo[:, k, :], m.raw[:, k, :], w_hi[:, k, :].bitcast(F32),
                                  ALU.subtract).then_inc(s_lo[who], 1)

        def dve_sum(dve, c, i, dst):
            wait(dve, s_part[i], c + 1)
            wait(dve, (s_sg, s_h)[i], c)
            dve.tensor_tensor(dst[0:C, :], ps_gu[i][0:C, 0:FH], part[0:C, i, :], ALU.add)
            dve.tensor_tensor(dst[C:H, :], ps_gu[i][C:H, FH:F], part[C:H, i, :], ALU.add).then_inc(s_sum[i], 1)

        def dve_hidden(dve, c):
            dve_sum(dve, c - 1, 1, up)
            wait(dve, s_sum[1], c)
            wait(dve, s_sg, c)
            wait(dve, s_ht, c - 1)
            dve.tensor_tensor(hid[:], act_g[:], up[:], ALU.mult).then_inc(s_h, 1)

        def dve_h_lo(dve, c):
            wait(dve, s_hhi, c)
            dve.tensor_tensor(hst[:, :, :, C:H], ps_h[:, 0:2 * P].rearrange("p (k h c) -> p k h c", k=2, h=2),
                              hst[:, :, :, 0:C].bitcast(F32), ALU.subtract).then_inc(s_hlo, 1)

        def dve_y(dve, c):
            wait(dve, s_yp, 2 * c)
            wait(dve, s_st, 16 * c - 16)
            for n in range(2):
                o = dve.tensor_tensor(yrow[:, n * 512:(n + 1) * 512], ps_y[n][0:C, :],
                                      ypart[:, n * 512:(n + 1) * 512], ALU.add)
            o.then_inc(s_y, 1)

        def dve_x_lo(dve, c, u):
            wait(dve, s_xhi, c * 2 + 2)
            for b, src, dst in rows_view(c, u):
                o = dve.tensor_tensor(dst[:, :, C:H], src, dst[:, :, 0:C].bitcast(F32), ALU.subtract)
            o.then_inc(s_xlo, 1)

        def dve_step(dve, c, u):
            start = isinstance(c, int) and c == 0
            if start:
                dve_x_lo(dve, 0, 0)
            for k in GATE:
                split(dve, "dve", c, k)
            if not start:
                if not (isinstance(c, int) and c == 1):
                    dve_y(dve, c - 1)
                dve_hidden(dve, c)
                split(dve, "dve", c, DOWN[0])
                dve_h_lo(dve, c)
                split(dve, "dve", c, DOWN[1])
            split(dve, "dve", c, UP[0])
            dve_sum(dve, c, 0, gate)
            split(dve, "dve", c, UP[1])
            dve_x_lo(dve, c + 1, 1 - u)

        def dve_tail(dve, c):
            dve_y(dve, c - 1)
            for k in DOWN:
                split(dve, "dve", c, k, True)
            dve_hidden(dve, c)
            dve_h_lo(dve, c)
            dve_y(dve, c)

        def pool_step(pool, c, u):
            for k in range(NPIECE):
                if not (isinstance(c, int) and c == 0 and k in DOWN):
                    split(pool, "pool", c, k)

        def pool_tail(pool, c):
            for k in DOWN:
                split(pool, "pool", c, k, True)
            pool.wait_ge(s_st, c * 16)

        def sp_load(sp, c, k, q, e, last=False):
            made(sp, LO, s_lo, c - 1, k)
            sp.dma_start(m.raw[:, k, :], piece_src(m, L, q, e)).then_inc(m.load[L][k], 16)

        def sp_step(sp, c, e, before):
            for k, q in ((0, 0), (1, 1)):
                sp_load(sp, c, k, q, e)
            if not (isinstance(c, int) and c == 1):
                for k, q in ((2, 4), (3, 5)):
                    sp_load(sp, c, k, q, before)
            for k, q in ((4, 2), (5, 3)):
                sp_load(sp, c, k, q, e)

        def pipeline(eng, step, tail):
            step(eng, 0, 0)
            step(eng, 1, 1)
            with eng.Fori(1, E // 2) as i:
                step(eng, i * 2, 0)
                step(eng, i * 2 + 1, 1)
            n = eng.value_load(m.novf[0:1, 0:1], min_val=0, max_val=N_OVF)
            with eng.Fori(0, N_OVF // 2) as j:
                with eng.If(j * 2 < n):
                    step(eng, j * 2 + E, 0)
                with eng.If(j * 2 + 1 < n):
                    step(eng, j * 2 + (E + 1), 1)
            tail(eng, n + E)

        block = ctx.enter_context(nc.Block())

        @block.sync
        def _(sp):
            def expert(i):
                return sp.value_load(m.ovf_e[0:1, bass.ds(i, 1)], min_val=0, max_val=E - 1)

            sp_step(sp, 1, 1, 0)
            sp_step(sp, 2, 2, 1)
            with sp.Fori(3, E) as c:
                sp_step(sp, c, c, c - 1)
            n = sp.value_load(m.novf[0:1, 0:1], min_val=0, max_val=N_OVF)
            with sp.Fori(0, N_OVF) as j:
                with sp.If(j < n):
                    sp_step(sp, j + E, expert(j + 1), expert(j))
            e = expert(n)
            for k, q in ((2, 4), (3, 5)):
                sp_load(sp, n + E, k, q, e)

        @block.scalar
        def _(act):
            pipeline(act, act_step, act_tail)

        @block.vector
        def _(dve):
            pipeline(dve, dve_step, dve_tail)

        @block.gpsimd
        def _(pool):
            pipeline(pool, pool_step, pool_tail)

        @block.tensor
        def _(pe):
            pipeline(pe, pe_step, lambda eng, c: pe_down(eng, c, True))


def combine(nc, m, L):
    with ExitStack() as ctx:
        rows = ctx.enter_context(nc.sbuf_tensor(f"k{L}_rows", [P, NT, 2, D], F32))
        s_in = [m.sem(f"k{L}_in{t}") for t in range(NT)]
        s_add = m.sem(f"k{L}_added")
        block = ctx.enter_context(nc.Block())

        @block.gpsimd
        def _(pool):
            for t in range(NT):
                for k in range(2):
                    pool.indirect_dma_start(out=rows[:, t, k, :], out_offset=None, in_=m.slots_y[:, :],
                                            in_offset=bass.IndirectOffsetOnAxis(ap=m.idx[:, t, k:k + 1], axis=0)
                                            ).then_inc(s_in[t], 16)

        @block.vector
        def _(dve):
            for t in range(NT):
                dve.wait_ge(s_in[t], 32)
                for k in range(2):
                    dve.scalar_tensor_tensor(out=m.x[:, t, :], in0=rows[:, t, k, :], scalar=m.wts[:, t, k:k + 1],
                                             in1=m.x[:, t, :], op0=ALU.mult, op1=ALU.add).then_inc(s_add, 1)
                    dve.wait_ge(s_add, 2 * t + k + 1)


def final_norm(nc, m):
    with ExitStack() as ctx:
        gb = ctx.enter_context(nc.sbuf_tensor("f_gb", [P, D], F32))
        y = ctx.enter_context(nc.sbuf_tensor("f_y", [P, NT, D], F32))
        junk = ctx.enter_context(nc.sbuf_tensor("f_junk", [P, D], F32))
        tmp = ctx.enter_context(nc.sbuf_tensor("f_tmp", [P, NT], F32))
        nrm = Norm(m, "f", 4)
        s_gb, s_out = m.sem("f_gain_in"), m.sem("f_out")
        block = ctx.enter_context(nc.Block())
        out = m.out.rearrange("b (t p) d -> t p (b d)", p=P)

        @block.sync
        def _(sp):
            sp.dma_start(gb[:], m.a["norm_final"].rearrange("(a d) -> a d", a=1).broadcast_to([P, D])).then_inc(s_gb, 16)
            for t in range(NT):
                sp.wait_ge(nrm.xn, t + 1)
                sp.dma_start(out[t], y[:, t, :]).then_inc(s_out, 16)
            sp.wait_ge(s_out, 16 * NT)

        @block.scalar
        def _(act):
            nrm.scalar_stats(act, junk[:])

        @block.vector
        def _(dve):
            nrm.vector_stats(dve, tmp[:])
            dve.wait_ge(s_gb, 16)
            for t in range(NT):
                dve.scalar_tensor_tensor(out=y[:, t, :], in0=m.x[:, t, :], scalar=m.rstd[:, 4, t:t + 1], in1=gb[:],
                                         op0=ALU.mult, op1=ALU.mult).then_inc(nrm.xn, 1)


N_SHARED = 2


def shared_kv(nc, m, ctx):
    a = m.a

    def keep(name, shape, dt=F32):
        return ctx.enter_context(nc.sbuf_tensor("a_" + name, shape, dt))

    m.kT = keep("kT", [P, 2, NG, S])
    m.v = keep("v", [P, NT, 2, NG, HD])
    m.q = keep("q", [P, NK, S])
    m.qr = keep("qr", [P, NK, S])
    m.gates = keep("gates", [P, NT, NH, NBR])
    m.kc = keep("kc", [P, NG, NCMP])
    m.vc = keep("vc", [NCMP, NG, HD])
    with ExitStack() as between:
        cvT = between.enter_context(nc.sbuf_tensor("b_cvT", [P, 2, 2, S], F32))
        for stage, letter in ((norm_and_project, "b_"), (compress, "z_")):
            with ExitStack() as tmp:
                def sb(name, shape, dt=F32):
                    return tmp.enter_context(nc.sbuf_tensor(letter + name, shape, dt))

                stage(nc, m, sb, cvT)


def norm_and_project(nc, m, sb, cvT):
    a = m.a
    NF = 4 + 4 + 8
    hkv = sb("hkv", [P, NK, S])
    hq = sb("hq", [P, NK, S])
    gain = sb("gain", [P, 2, NK])
    wk = m.raw[:, 0:2, :].rearrange("p b (k n) -> p b k n", k=NK)
    wv = m.raw[:, 2:4, :].rearrange("p b (k n) -> p b k n", k=NK)
    wg = sb("wg", [P, NK, NH * NBR])
    rope = sb("rope", [P, 2, S])
    perm = sb("perm", [P, P])
    raw = sb("rawk", [P, 2, S])
    prod = sb("prod", [P, 2, S])
    junk = prod[:].rearrange("p b s -> p (b s)")
    xn = m.qr[:].rearrange("p k s -> p (k s)").rearrange("p (t d) -> p t d", t=NT)
    small = sb("tmp", [P, NT])
    posi = sb("posi", [P, S], I32)
    freq = sb("freq", [P, 1])
    ang = m.qr[:, 0:3, :]
    gtmp = sb("gtmp", [P, NT, NH * NBR])
    nrm = Norm(m, "b", 2)
    s_gain, s_wg, s_pos = m.sem("b_gain_in"), m.sem("b_gate_w_in"), m.sem("b_pos_in")
    s_wk = [m.sem(f"b_wk{i}") for i in range(2)]
    s_wv = m.sem("b_wv_in")
    s_feat, s_tok = m.sem("b_features"), m.sem("b_tokens")
    s_raw, s_swap, s_rot = m.sem("b_raw"), m.sem("b_swapped"), m.sem("b_rotated")
    s_own, s_sin, s_ang, s_perm = m.sem("b_own2"), m.sem("b_sin"), m.sem("b_angles"), m.sem("b_perm")
    s_cv, s_v, s_g, s_ge = m.sem("b_cv"), m.sem("b_v"), m.sem("b_gate"), m.sem("b_gate_exp")
    block_of = nc.Block()
    cols = [("w_kv", 0), ("w_kv", 256), ("w_kv", 512), ("w_kv", 1024)] + [("attn_w_in", 256 * i) for i in range(4)]

    def weight(name, c, n):
        w = a[name] if name == "w_kv" else a[name][0]
        return w.rearrange("(p k) c -> p k c", k=NK)[:, :, c:c + n]

    rotated = list(range(4, NF))
    with block_of as block:

        @block.sync
        def _(sp):
            with nc.allow_non_contiguous_dma(reason="small vectors"):
                sp.dma_start(gain[:, 0, :], a["norm_kv"].rearrange("(p k) -> p k", k=NK)).then_inc(s_gain, 16)
                sp.dma_start(gain[:, 1, :], a["norm_mix"][1].rearrange("(p k) -> p k", k=NK)).then_inc(s_gain, 16)
                for i in range(4):
                    sp.dma_start(freq[32 * i:32 * i + 32, :], a["inv_freq"].rearrange("(p a) -> p a", a=1)
                                 ).then_inc(s_pos, 16)
            sp.dma_start(posi[:], a["positions"].broadcast_to([P, S])).then_inc(s_pos, 16)
            for n, (name, c) in enumerate(cols):
                if n >= 2:
                    sp.wait_ge(s_feat, 2 * (n - 1))
                sp.dma_start(wk[:, n % 2, :, :], weight(name, c, 256)).then_inc(s_wk[n % 2], 16)
                if n == 1:
                    sp.dma_start(wv[:, 0, :, :], weight("w_kv", 768, 256)).then_inc(s_wv, 16)
                    sp.dma_start(wv[:, 1, :, :], weight("w_kv", 1280, 256)).then_inc(s_wv, 16)
                    sp.dma_start(wg[:], weight("attn_w_in", NH * HD, NH * NBR)).then_inc(s_wg, 16)

        @block.gpsimd
        def _(pool):
            for i in range(4):
                o = 32 * (i ^ 1)
                p = pool.tensor_copy(perm[:, 32 * i:32 * i + 32], m.ident[:, o:o + 32])
            p.then_inc(s_perm, 1)

        @block.scalar
        def _(act):
            nrm.scalar_stats(act, junk)
            act.wait_ge(s_gain, 32)
            nrm.evacuate(act, 0, [(hkv, gain[:, 0, :]), (hq, gain[:, 1, :])])
            act.wait_ge(s_ang, 1)
            act.activation(rope[:, 0, :], ang[:, 1, :], ACT.Sin).then_inc(s_sin, 1)
            act.activation(rope[:, 1, :], ang[:, 0, :], ACT.Sin).then_inc(s_sin, 1)
            for i in range(NF):
                act.wait_ge(s_feat, i + 1)
                if i < 4:
                    act.activation(cvT[:, i // 2, i % 2, :], m.ps[i % 4][:], ACT.Copy).then_inc(s_raw, 1)
                else:
                    if i >= 6 and i < 8:
                        act.wait_ge(s_rot, i - 5)
                    dst = raw[:, i % 2, :] if i < 8 else m.q[:, i - 8, :]
                    act.activation(dst, m.ps[i % 4][:], ACT.Copy).then_inc(s_raw, 1)
            for t in range(NT):
                act.wait_ge(s_g, t + 1)
            act.activation(gtmp[:], gtmp[:], ACT.Exp, scale=-1.0).then_inc(s_ge, 1)

        @block.vector
        def _(dve):
            own = Chain(dve, s_own)
            nrm.vector_stats(dve, small[:])
            nrm.vector_normed(dve, xn)
            dve.wait_ge(s_gain, 32)
            nrm.evacuate(dve, 1, [(hkv, gain[:, 0, :]), (hq, gain[:, 1, :])])
            dve.wait_ge(s_pos, 16 * 5)
            a0, a1, a2 = (ang[:, i, :] for i in range(3))
            own.step(dve.tensor_copy(a1, posi[:]))
            own.step(dve.tensor_scalar(a0, a1, freq[:, 0:1], None, ALU.mult))
            own.step(dve.tensor_scalar(a1, a0, 1.0 / (2 * PI), MAGIC, ALU.mult, ALU.add))
            own.step(dve.tensor_scalar(a1, a1, MAGIC, None, ALU.subtract))
            own.step(dve.scalar_tensor_tensor(out=a0, in0=a1, scalar=-TWO_PI[0], in1=a0, op0=ALU.mult, op1=ALU.add))
            own.step(dve.scalar_tensor_tensor(out=a0, in0=a1, scalar=-TWO_PI[1], in1=a0, op0=ALU.mult, op1=ALU.add))
            own.step(dve.scalar_tensor_tensor(out=a0, in0=a1, scalar=-TWO_PI[2], in1=a0, op0=ALU.mult, op1=ALU.add))
            own.step(dve.tensor_scalar(a0, a0, PI32, -PI32, ALU.min, ALU.max))
            own.step(dve.tensor_scalar(a2, a0, -1.0, None, ALU.mult))
            own.step(dve.tensor_tensor(a2, a2, a0, ALU.max))
            dve.tensor_scalar(a1, a2, -1.0, PI / 2, ALU.mult, ALU.add).then_inc(s_ang, 1)
            dve.wait_ge(s_sin, 2)
            for i in (0, 2):
                own.step(dve.tensor_scalar(rope[32 * i:32 * i + 32, 1, :], rope[32 * i:32 * i + 32, 1, :], -1.0, None,
                                           ALU.mult))
            for j, i in enumerate(rotated):
                src = raw[:, i % 2, :] if i < 8 else m.q[:, i - 8, :]
                dve.wait_ge(s_raw, i + 1)
                dve.tensor_tensor(prod[:, 0, :], src, rope[:, 0, :], ALU.mult).then_inc(s_v, 1)
                dve.wait_ge(s_swap, j + 1)
                own.step(dve.tensor_tensor(prod[:, 1, :], m.ps[4 + j % 2][:], rope[:, 1, :], ALU.mult))
                dve.wait_ge(s_v, j + 1)
                if i < 8:
                    br, g0 = (i - 4) // 2, 2 * (i % 2)
                    for g in range(2):
                        rows = slice(64 * g, 64 * g + 64)
                        for to in range(2):
                            r = dve.tensor_tensor(m.kT[64 * to:64 * to + 64, br, g0 + g, :], prod[rows, 0, :],
                                                  prod[rows, 1, :], ALU.add)
                else:
                    r = dve.tensor_tensor(m.qr[:, i - 8, :], prod[:, 0, :], prod[:, 1, :], ALU.add)
                r.then_inc(s_rot, 1)
                dve.wait_ge(s_rot, j + 1)
            for t in range(NT):
                dve.wait_ge(s_tok, t + 1)
                dve.tensor_copy(m.v[:, t, :, :, :].rearrange("p b g d -> p (b g d)"), m.ps[6][:]).then_inc(s_cv, 1)
                dve.tensor_copy(gtmp[:, t, :], m.ps[7][:, 0:NH * NBR]).then_inc(s_g, 1)
            dve.wait_ge(s_ge, 1)
            own.step(dve.tensor_scalar(gtmp[:], gtmp[:], 1.0, None, ALU.add))
            own.step(dve.reciprocal(m.gates[:].rearrange("p t h b -> p t (h b)"), gtmp[:]))

        @block.tensor
        def _(pe):
            nrm.tensor(pe, xn)
            nrm.wait_hT(pe)

            def swap(j):
                i = rotated[j]
                src = raw[:, i % 2, :] if i < 8 else m.q[:, i - 8, :]
                pe.wait_ge(s_raw, i + 1)
                if j == 0:
                    pe.wait_ge(s_perm, 1)
                if j >= 2:
                    pe.wait_ge(s_rot, j - 1)
                pe.matmul(m.ps[4 + j % 2][:], perm[:], src, start=True, stop=True).then_inc(s_swap, 1)

            for i in range(NF):
                n = i // 2
                pe.wait_ge(s_wk[n % 2], 16 * (n // 2 + 1))
                if i >= 4:
                    pe.wait_ge(s_raw, i - 3)
                h = hkv if i < 8 else hq
                for k in range(NK):
                    mm = pe.matmul(m.ps[i % 4][:], wk[:, n % 2, k, (i % 2) * P:(i % 2 + 1) * P], h[:, k, :],
                                   start=(k == 0), stop=(k == NK - 1))
                mm.then_inc(s_feat, 1)
                if i >= 5:
                    swap(i - 5)
            swap(len(rotated) - 1)
            pe.wait_ge(s_wv, 32)
            pe.wait_ge(s_wg, 16)
            for t in range(NT):
                if t:
                    pe.wait_ge(s_g, t)
                for k in range(NK):
                    pe.matmul(m.ps[6][:].rearrange("p (b c) -> p b c", b=2), hkv[:, k, t * P:(t + 1) * P], wv[:, :, k, :],
                              start=(k == 0), stop=(k == NK - 1))
                for k in range(NK):
                    mm = pe.matmul(m.ps[7][:, 0:NH * NBR], hq[:, k, t * P:(t + 1) * P], wg[:, k, :],
                                   start=(k == 0), stop=(k == NK - 1))
                mm.then_inc(s_tok, 1)


def compress(nc, m, sb, cvT):
    a = m.a
    NJ = CMP // 2
    NB = NG * NCMP
    two = sb("two", [P, 2, NG, S])
    blk = sb("blk", [P, 2, NJ, NG, NCMP])
    pos = sb("pos", [P, 2, NJ])
    w1 = m.raw[:, 0:4, :].rearrange("p (i h) (j n) -> p i (h j) n", i=2, n=HID)
    w2 = sb("w2", [P, 2, 2, HD])
    hid = sb("hid", [P, 2, HID])
    t1 = sb("t1", [P, 2, HID])
    hT = sb("hidT", [P, 2, 2, NB])
    s_in = [m.sem("z_w1_in"), m.sem("z_pos_in")]
    s_two, s_blk, s_hid, s_hs = m.sem("z_two"), m.sem("z_blocks"), m.sem("z_hidden"), m.sem("z_hid_sb")
    s_th, s_gelu, s_tr, s_hT, s_out = (m.sem(n) for n in ("z_tanh", "z_gelu", "z_tr", "z_hT", "z_out"))
    s_own, s_kc = m.sem("z_own"), m.sem("z_kc")
    with nc.Block() as block:

        @block.sync
        def _(sp):
            with nc.allow_non_contiguous_dma(reason="2,048 position embeddings"):
                for i, c in enumerate("kv"):
                    sp.dma_start(w1[:, i], a[f"cmp_w1_{c}"].rearrange("(j p) n -> p j n", p=P)).then_inc(s_in[0], 16)
                    sp.dma_start(w2[:, i], a[f"cmp_w2_{c}"].rearrange("(k p) n -> p k n", p=P)).then_inc(s_in[0], 16)
                    sp.dma_start(pos[:, i], a[f"cmp_pos_{c}"].rearrange("(j two) d -> (two d) j", two=2)
                                 ).then_inc(s_in[1], 16)

        @block.vector
        def _(dve):
            own = Chain(dve, s_own)
            for i in range(2):
                for g in range(NG):
                    src = cvT[64 * (g % 2):64 * (g % 2) + 64, i, g // 2, :]
                    dve.tensor_copy(two[0:64, i, g, :], src)
                    c = dve.tensor_copy(two[64:P, i, g, 0:S - 1], src[:, 1:S])
                c.then_inc(s_two, 1)
            dve.wait_ge(s_in[1], 32)
            for i in range(2):
                dve.wait_ge(s_two, i + 1)
                for j in range(NJ):
                    src = two[:, i, :, 2 * j:2 * j + (NCMP - 1) * STRIDE + 1:STRIDE]
                    b = dve.tensor_scalar(blk[:, i, j], src, pos[:, i, j:j + 1], None, ALU.add)
                b.then_inc(s_blk, 1)
            for i in range(2):
                dve.wait_ge(s_hid, i + 1)
                h, t = hid[0:NB, i, :], t1[0:NB, i, :]
                own.step(dve.tensor_copy(h, m.ps[i][0:NB, 0:HID]))
                own.step(dve.tensor_tensor(t, h, h, ALU.mult))
                own.step(dve.tensor_scalar(t, t, 0.044715, 1.0, ALU.mult, ALU.add))
                dve.tensor_tensor(t, t, h, ALU.mult).then_inc(s_hs, 1)
            for i in range(2):
                h, t = hid[0:NB, i, :], t1[0:NB, i, :]
                dve.wait_ge(s_th, i + 1)
                own.step(dve.tensor_scalar(t, t, 1.0, 0.5, ALU.add, ALU.mult))
                dve.tensor_tensor(h, h, t, ALU.mult).then_inc(s_gelu, 1)
            for i in range(2):
                dve.wait_ge(s_tr, i + 1)
                dve.tensor_copy(hT[:, i], m.ps[2 + i][:, 0:2 * NB].rearrange("p (k n) -> p k n", k=2)).then_inc(s_hT, 1)
            dve.wait_ge(s_out, 1)
            for to in range(2):
                dve.tensor_copy(m.kc[64 * to:64 * to + 64].rearrange("p g c -> p (g c)"), m.ps[4][0:64, 0:NB]
                                ).then_inc(s_kc, 1)
            dve.wait_ge(s_out, 2)
            dve.tensor_copy(m.vc[:].rearrange("p g d -> p (g d)"), m.ps[5][0:NCMP, 0:NG * HD]).then_inc(s_kc, 1)

        @block.scalar
        def _(act):
            for i in range(2):
                act.wait_ge(s_hs, i + 1)
                act.activation(t1[0:NB, i, :], t1[0:NB, i, :], ACT.Tanh, scale=(2 / PI) ** 0.5).then_inc(s_th, 1)

        @block.tensor
        def _(pe):
            pe.wait_ge(s_in[0], 64)
            for i in range(2):
                pe.wait_ge(s_blk, i + 1)
                for j in range(NJ):
                    mm = pe.matmul(m.ps[i][0:NB, 0:HID], blk[:, i, j].rearrange("p g c -> p (g c)"), w1[:, i, j, :],
                                   start=(j == 0), stop=(j == NJ - 1))
                mm.then_inc(s_hid, 1)
            for i in range(2):
                pe.wait_ge(s_gelu, i + 1)
                for k in range(2):
                    tr = pe.transpose(m.ps[2 + i][:, k * NB:(k + 1) * NB], hid[0:NB, i, k * P:(k + 1) * P],
                                      m.ident[0:NB, 0:NB])
                tr.then_inc(s_tr, 1)
            pe.wait_ge(s_hT, 2)
            for k in range(2):
                mm = pe.matmul(m.ps[4][0:64, 0:NB], w2[:, 0, k, :], hT[:, 0, k, :], start=(k == 0), stop=(k == 1))
            mm.then_inc(s_out, 1)
            for g in range(NG):
                for k in range(2):
                    mm = pe.matmul(m.ps[5][0:NCMP, g * HD:(g + 1) * HD], hT[:, 1, k, g * NCMP:(g + 1) * NCMP],
                                   w2[:, 1, k, :], start=(k == 0), stop=(k == 1))
            mm.then_inc(s_out, 1)


def attention(nc, m):
    a = m.a
    with ExitStack() as ctx:
        def sb(name, shape, dt=F32):
            return ctx.enter_context(nc.sbuf_tensor("t_" + name, shape, dt))

        causal = sb("causal", [P, P], BF16)
        cmask = sb("cmask", [P, NT, NCMP])
        zero = sb("zero", [P, P])
        oT = m.q
        wout = sb("wout", [P, NK, D])
        pr = sb("pr", [P, 2, HPG, S])
        prT = sb("prT", [P, 2, NT, HPG * P])
        pc = sb("pc", [P, 2, HPG, NCMP])
        pcT = sb("pcT", [NCMP, HPG * P])
        mx = sb("mx", [P, 2, HPG])
        sm = sb("sm", [P, 2, HPG])
        s_wo, s_mask, s_z = m.sem("t_wout_in"), m.sem("t_masks"), m.sem("t_zero")
        s_sc, s_mx, s_ex, s_pn = m.sem("t_scores"), m.sem("t_max"), m.sem("t_exp"), m.sem("t_scaled")
        s_tr, s_prT, s_pv, s_oT = m.sem("t_tr"), m.sem("t_prT"), m.sem("t_pv"), m.sem("t_oT")
        s_own, s_o, s_res = m.sem("t_own"), m.sem("t_out"), m.sem("t_res")
        steps = [(t, g, b) for t in range(NT) for g in range(NG) for b in range(NBR)]
        tiles = [1 if b == 0 else t + 1 for t, g, b in steps]
        before = [sum(tiles[:i]) for i in range(len(steps) + 1)]

        block = ctx.enter_context(nc.Block())

        @block.sync
        def _(sp):
            sp.dma_start(wout[:], a["attn_w_out"][0].rearrange("(j p) n -> p j n", p=P)).then_inc(s_wo, 16)
            prefetch(sp, m, 1)

        @block.gpsimd
        def _(pool):
            pool.memset(zero[:], 0.0).then_inc(s_z, 1)
            pool.wait_ge(s_z, 1)
            pool.affine_select(out=causal[:], in_=zero[:], compare_op=ALU.is_ge, fill=NEG, base=0,
                               pattern=[[-1, P]], channel_multiplier=1).then_inc(s_mask, 1)
            for t in range(NT):
                pool.affine_select(out=cmask[:, t, :], in_=zero[:, 0:NCMP], compare_op=ALU.is_ge, fill=NEG,
                                   base=t * P - (CMP - 1), pattern=[[-STRIDE, NCMP]],
                                   channel_multiplier=1).then_inc(s_mask, 1)

        @block.tensor
        def _(pe):
            pe.wait_ge(s_mask, 1 + NT)

            def scores(i):
                t, g, b = steps[i]
                for h in range(HPG):
                    head = g * HPG + h
                    rows = slice(64 * (head % 2), 64 * (head % 2) + 64)
                    if i:
                        pe.wait_ge(s_ex, HPG * (i - 1) + h + 1)
                    if b == 0:
                        mm = pe.matmul(m.ps[h][:, 0:NCMP], m.q[rows, head // 2, t * P:(t + 1) * P], m.kc[rows, g, :],
                                       start=True, stop=True)
                    else:
                        n = (t + 1) * P
                        pe.matmul(m.ps[h][:, 0:n], m.qr[rows, head // 2, t * P:(t + 1) * P],
                                  m.kT[rows, b - 1, g, 0:n], start=True, stop=False)
                        mm = pe.matmul(m.ps[h][:, t * P:n], m.identb[:], causal[:], start=False, stop=True)
                    mm.then_inc(s_sc, 1)

            def values(i):
                t, g, b = steps[i]
                src, n = (pc, 1) if b == 0 else (pr, t + 1)
                for j in range(n):
                    bank = m.ps[4 + (before[i] + j) % 2]
                    if before[i] + j >= 2:
                        pe.wait_ge(s_prT, before[i] + j - 1)
                    for h in range(HPG):
                        if j == 0:
                            pe.wait_ge(s_pn, HPG * i + h + 1)
                        if b == 0:
                            tr = pe.transpose(bank[0:NCMP, h * P:(h + 1) * P], pc[:, i % 2, h, :], m.ident[:])
                        else:
                            tr = pe.transpose(bank[:, h * P:(h + 1) * P], pr[:, i % 2, h, j * P:(j + 1) * P], m.ident[:])
                    tr.then_inc(s_tr, 1)

            def product(i):
                t, g, b = steps[i]
                o = i // NBR
                if b == 0 and o >= 2:
                    pe.wait_ge(s_oT, o - 1)
                n = 1 if b == 0 else t + 1
                for j in range(n):
                    pe.wait_ge(s_prT, before[i] + j + 1)
                    if b == 0:
                        mm = pe.matmul(m.ps[6 + o % 2][0:HD, :], m.vc[:, g, :], pcT[:], start=True, stop=False)
                    else:
                        mm = pe.matmul(m.ps[6 + o % 2][0:HD, :], m.v[:, j, b - 1, g, :], prT[:, i % 2, j, :],
                                       start=False, stop=(b == 2 and j == t))
                mm.then_inc(s_pv, 1)

            for i in range(len(steps) + 2):
                if i < len(steps):
                    scores(i)
                if i >= 1 and i - 1 < len(steps):
                    values(i - 1)
                if i >= 2:
                    product(i - 2)
            pe.wait_ge(s_wo, 16)
            pe.wait_ge(s_oT, len(steps) // NBR)
            project_out(pe, m, oT, wout, s_o)

        @block.vector
        def _(dve):
            own = Chain(dve, s_own)
            dve.wait_ge(s_mask, 1 + NT)

            def maxima(i):
                t, g, b = steps[i]
                if i >= 2:
                    dve.wait_ge(s_ex, HPG * (i - 1))
                for h in range(HPG):
                    dve.wait_ge(s_sc, HPG * i + h + 1)
                    if b == 0:
                        own.step(dve.tensor_tensor(pc[:, i % 2, h, :], m.ps[h][:, 0:NCMP], cmask[:, t, :], ALU.add))
                        own.step(dve.tensor_reduce(mx[:, i % 2, h:h + 1], pc[:, i % 2, h, :], AX.X, ALU.max))
                        dve.tensor_scalar(mx[:, i % 2, h:h + 1], mx[:, i % 2, h:h + 1], 0.1 * NEG, -SCALE,
                                          ALU.max, ALU.mult).then_inc(s_mx, 1)
                    else:
                        own.step(dve.tensor_reduce(mx[:, i % 2, h:h + 1], m.ps[h][:, 0:(t + 1) * P], AX.X, ALU.max))
                        dve.tensor_scalar(mx[:, i % 2, h:h + 1], mx[:, i % 2, h:h + 1], -SCALE, None,
                                          ALU.mult).then_inc(s_mx, 1)

            def scale(i):
                t, g, b = steps[i]
                dve.wait_ge(s_ex, HPG * (i + 1))
                own.step(dve.tensor_scalar(sm[:, i % 2, :], sm[:, i % 2, :], 1e-30, None, ALU.max))
                own.step(dve.reciprocal(sm[:, i % 2, :], sm[:, i % 2, :]))
                own.step(dve.tensor_tensor(sm[:, i % 2, :], sm[:, i % 2, :],
                                           m.gates[:, t, g * HPG:(g + 1) * HPG, b], ALU.mult))
                for h in range(HPG):
                    p = pc[:, i % 2, h, :] if b == 0 else pr[:, i % 2, h, 0:(t + 1) * P]
                    dve.tensor_scalar(p, p, sm[:, i % 2, h:h + 1], None, ALU.mult).then_inc(s_pn, 1)

            def transposed(i):
                t, g, b = steps[i]
                for j in range(1 if b == 0 else t + 1):
                    n = before[i] + j
                    dve.wait_ge(s_tr, n + 1)
                    if b == 0 and i >= 3:
                        dve.wait_ge(s_pv, i - 2)
                    if b and i >= 2:
                        dve.wait_ge(s_pv, i - 1)
                    if b == 0:
                        dve.tensor_copy(pcT[:], m.ps[4 + n % 2][0:NCMP, :]).then_inc(s_prT, 1)
                    else:
                        dve.tensor_copy(prT[:, i % 2, j, :], m.ps[4 + n % 2][:]).then_inc(s_prT, 1)

            for i in range(len(steps) + 1):
                if i < len(steps):
                    maxima(i)
                if i >= 1:
                    scale(i - 1)
                    transposed(i - 1)
            add_residual(dve, m, s_o, s_res)

        @block.scalar
        def _(act):
            def exps(i):
                t, g, b = steps[i]
                if i >= 2:
                    act.wait_ge(s_tr, before[i - 1])
                for h in range(HPG):
                    act.wait_ge(s_mx, HPG * i + h + 1)
                    n = NCMP if b == 0 else (t + 1) * P
                    src = pc[:, i % 2, h, :] if b == 0 else m.ps[h][:, 0:n]
                    dst = pc[:, i % 2, h, :] if b == 0 else pr[:, i % 2, h, 0:n]
                    act.activation(dst, src, ACT.Exp, bias=mx[:, i % 2, h:h + 1], scale=SCALE,
                                   accum_out=sm[:, i % 2, h:h + 1]).then_inc(s_ex, 1)

            def out(o):
                t, g = o // NG, o % NG
                act.wait_ge(s_pv, NBR * (o + 1))
                src = m.ps[6 + o % 2][0:HD, :].rearrange("p (j two q) -> p j two q", j=2, two=2)
                for half in range(2):
                    c = act.activation(oT[64 * half:64 * half + 64, 2 * g:2 * g + 2, t * P:(t + 1) * P],
                                       src[:, :, half, :], ACT.Copy)
                c.then_inc(s_oT, 1)

            for i in range(len(steps) + 3):
                if i < len(steps):
                    exps(i)
                if i >= 5 and (i - 5) % NBR == 0:
                    out((i - 5) // NBR)


_INS = ["x", "positions", "norm_mix", "norm_ffn", "conv_w_in", "conv_w", "conv_w_out", "norm_kv", "w_kv",
        "cmp_pos_k", "cmp_w1_k", "cmp_w2_k", "cmp_pos_v", "cmp_w1_v", "cmp_w2_v", "attn_w_in", "attn_w_out",
        "router_group_w", "router_group_b", "router_expert_w", "router_expert_b",
        "expert_w_gate", "expert_w_up", "expert_w_down", "norm_final"]


def kernel(**inputs):
    import numpy as np
    import concourse.bacc as bacc
    from concourse.bass_utils import run_bass_kernel_spmd

    nc = bacc.Bacc("TRN2", target_bir_lowering=False, num_devices=1)
    arrays = {f"in_{name}": np.ascontiguousarray(inputs[name]) for name in _INS}
    half = HD // 2
    arrays["in_inv_freq"] = (np.float32(10000.0) ** (-np.arange(half, dtype=np.float32) / np.float32(half)))
    a = {name[3:]: nc.dram_tensor(name, v.shape, mybir.dt.from_np(v.dtype), kind="ExternalInput").ap()
         for name, v in arrays.items()}
    out = nc.dram_tensor("out_0", (1, S, D), F32, kind="ExternalOutput").ap()
    program(nc, a, out)
    r = run_bass_kernel_spmd(nc, [arrays], core_ids=[0])
    return r.results[0]["out_0"]
```

```python
from contextlib import ExitStack

import concourse.bass as bass
from concourse import mybir

ALU = mybir.AluOpType
ACT = mybir.ActivationFunctionType
AX = mybir.AxisListType
F32 = mybir.dt.float32
F32R = mybir.dt.float32r
BF16 = mybir.dt.bfloat16
I32 = mybir.dt.int32
U32 = mybir.dt.uint32

P = 128
S = 512
D = 1024
NT = S // P
NK = D // P
EPS = 1e-6
NEG = -1e30

HD = 64
NH = 16
NG = 4
HPG = NH // NG
NBR = 3
CMP = 32
STRIDE = 16
NCMP = (S - CMP) // STRIDE + 1
NBLK = 32
HID = 256
SCALE = HD ** -0.5
MAGIC = 12582912.0
PI = 3.141592653589793
PI32 = 3.1415925
TWO_PI = (6.28125, 0.0019354820251464844, -1.7484556025237907e-07)

G = 4
EPG = 8
E = G * EPG
F = D // 2
KF = F // P
C = 64
N_OVF = 2 * S // C
ROWS = (E + N_OVF + 2) * C
NPIECE = 6
PIECE = 2048


class Chain:

    def __init__(self, eng, sem, base=0):
        self.eng, self.sem, self.n, self.base = eng, sem, 0, base

    def step(self, ins):
        self.n += 1
        ins.then_inc(self.sem, 1)
        self.eng.wait_ge(self.sem, self.base + self.n)


class Mem:
    pass


def program(nc, a, out):
    with ExitStack() as ctx:
        m = Mem()
        m.a, m.out = a, out

        def sb(name, shape, dt=F32):
            return ctx.enter_context(nc.sbuf_tensor(name, shape, dt))

        def sem(name):
            return ctx.enter_context(nc.semaphore(name))

        m.stage_sems = []

        def stage_sem(name):
            m.stage_sems.append(nc.alloc_semaphore(name=name))
            return m.stage_sems[-1]

        m.sem = stage_sem
        m.x = sb("x_res", [P, NT, D])
        m.raw = sb("raw", [P, NPIECE, PIECE])
        m.ident = sb("ident", [P, P])
        m.identb = sb("identb", [P, P], BF16)
        m.before = sb("before", [P, P], BF16)
        m.ones = sb("ones", [P, P], BF16)
        m.iota = sb("iota", [P, 48])
        m.ss = sb("ss", [P, 8])
        m.rstd = sb("rstd", [P, 5, NT])
        m.idx = sb("idx", [P, NT, 2], U32)
        m.wts = sb("wts", [P, NT, 2])
        m.novf = sb("novf", [1, 1], I32)
        m.ovf_e = sb("ovf_e", [1, N_OVF + 1], I32)
        m.ps = [ctx.enter_context(nc.psum_tensor(f"ps{i}", [P, 512], F32)) for i in range(8)]
        m.slots_x = nc.dram_tensor("slots_x", (ROWS, D), F32, kind="Internal").ap()
        m.slots_y = nc.dram_tensor("slots_y", (ROWS, D), F32, kind="Internal").ap()
        m.ready = sem("constants_ready")
        m.load = [[sem(f"load{L}_{q}") for q in range(NPIECE)] for L in range(2)]

        setup(nc, m)
        conv_mixer(nc, m)
        moe(nc, m, 0)
        combine(nc, m, 0)
        recycle_semaphores(nc, m)
        with ExitStack() as kvctx:
            shared_kv(nc, m, kvctx)
            attention(nc, m)
        moe(nc, m, 1)
        combine(nc, m, 1)
        final_norm(nc, m)


def moe(nc, m, L):
    with ExitStack() as ctx:
        w = Weights(nc, m, L, ctx)
        router(nc, m, L, w)
        experts(nc, m, L, w)


def recycle_semaphores(nc, m):
    nc.clear_and_free_semaphores(m.stage_sems)
    m.stage_sems = []
    nc.all_engine_barrier()


def setup(nc, m):
    filled = m.sem("const_filled")
    m.x_in = [m.sem(f"x_in{t}") for t in range(NT)]
    with nc.Block() as block:

        @block.sync
        def _(sp):
            for t in range(NT):
                sp.dma_start(m.x[:, t, :], m.a["x"][0, t * P:(t + 1) * P, :]).then_inc(m.x_in[t], 16)

        @block.gpsimd
        def _(pool):
            pool.memset(m.ident[:], 0.0).then_inc(filled, 1)
            pool.memset(m.ones[:], 1.0).then_inc(filled, 1)
            pool.iota(m.iota[:], [[1, 48]], base=0, channel_multiplier=0,
                      allow_small_or_imprecise_dtypes=True).then_inc(filled, 1)
            pool.wait_ge(filled, 3)
            pool.affine_select(out=m.ident[:], in_=m.ident[:], compare_op=ALU.not_equal, fill=1.0, base=0,
                               pattern=[[-1, P]], channel_multiplier=1).then_inc(filled, 1)
            pool.affine_select(out=m.before[:], in_=m.ones[:], compare_op=ALU.is_gt, fill=0.0, base=0,
                               pattern=[[1, P]], channel_multiplier=-1).then_inc(filled, 1)
            pool.wait_ge(filled, 5)
            pool.tensor_copy(m.identb[:], m.ident[:]).then_inc(m.ready, 1)
            pool.wait_ge(m.ready, 1)


def sum_squares(act, m, sq, junk, wait_tile):
    for t in range(NT):
        wait_tile(t)
        if t:
            act.wait_ge(sq, t)
        act.activation(junk, m.x[:, t, :], ACT.Square, accum_out=m.ss[:, t:t + 1]).then_inc(sq, 1)


class Norm:

    def __init__(self, m, name, n):
        self.m, self.n = m, n
        self.ms, self.rt = m.sem(name + "_mean"), m.sem(name + "_root")
        self.own, self.xn = m.sem(name + "_own"), m.sem(name + "_normed")
        self.tr, self.ev = m.sem(name + "_transposed"), [m.sem(name + "_hT_act"), m.sem(name + "_hT_dve")]

    def scalar_root(self, act):
        m = self.m
        act.wait_ge(self.ms, 1)
        act.activation(m.rstd[:, self.n, :], m.ss[:, 4:8], ACT.Sqrt).then_inc(self.rt, 1)

    def vector_stats(self, dve, tmp):
        m, own = self.m, Chain(dve, self.own)
        dve.tensor_scalar(m.ss[:, 4:8], m.ss[:, 0:4], 1.0 / D, EPS, ALU.mult, ALU.add).then_inc(self.ms, 1)
        dve.wait_ge(self.rt, 1)
        r = m.rstd[:, self.n, :]
        own.step(dve.reciprocal(r, r))
        own.step(dve.tensor_tensor(tmp, r, r, ALU.mult))
        own.step(dve.tensor_tensor(tmp, tmp, m.ss[:, 4:8], ALU.mult))
        own.step(dve.tensor_scalar(tmp, tmp, -0.5, 1.5, ALU.mult, ALU.add))
        own.step(dve.tensor_tensor(r, r, tmp, ALU.mult))

    def vector_normed(self, dve, xn):
        for t in range(NT):
            dve.tensor_scalar(xn[:, t, :], self.m.x[:, t, :], self.m.rstd[:, self.n, t:t + 1], None,
                              ALU.mult).then_inc(self.xn, 1)

    def tensor(self, pe, xn):
        for t in range(NT):
            pe.wait_ge(self.xn, t + 1)
            for k in range(NK):
                tr = pe.transpose(self.m.ps[k][:, t * P:(t + 1) * P], xn[:, t, k::NK], self.m.ident[:])
                if t == NT - 1:
                    tr.then_inc(self.tr, 1)

    def evacuate(self, eng, dve, outs):
        for k in range(dve, NK, 2):
            eng.wait_ge(self.tr, k + 1)
            for hT, gain in outs:
                src, g = self.m.ps[k][:], None if gain is None else gain[:, k:k + 1]
                if dve:
                    i = eng.tensor_copy(hT[:, k, :], src) if g is None else \
                        eng.tensor_scalar(hT[:, k, :], src, g, None, ALU.mult)
                else:
                    i = eng.activation(hT[:, k, :], src, ACT.Copy, scale=1.0 if g is None else g)
            i.then_inc(self.ev[dve], 1)

    def wait_hT(self, pe):
        pe.wait_ge(self.ev[0], NK // 2)
        pe.wait_ge(self.ev[1], NK // 2)


def conv_mixer(nc, m):
    a = m.a
    CW = 256
    NCH = D // CW
    with ExitStack() as ctx:
        def sb(name, shape, dt=F32):
            return ctx.enter_context(nc.sbuf_tensor(name, shape, dt))

        hT = sb("c_hT", [P, NK, S])
        gain = sb("c_gain", [P, NK])
        cw = sb("c_cw", [P, 3, NK])
        win = sb("c_win", [P, 2, NK, 3, CW])
        wout = sb("c_wout", [P, NK, D])
        gated = sb("c_gated", [P, NK, S])
        xn = gated.rearrange("p k s -> p (k s)").rearrange("p (t d) -> p t d", t=NT)
        u = sb("c_u", [P, 2, S + 2])
        csb = sb("c_csb", [P, 2, S])
        y = sb("c_y", [P, 2, S])
        tmp = sb("c_tmp", [P, NT])
        zero = sb("c_zero", [P, D])
        s_zero, s_blank = m.sem("c_zero_set"), m.sem("c_blank_rows")
        nrm = Norm(m, "c", 0)
        s_gain, s_cw, s_wout = m.sem("c_gain_in"), m.sem("c_cw_in"), m.sem("c_wout_in")
        s_win = [m.sem(f"c_win{i}") for i in range(2)]
        s_proj, s_cc, s_own = m.sem("c_projected"), m.sem("c_copied"), m.sem("c_own2")
        s_sq, s_sq2 = m.sem("c_squares"), m.sem("c_squares_after")
        s_u, s_gated, s_o, s_res = m.sem("c_u_done"), m.sem("c_gated_done"), m.sem("c_out"), m.sem("c_res")
        block = ctx.enter_context(nc.Block())
        w_in = a["conv_w_in"][0].rearrange("(p k) (c n w) -> n c p k w", k=NK, c=3, w=CW)

        @block.sync
        def _(sp):
            with nc.allow_non_contiguous_dma(reason="small vectors"):
                sp.dma_start(gain[:], a["norm_mix"][0].rearrange("(p k) -> p k", k=NK)).then_inc(s_gain, 16)
                sp.dma_start(cw[:], a["conv_w"][0].rearrange("w (j p) -> p w j", p=P)).then_inc(s_cw, 16)
            for n in range(NCH):
                if n >= 2:
                    sp.wait_ge(s_proj, 6 * (n - 1))
                for c in range(3):
                    sp.dma_start(win[:, n % 2, :, c, :], w_in[n, c]).then_inc(s_win[n % 2], 16)
            sp.dma_start(wout[:], a["conv_w_out"][0].rearrange("(j p) n -> p j n", p=P)).then_inc(s_wout, 16)
            prefetch(sp, m, 0)
            sp.wait_ge(s_zero, 1)
            blank = [m.slots_x[i * P:(i + 1) * P, :] for i in range(ROWS // P)]
            blank += [m.slots_y[i * P:(i + 1) * P, :] for i in range(E * C // P, ROWS // P)]
            for rows in blank:
                sp.dma_start(rows, zero[:]).then_inc(s_blank, 16)
            sp.wait_ge(s_blank, 16 * len(blank))

        @block.scalar
        def _(act):
            junk = y[:].rearrange("p b s -> p (b s)")
            sum_squares(act, m, s_sq, junk, lambda t: act.wait_ge(m.x_in[t], 16))
            nrm.scalar_root(act)
            act.wait_ge(s_gain, 16)
            nrm.evacuate(act, 0, [(hT, gain)])
            for j in range(NK):
                act.wait_ge(s_proj, 3 * j + 1)
                if j >= 2:
                    act.wait_ge(s_u, j - 1)
                act.activation(csb[:, j % 2, :], m.ps[3 * (j % 2)][:], ACT.Copy).then_inc(s_cc, 1)
            sum_squares(act, m, s_sq2, junk, lambda t: act.wait_ge(s_res, 2 * t + 2))

        @block.vector
        def _(dve):
            own = Chain(dve, s_own)
            dve.memset(zero[:], 0.0).then_inc(s_zero, 1)
            for b in range(2):
                own.step(dve.memset(u[:, b, 0:2], 0.0))
            dve.wait_ge(s_sq, NT)
            nrm.vector_stats(dve, tmp[:])
            nrm.vector_normed(dve, xn)
            dve.wait_ge(s_gain, 16)
            nrm.evacuate(dve, 1, [(hT, gain)])
            dve.wait_ge(s_cw, 16)
            for j in range(NK):
                b = j % 2
                dve.wait_ge(s_cc, j + 1)
                dve.wait_ge(s_proj, 3 * j + 2)
                dve.tensor_tensor(u[:, b, 2:], csb[:, b, :], m.ps[3 * b + 1][:], ALU.mult).then_inc(s_u, 1)
                dve.wait_ge(s_u, j + 1)
                own.step(dve.tensor_scalar(y[:, b, :], u[:, b, 0:S], cw[:, 0, j:j + 1], None, ALU.mult))
                for w in (1, 2):
                    own.step(dve.scalar_tensor_tensor(out=y[:, b, :], in0=u[:, b, w:w + S],
                                                      scalar=cw[:, w, j:j + 1], in1=y[:, b, :],
                                                      op0=ALU.mult, op1=ALU.add))
                dve.wait_ge(s_proj, 3 * j + 3)
                dve.tensor_tensor(gated[:, j, :], y[:, b, :], m.ps[3 * b + 2][:], ALU.mult).then_inc(s_gated, 1)
            add_residual(dve, m, s_o, s_res)

        @block.tensor
        def _(pe):
            nrm.tensor(pe, xn)
            nrm.wait_hT(pe)
            for j in range(NK):
                n = j // 2
                pe.wait_ge(s_win[n % 2], 48 * (n // 2 + 1))
                if j >= 2:
                    pe.wait_ge(s_gated, j - 1)
                for i, c in enumerate((1, 2, 0)):
                    for k in range(NK):
                        mm = pe.matmul(m.ps[3 * (j % 2) + i][:],
                                       win[:, n % 2, k, c, (j % 2) * P:(j % 2 + 1) * P], hT[:, k, :],
                                       start=(k == 0), stop=(k == NK - 1))
                    mm.then_inc(s_proj, 1)
            pe.wait_ge(s_wout, 16)
            pe.wait_ge(s_gated, NK)
            project_out(pe, m, gated, wout, s_o)


def project_out(pe, m, feats, w, s_o):
    for t in range(NT):
        for h in range(2):
            for k in range(NK):
                mm = pe.matmul(m.ps[2 * t + h][:], feats[:, k, t * P:(t + 1) * P], w[:, k, h * 512:(h + 1) * 512],
                               start=(k == 0), stop=(k == NK - 1))
            mm.then_inc(s_o, 1)


def add_residual(dve, m, s_o, s_res):
    for i in range(2 * NT):
        dve.wait_ge(s_o, i + 1)
        x = m.x[:, i // 2, (i % 2) * 512:(i % 2 + 1) * 512]
        dve.tensor_tensor(x, x, m.ps[i][:], ALU.add).then_inc(s_res, 1)


def piece_src(m, L, q, e):
    name = ("expert_w_gate", "expert_w_up", "expert_w_down")[q // 2]
    w = m.a[name][L]
    if q < 4:
        w = w.rearrange("e (p h k) n -> h e p (k n)", p=P, h=2)[q % 2]
    else:
        w = w.rearrange("e (h p k) n -> h e p (k n)", h=2, p=P)[q % 2]
    return w[e] if isinstance(e, int) else w[bass.ds(e, 1)].rearrange("e p n -> (e p) n")


def prefetch(sp, m, L, slots=(0, 1, 4, 5, 2, 3)):
    piece = {0: 0, 1: 1, 4: 2, 5: 3, 2: 4, 3: 5}
    for slot in slots:
        q = piece[slot]
        sp.dma_start(m.raw[:, slot, :], piece_src(m, L, q, 0)).then_inc(m.load[L][slot], 16)


def router(nc, m, L, w):
    a = m.a
    with ExitStack() as ctx:
        def sb(name, shape, dt=F32):
            return ctx.enter_context(nc.sbuf_tensor(f"r{L}_{name}", shape, dt))

        def sem(name):
            return m.sem(f"r{L}_{name}")

        NL = G + E
        xn = sb("xn", [P, NT, D])
        hT = sb("hT", [P, NK, S])
        gb = sb("gb", [P, D])
        wr = sb("wr", [P, NK, NL])
        bias = sb("bias", [P, NL])
        lg = sb("lg", [P, NT, NL])
        t4 = [sb(f"t4_{i}", [P, NT, G]) for i in range(3)]
        el = sb("el", [P, NT, E])
        t32 = sb("t32", [P, NT, E])
        oh = [sb(f"oh{i}", [P, NT, E]) for i in range(2)]
        both = sb("both", [P, NT, E], BF16)
        c1 = [sb(f"c1_{i}", [P, NT]) for i in range(6)]
        rank = sb("rank", [P, NT, E])
        slot = sb("slot", [P, NT, E])
        late = sb("late", [P, NT, E])
        cnt = sb("cnt", [P, E])
        t28 = sb("t28", [P, E, 8])
        ovn = sb("ovn", [P, E])
        inc = sb("inc", [P, E])
        onef = sb("onef", [P, E])
        base = sb("base", [P, 2, E])
        slotf = sb("slotf", [P, NT, 2])
        tab = sb("tab", [1, N_OVF, E])
        tabf = sb("tabf", [1, N_OVF + 1])
        tmp = sb("tmp", [P, NT])
        nrm = Norm(m, f"r{L}", 1 + 2 * L)
        s_w, s_gb = sem("weights_in"), sem("gain_in")
        s_lg, s_one, s_rank = sem("logits"), sem("onehot"), sem("ranks")
        s_ge, s_e, s_own = sem("exp_ready"), sem("exp_done"), sem("own2")
        s_slots, s_rows = sem("slots_ready"), sem("rows_out")
        block = ctx.enter_context(nc.Block())

        @block.sync
        def _(sp):
            sp.dma_start(gb[:], a["norm_ffn"][L:L + 1, :].broadcast_to([P, D])).then_inc(s_gb, 16)
            with nc.allow_non_contiguous_dma(reason="router weights are 1% of the bytes"):
                sp.dma_start(wr[:, :, 0:G], a["router_group_w"][L].rearrange("(p k) g -> p k g", k=NK)).then_inc(s_w, 16)
                sp.dma_start(wr[:, :, G:], a["router_expert_w"][L].rearrange("(p k) g -> p k g", k=NK)).then_inc(s_w, 16)
                sp.dma_start(bias[:, 0:G], a["router_group_b"][L:L + 1, :].broadcast_to([P, G])).then_inc(s_w, 16)
                sp.dma_start(bias[:, G:], a["router_expert_b"][L:L + 1, :].broadcast_to([P, E])).then_inc(s_w, 16)

            w.load_second(sp)

        @block.scalar
        def _(act):
            nrm.scalar_root(act)
            nrm.evacuate(act, 0, [(hT, None)])
            w.split_first(act, "act")
            act.wait_ge(s_ge, 1)
            act.activation(t4[1][:], t4[0][:], ACT.Exp).then_inc(s_e, 1)
            act.wait_ge(s_ge, 2)
            act.activation(c1[3][:], c1[2][:], ACT.Exp).then_inc(s_e, 1)

        @block.tensor
        def _(pe):
            nrm.tensor(pe, xn)
            nrm.wait_hT(pe)
            pe.wait_ge(s_w, 64)
            for t in range(NT):
                for k in range(NK):
                    mm = pe.matmul(m.ps[0][:, t * NL:(t + 1) * NL], hT[:, k, t * P:(t + 1) * P], wr[:, k, :],
                                   start=(k == 0), stop=(k == NK - 1))
            mm.then_inc(s_lg, 1)
            pe.wait_ge(s_one, 1)
            for t in range(NT):
                for t2 in range(t + 1):
                    mm = pe.matmul(m.ps[1][:, t * E:(t + 1) * E], (m.before if t2 == t else m.ones)[:],
                                   both[:, t2, :], start=(t2 == 0), stop=(t2 == t))
            for t in range(NT):
                mm = pe.matmul(m.ps[1][:, NT * E:(NT + 1) * E], m.ones[:], both[:, t, :],
                               start=(t == 0), stop=(t == NT - 1))
            mm.then_inc(s_rank, 1)

        @block.vector
        def _(dve):
            own = Chain(dve, s_own)
            nrm.vector_stats(dve, tmp[:])
            dve.wait_ge(s_gb, 16)
            for t in range(NT):
                dve.scalar_tensor_tensor(out=xn[:, t, :], in0=m.x[:, t, :], scalar=m.rstd[:, nrm.n, t:t + 1],
                                         in1=gb[:], op0=ALU.mult, op1=ALU.mult).then_inc(nrm.xn, 1)
            nrm.evacuate(dve, 1, [(hT, None)])
            w.split_first(dve, "dve")
            dve.wait_ge(s_w, 64)
            dve.wait_ge(s_lg, 1)

            def bc(x, n):
                return x.unsqueeze(2).broadcast_to([P, NT, n])

            own.step(dve.tensor_tensor(lg[:], m.ps[0][:, 0:NT * NL].rearrange("p (t n) -> p t n", t=NT),
                                       bias[:].unsqueeze(1).broadcast_to([P, NT, NL]), ALU.add))

            def first_max(vals, n, top, onehot, scratch):
                own.step(dve.tensor_reduce(top, vals, AX.X, ALU.max))
                own.step(dve.tensor_tensor(scratch, vals, bc(top, n), ALU.is_equal))
                own.step(dve.tensor_tensor(scratch, scratch, down(n), ALU.mult))
                own.step(dve.tensor_reduce(c1[5][:], scratch, AX.X, ALU.max))
                own.step(dve.tensor_tensor(onehot, scratch, bc(c1[5][:], n), ALU.is_equal))

            own.step(dve.tensor_scalar(onef[:], m.iota[:, 0:E], -1.0, 64.0, ALU.mult, ALU.add))

            def down(n):
                return onef[:, 0:n].unsqueeze(1).broadcast_to([P, NT, n])

            gl = lg[:, :, 0:G]
            first_max(gl, G, c1[0][:], t4[2][:], t4[0][:])
            dve.tensor_tensor(t4[0][:], gl, bc(c1[0][:], G), ALU.subtract).then_inc(s_ge, 1)
            elv = el[:].rearrange("p t (g e) -> p t g e", g=G)
            gsel = t4[2][:].unsqueeze(3).broadcast_to([P, NT, G, EPG])
            own.step(dve.tensor_tensor(elv, lg[:, :, G:].rearrange("p t (g e) -> p t g e", g=G), gsel, ALU.mult))
            own.step(dve.tensor_scalar(t4[2][:], t4[2][:], -1.0, -NEG, ALU.add, ALU.mult))
            own.step(dve.tensor_tensor(elv, elv, gsel, ALU.add))
            first_max(el[:], E, c1[0][:], oh[0][:], t32[:])
            own.step(dve.scalar_tensor_tensor(out=el[:], in0=oh[0][:], scalar=NEG, in1=el[:],
                                              op0=ALU.mult, op1=ALU.add))
            first_max(el[:], E, c1[1][:], oh[1][:], t32[:])
            dve.tensor_tensor(both[:], oh[0][:], oh[1][:], ALU.add).then_inc(s_one, 1)
            dve.tensor_tensor(c1[2][:], c1[1][:], c1[0][:], ALU.subtract).then_inc(s_ge, 1)
            dve.wait_ge(s_e, 1)
            own.step(dve.tensor_reduce(c1[4][:], t4[1][:], AX.X, ALU.add))
            dve.wait_ge(s_e, 2)
            own.step(dve.tensor_scalar(c1[5][:], c1[3][:], 1.0, None, ALU.add))
            own.step(dve.tensor_tensor(c1[4][:], c1[4][:], c1[5][:], ALU.mult))
            own.step(dve.reciprocal(m.wts[:, :, 0], c1[4][:]))
            own.step(dve.tensor_tensor(m.wts[:, :, 1], m.wts[:, :, 0], c1[3][:], ALU.mult))

            dve.wait_ge(s_rank, 1)
            own.step(dve.tensor_copy(rank[:], m.ps[1][:, 0:NT * E].rearrange("p (t e) -> p t e", t=NT)))
            own.step(dve.tensor_copy(cnt[:], m.ps[1][:, NT * E:(NT + 1) * E]))
            own.step(dve.tensor_scalar(t28[:], m.iota[:, 0:8].unsqueeze(1).broadcast_to([P, E, 8]),
                                       1.0, float(C), ALU.add, ALU.mult))
            own.step(dve.tensor_tensor(t28[:], cnt[:].unsqueeze(2).broadcast_to([P, E, 8]), t28[:], ALU.is_gt))
            own.step(dve.tensor_reduce(ovn[:], t28[:], AX.X, ALU.add))
            own.step(dve.memset(onef[:], 1.0))
            own.step(dve.tensor_tensor_scan(inc[:], onef[:], ovn[:], 0.0, ALU.mult, ALU.add))
            own.step(dve.tensor_scalar(base[:, 0, :], m.iota[:, 0:E], float(C), None, ALU.mult))
            own.step(dve.tensor_tensor(base[:, 1, :], inc[:], ovn[:], ALU.subtract))
            own.step(dve.tensor_scalar(base[:, 1, :], base[:, 1, :], float(C), float(C * E - C), ALU.mult, ALU.add))
            own.step(dve.tensor_tensor(base[:, 1, :], base[:, 1, :], base[:, 0, :], ALU.subtract))
            own.step(dve.tensor_scalar(late[:], rank[:], float(C) - 0.5, None, ALU.is_gt))
            own.step(dve.tensor_tensor(late[:], late[:], base[:, 1, :].unsqueeze(1).broadcast_to([P, NT, E]), ALU.mult))
            own.step(dve.tensor_tensor(slot[:], rank[:], base[:, 0, :].unsqueeze(1).broadcast_to([P, NT, E]), ALU.add))
            own.step(dve.tensor_tensor(slot[:], slot[:], late[:], ALU.add))
            for k in range(2):
                own.step(dve.tensor_tensor(t32[:], slot[:], oh[k][:], ALU.mult))
                own.step(dve.tensor_reduce(slotf[:, :, k], t32[:], AX.X, ALU.add))
            dve.tensor_copy(m.idx[:], slotf[:]).then_inc(s_slots, 1)
            own.step(dve.tensor_tensor(tab[:], inc[0:1, :].unsqueeze(1).broadcast_to([1, N_OVF, E]),
                                       m.iota[0:1, 0:N_OVF].unsqueeze(2).broadcast_to([1, N_OVF, E]), ALU.is_le))
            own.step(dve.memset(tabf[:, 0:1], float(E - 1)))
            own.step(dve.tensor_reduce(tabf[:, 1:], tab[:], AX.X, ALU.add))
            own.step(dve.tensor_scalar(tabf[:], tabf[:], float(E - 1), None, ALU.min))
            own.step(dve.tensor_copy(m.ovf_e[:], tabf[:]))
            own.step(dve.tensor_copy(m.novf[:], inc[0:1, E - 1:E]))

        @block.gpsimd
        def _(pool):
            w.split_first(pool, "pool")
            pool.wait_ge(s_slots, 1)
            pool.wait_ge(nrm.xn, NT)
            for t in range(NT):
                for k in range(2):
                    pool.indirect_dma_start(out=m.slots_x[:, :],
                                            out_offset=bass.IndirectOffsetOnAxis(ap=m.idx[:, t, k:k + 1], axis=0),
                                            in_=xn[:, t, :], in_offset=None).then_inc(s_rows, 16)
            pool.wait_ge(s_rows, 16 * 2 * NT)


def may_wait(eng, s, v):
    if not isinstance(v, int) or v > 0:
        eng.wait_ge(s, v)


GATE, DOWN, UP = (0, 1), (2, 3), (4, 5)
HI = ("act", "act", "dve", "act", "dve", "act")
LO = ("dve", "dve", "dve", "pool", "dve", "dve")


class Weights:

    def __init__(self, nc, m, L, ctx):
        self.m, self.L, self.parts = m, L, {}
        self.s_hi = {"act": m.sem(f"w{L}_hi_act"), "dve": m.sem(f"w{L}_hi_dve")}
        self.s_lo = {"dve": m.sem(f"w{L}_lo_dve"), "pool": m.sem(f"w{L}_lo_pool")}
        self.s_used = m.sem(f"w{L}_used")
        self.make_room(nc, ctx, "gate_up", GATE + UP)

    def make_room(self, nc, ctx, name, pieces):
        hi, lo = (ctx.enter_context(nc.sbuf_tensor(f"w{self.L}_{name}_{part}", [P, len(pieces), PIECE], F32R))
                  for part in ("hi", "lo"))
        for n, k in enumerate(pieces):
            self.parts[k] = (hi[:, n, :], lo[:, n, :])

    def made(self, eng, table, c, k, last=False):
        who, first_step = table[k], isinstance(c, int) and c == 0
        down = sum(table[q] == who for q in DOWN)
        before = [q for q in range(k) if not (last and q in GATE) and not (first_step and q in DOWN)]
        first = 0 if first_step else c * table.count(who) - down
        may_wait(eng, (self.s_hi if table is HI else self.s_lo)[who],
                 first + sum(table[q] == who for q in before) + 1)

    def used(self, eng, c, k, last=False):
        if isinstance(c, int) and c < 0 or isinstance(c, int) and c == 0 and k in DOWN:
            return
        if isinstance(c, int) and c == 0:
            eng.wait_ge(self.s_used, {0: 1, 1: 2, 4: 3, 5: 4}[k])
        else:
            eng.wait_ge(self.s_used, c * NPIECE - 2 + k + 1 - (2 if last else 0))

    def split(self, eng, who, c, k, last=False):
        raw, (hi, lo) = self.m.raw[:, k, :], self.parts[k]
        if HI[k] == who:
            may_wait(eng, self.m.load[self.L][k], (c if k in DOWN else c + 1) * 16)
            self.used(eng, c - 1, k)
            h = eng.activation(hi, raw, ACT.Copy) if who == "act" else eng.tensor_copy(hi, raw)
            h.then_inc(self.s_hi[who], 1)
        if LO[k] == who:
            self.made(eng, HI, c, k, last)
            self.used(eng, c - 1, k)
            eng.tensor_tensor(lo, raw, hi.bitcast(F32), ALU.subtract).then_inc(self.s_lo[who], 1)

    def load(self, sp, c, k, q, e):
        self.made(sp, LO, c - 1, k)
        sp.dma_start(self.m.raw[:, k, :], piece_src(self.m, self.L, q, e)).then_inc(self.m.load[self.L][k], 16)

    def split_first(self, eng, who):
        for k in GATE + UP:
            self.split(eng, who, 0, k)

    def load_second(self, sp):
        for k, q in zip(GATE + UP, range(4)):
            self.load(sp, 1, k, q, 1)


def experts(nc, m, L, w):
    with ExitStack() as ctx:
        def sb(name, shape, dt=F32):
            return ctx.enter_context(nc.sbuf_tensor(f"e{L}_{name}", shape, dt))

        def sem(name):
            return m.sem(f"e{L}_{name}")

        H = 2 * C
        FH = F // 2
        xrow = sb("xrow", [P, D])
        xst = sb("xst", [P, 2, NK, H], F32R)
        w.make_room(nc, ctx, "down", DOWN)
        part = sb("part", [P, 2, FH])
        gate = sb("gate", [P, FH])
        up = sb("up", [P, FH])
        act_g = sb("act_g", [P, FH])
        hid = sb("hid", [P, FH])
        hst = sb("hst", [P, 2, 2, H], F32R)
        ypart = sb("ypart", [C, D])
        yrow = sb("yrow", [C, D])
        s_xl, s_st = sem("x_in"), sem("y_out")
        s_xt, s_xhi, s_xlo = sem("x_transposed"), sem("x_hi"), sem("x_lo")
        s_used = w.s_used
        s_part = [sem("gate_part"), sem("up_part")]
        s_sum = [sem("gate_sum"), sem("up_sum")]
        s_sg, s_h = sem("silu"), sem("hidden")
        s_ht, s_hhi, s_hlo = sem("h_transposed"), sem("h_hi"), sem("h_lo")
        s_yp, s_y = sem("y_part"), sem("y_sum")
        ps_x, ps_gu, ps_h, ps_y = m.ps[0:2], m.ps[2:4], m.ps[4], m.ps[5:7]
        wait, made, used = may_wait, w.made, w.used

        def pe_rows(pe, i):
            wait(pe, s_xl, i * 16 + 16)
            wait(pe, s_xlo, i * 2)
            for k in range(NK):
                mm = pe.transpose(ps_x[k // 4][:, (k % 4) * P:(k % 4 + 1) * P], xrow[:, k::NK], m.ident[:])
            mm.then_inc(s_xt, 1)

        def pe_gate_up(pe, c, u, i, pieces):
            wait(pe, s_xlo, c + 1)
            for b, k in enumerate(pieces):
                made(pe, LO, c, k)
                if b == 0:
                    wait(pe, s_sum[i], c)
                for kk in range(4):
                    for part in range(2):
                        mm = pe.matmul(ps_gu[i][:], xst[:, u, 4 * b + kk, :], w.parts[k][part][:, kk * F:(kk + 1) * F],
                                       start=(b == 0 and kk == 0 and part == 0),
                                       stop=(b == 1 and kk == 3 and part == 1))
                mm.then_inc(s_used, 1)

        def pe_down(pe, c, last=False):
            wait(pe, s_h, c)
            wait(pe, s_hlo, c - 1)
            for k in range(2):
                mm = pe.transpose(ps_h[:, k * P:(k + 1) * P], hid[:, k::2], m.ident[:])
            mm.then_inc(s_ht, 1)
            wait(pe, s_hlo, c)
            wait(pe, s_y, c - 1)
            for h, k in enumerate(DOWN):
                made(pe, LO, c, k, last)
                for kk in range(2):
                    for part in range(2):
                        for n in range(2):
                            mm = pe.matmul(ps_y[n][:], hst[:, kk, h, :],
                                           w.parts[k][part][:, kk * D + n * 512:kk * D + (n + 1) * 512],
                                           start=(h == 0 and kk == 0 and part == 0),
                                           stop=(h == 1 and kk == 1 and part == 1))
                mm.then_inc(s_used, 1)

        def pe_step(pe, c, u):
            if isinstance(c, int) and c == 0:
                pe_rows(pe, 0)
            pe_gate_up(pe, c, u, 0, GATE)
            if u == 1:
                pe_rows(pe, (c + 1) // 2 if isinstance(c, int) else (c + 1) >> 1)
            if not (isinstance(c, int) and c == 0):
                pe_down(pe, c)
            pe_gate_up(pe, c, u, 1, UP)

        def act_rows_in(act, i):
            wait(act, s_xt, i)
            act.dma_start(xrow[:], m.slots_x[bass.ds(i * H, H), :]).then_inc(s_xl, 16)

        def act_hi(act, c, k, last=False):
            if HI[k] == "act":
                w.split(act, "act", c, k, last)

        def act_part(act, c, i, at, k, last=False):
            used(act, at, k)
            wait(act, s_sum[i], c)
            act.activation(part[0:C, i, :], ps_gu[i][C:H, 0:FH], ACT.Copy)
            act.activation(part[C:H, i, :], ps_gu[i][0:C, FH:F], ACT.Copy).then_inc(s_part[i], 1)

        def act_h_hi(act, c):
            wait(act, s_ht, c)
            used(act, c - 1, DOWN[1])
            act.activation(hst[:, :, :, 0:C], ps_h[:, 0:2 * P].rearrange("p (k h c) -> p k h c", k=2, h=2),
                           ACT.Copy).then_inc(s_hhi, 1)

        def act_y(act, c, last=False):
            used(act, c, DOWN[1], last)
            wait(act, s_y, c - 1)
            for n in range(2):
                act.activation(ypart[:, n * 512:(n + 1) * 512], ps_y[n][C:H, :], ACT.Copy).then_inc(s_yp, 1)
            wait(act, s_y, c)
            act.dma_start(m.slots_y[bass.ds(c * C - C, C), :], yrow[:]).then_inc(s_st, 16)

        def rows_view(c, u):
            return [(b, ps_x[b][:].rearrange("p (k u c) -> p k u c", k=4, u=2)[:, :, u, :],
                     xst[:, u, 4 * b:4 * b + 4, :]) for b in range(2)]

        def act_x_hi(act, c, u):
            wait(act, s_xt, (c // 2 if isinstance(c, int) else c >> 1) + 1)
            used(act, c - 2, UP[1])
            for b, src, dst in rows_view(c, u):
                act.activation(dst[:, :, 0:C], src, ACT.Copy).then_inc(s_xhi, 1)

        def act_step(act, c, u):
            start = isinstance(c, int) and c == 0
            if start:
                act_rows_in(act, 0)
            elif u == 0:
                act_rows_in(act, (c >> 1) + 1)
            if start:
                act_x_hi(act, 0, 0)
                act_rows_in(act, 1)
            else:
                for k in GATE:
                    act_hi(act, c, k)
            if not start:
                act_part(act, c - 1, 1, c - 1, UP[1])
                act_hi(act, c, DOWN[0])
                if not (isinstance(c, int) and c == 1):
                    act_y(act, c - 1)
                act_hi(act, c, DOWN[1])
                act_hi(act, c, UP[0])
            act_part(act, c, 0, c, GATE[1])
            if not start:
                act_h_hi(act, c)
            wait(act, s_sum[0], c + 1)
            wait(act, s_h, c)
            act.activation(act_g[:], gate[:], ACT.Silu).then_inc(s_sg, 1)
            if not start:
                act_hi(act, c, UP[1])
            act_x_hi(act, c + 1, 1 - u)

        def act_tail(act, c):
            act_y(act, c - 1)
            act_part(act, c - 1, 1, c - 1, UP[1])
            for k in DOWN:
                act_hi(act, c, k, True)
            act_h_hi(act, c)
            act_y(act, c, True)

        split = w.split

        def dve_sum(dve, c, i, dst):
            wait(dve, s_part[i], c + 1)
            wait(dve, (s_sg, s_h)[i], c)
            dve.tensor_tensor(dst[0:C, :], ps_gu[i][0:C, 0:FH], part[0:C, i, :], ALU.add)
            dve.tensor_tensor(dst[C:H, :], ps_gu[i][C:H, FH:F], part[C:H, i, :], ALU.add).then_inc(s_sum[i], 1)

        def dve_hidden(dve, c):
            dve_sum(dve, c - 1, 1, up)
            wait(dve, s_sum[1], c)
            wait(dve, s_sg, c)
            wait(dve, s_ht, c - 1)
            dve.tensor_tensor(hid[:], act_g[:], up[:], ALU.mult).then_inc(s_h, 1)

        def dve_h_lo(dve, c):
            wait(dve, s_hhi, c)
            dve.tensor_tensor(hst[:, :, :, C:H], ps_h[:, 0:2 * P].rearrange("p (k h c) -> p k h c", k=2, h=2),
                              hst[:, :, :, 0:C].bitcast(F32), ALU.subtract).then_inc(s_hlo, 1)

        def dve_y(dve, c):
            wait(dve, s_yp, 2 * c)
            wait(dve, s_st, 16 * c - 16)
            for n in range(2):
                o = dve.tensor_tensor(yrow[:, n * 512:(n + 1) * 512], ps_y[n][0:C, :],
                                      ypart[:, n * 512:(n + 1) * 512], ALU.add)
            o.then_inc(s_y, 1)

        def dve_x_lo(dve, c, u):
            wait(dve, s_xhi, c * 2 + 2)
            for b, src, dst in rows_view(c, u):
                o = dve.tensor_tensor(dst[:, :, C:H], src, dst[:, :, 0:C].bitcast(F32), ALU.subtract)
            o.then_inc(s_xlo, 1)

        def dve_step(dve, c, u):
            start = isinstance(c, int) and c == 0
            if start:
                dve_x_lo(dve, 0, 0)
            else:
                for k in GATE:
                    split(dve, "dve", c, k)
                if not (isinstance(c, int) and c == 1):
                    dve_y(dve, c - 1)
                dve_hidden(dve, c)
                split(dve, "dve", c, DOWN[0])
            dve_sum(dve, c, 0, gate)
            if not start:
                split(dve, "dve", c, DOWN[1])
                dve_h_lo(dve, c)
                for k in UP:
                    split(dve, "dve", c, k)
            dve_x_lo(dve, c + 1, 1 - u)

        def dve_tail(dve, c):
            dve_y(dve, c - 1)
            for k in DOWN:
                split(dve, "dve", c, k, True)
            dve_hidden(dve, c)
            dve_h_lo(dve, c)
            dve_y(dve, c)

        def pool_step(pool, c, u):
            if not (isinstance(c, int) and c == 0):
                for k in range(NPIECE):
                    split(pool, "pool", c, k)

        def pool_tail(pool, c):
            for k in DOWN:
                split(pool, "pool", c, k, True)
            pool.wait_ge(s_st, c * 16)

        sp_load = w.load

        def sp_step(sp, c, e, before):
            for k, q in ((0, 0), (1, 1)):
                sp_load(sp, c, k, q, e)
            for k, q in ((2, 4), (3, 5)):
                sp_load(sp, c, k, q, before)
            for k, q in ((4, 2), (5, 3)):
                sp_load(sp, c, k, q, e)

        def pipeline(eng, step, tail):
            step(eng, 0, 0)
            step(eng, 1, 1)
            with eng.Fori(1, E // 2) as i:
                step(eng, i * 2, 0)
                step(eng, i * 2 + 1, 1)
            n = eng.value_load(m.novf[0:1, 0:1], min_val=0, max_val=N_OVF)
            with eng.Fori(0, N_OVF // 2) as j:
                with eng.If(j * 2 < n):
                    step(eng, j * 2 + E, 0)
                with eng.If(j * 2 + 1 < n):
                    step(eng, j * 2 + (E + 1), 1)
            tail(eng, n + E)

        block = ctx.enter_context(nc.Block())

        @block.sync
        def _(sp):
            def expert(i):
                return sp.value_load(m.ovf_e[0:1, bass.ds(i, 1)], min_val=0, max_val=E - 1)

            sp_step(sp, 2, 2, 1)
            with sp.Fori(3, E) as c:
                sp_step(sp, c, c, c - 1)
            n = sp.value_load(m.novf[0:1, 0:1], min_val=0, max_val=N_OVF)
            with sp.Fori(0, N_OVF) as j:
                with sp.If(j < n):
                    sp_step(sp, j + E, expert(j + 1), expert(j))
            e = expert(n)
            for k, q in ((2, 4), (3, 5)):
                sp_load(sp, n + E, k, q, e)

        @block.scalar
        def _(act):
            pipeline(act, act_step, act_tail)

        @block.vector
        def _(dve):
            pipeline(dve, dve_step, dve_tail)

        @block.gpsimd
        def _(pool):
            pipeline(pool, pool_step, pool_tail)

        @block.tensor
        def _(pe):
            pipeline(pe, pe_step, lambda eng, c: pe_down(eng, c, True))


def combine(nc, m, L):
    with ExitStack() as ctx:
        rows = ctx.enter_context(nc.sbuf_tensor(f"k{L}_rows", [P, NT, 2, D], F32))
        junk = ctx.enter_context(nc.sbuf_tensor(f"k{L}_junk", [P, D], F32))
        s_in = [m.sem(f"k{L}_in{t}") for t in range(NT)]
        s_add, s_sq = m.sem(f"k{L}_added"), m.sem(f"k{L}_squares")
        block = ctx.enter_context(nc.Block())

        @block.scalar
        def _(act):
            sum_squares(act, m, s_sq, junk[:], lambda t: act.wait_ge(s_add, 2 * t + 2))

        @block.gpsimd
        def _(pool):
            for t in range(NT):
                for k in range(2):
                    pool.indirect_dma_start(out=rows[:, t, k, :], out_offset=None, in_=m.slots_y[:, :],
                                            in_offset=bass.IndirectOffsetOnAxis(ap=m.idx[:, t, k:k + 1], axis=0)
                                            ).then_inc(s_in[t], 16)

        @block.vector
        def _(dve):
            for t in range(NT):
                dve.wait_ge(s_in[t], 32)
                for k in range(2):
                    dve.scalar_tensor_tensor(out=m.x[:, t, :], in0=rows[:, t, k, :], scalar=m.wts[:, t, k:k + 1],
                                             in1=m.x[:, t, :], op0=ALU.mult, op1=ALU.add).then_inc(s_add, 1)
                    dve.wait_ge(s_add, 2 * t + k + 1)


def final_norm(nc, m):
    with ExitStack() as ctx:
        gb = ctx.enter_context(nc.sbuf_tensor("f_gb", [P, D], F32))
        y = ctx.enter_context(nc.sbuf_tensor("f_y", [P, NT, D], F32))
        tmp = ctx.enter_context(nc.sbuf_tensor("f_tmp", [P, NT], F32))
        nrm = Norm(m, "f", 4)
        s_gb, s_out = m.sem("f_gain_in"), m.sem("f_out")
        block = ctx.enter_context(nc.Block())
        out = m.out.rearrange("b (t p) d -> t p (b d)", p=P)

        @block.sync
        def _(sp):
            sp.dma_start(gb[:], m.a["norm_final"].rearrange("(a d) -> a d", a=1).broadcast_to([P, D])).then_inc(s_gb, 16)
            for t in range(NT):
                sp.wait_ge(nrm.xn, t + 1)
                sp.dma_start(out[t], y[:, t, :]).then_inc(s_out, 16)
            sp.wait_ge(s_out, 16 * NT)

        @block.scalar
        def _(act):
            nrm.scalar_root(act)

        @block.vector
        def _(dve):
            nrm.vector_stats(dve, tmp[:])
            dve.wait_ge(s_gb, 16)
            for t in range(NT):
                dve.scalar_tensor_tensor(out=y[:, t, :], in0=m.x[:, t, :], scalar=m.rstd[:, 4, t:t + 1], in1=gb[:],
                                         op0=ALU.mult, op1=ALU.mult).then_inc(nrm.xn, 1)


N_SHARED = 2


def shared_kv(nc, m, ctx):
    a = m.a

    def keep(name, shape, dt=F32):
        return ctx.enter_context(nc.sbuf_tensor("a_" + name, shape, dt))

    m.kT = keep("kT", [P, 2, NG, S])
    m.v = keep("v", [P, NT, 2, NG, 2, HD], F32R)
    m.q = keep("q", [P, NK, S])
    m.qr = keep("qr", [P, NK, S])
    m.gates = keep("gates", [P, NT, NH, NBR])
    m.kc = keep("kc", [P, NG, NBLK])
    m.w1_in = m.sem("a_w1_in")
    m.vc = keep("vc", [P, NG, 2, 2 * HD])
    with ExitStack() as between:
        cvT = between.enter_context(nc.sbuf_tensor("b_cvT", [P, 2, 2, S], F32))
        for stage, letter in ((norm_and_project, "b_"), (compress, "z_")):
            with ExitStack() as tmp:
                def sb(name, shape, dt=F32):
                    return tmp.enter_context(nc.sbuf_tensor(letter + name, shape, dt))

                stage(nc, m, sb, cvT)


def norm_and_project(nc, m, sb, cvT):
    a = m.a
    NF = 4 + 4 + 8
    hkv = sb("hkv", [P, NK, S])
    hq = sb("hq", [P, NK, S])
    gain = sb("gain", [P, 2, NK])
    wk = m.raw[:, 0:2, :].rearrange("p b (k n) -> p b k n", k=NK)
    wv = m.raw[:, 2:4, :].rearrange("p b (k n) -> p b k n", k=NK)
    wg = sb("wg", [P, NK, NH * NBR])
    rope = sb("rope", [P, 2, S])
    perm = sb("perm", [P, P])
    raw = sb("rawk", [P, 2, S])
    prod = sb("prod", [P, 2, S])
    xn = m.qr[:].rearrange("p k s -> p (k s)").rearrange("p (t d) -> p t d", t=NT)
    small = sb("tmp", [P, NT])
    posi = sb("posi", [P, S], I32)
    freq = sb("freq", [P, 1])
    ang = m.qr[:, 0:3, :]
    gtmp = sb("gtmp", [P, NT, NH * NBR])
    nrm = Norm(m, "b", 2)
    s_gain, s_wg, s_pos = m.sem("b_gain_in"), m.sem("b_gate_w_in"), m.sem("b_pos_in")
    s_wk = [m.sem(f"b_wk{i}") for i in range(2)]
    s_wv = m.sem("b_wv_in")
    s_feat, s_tok = m.sem("b_features"), m.sem("b_tokens")
    s_raw, s_swap, s_rot = m.sem("b_raw"), m.sem("b_swapped"), m.sem("b_rotated")
    s_own, s_sin, s_ang, s_perm = m.sem("b_own2"), m.sem("b_sin"), m.sem("b_angles"), m.sem("b_perm")
    s_cv, s_v, s_g, s_ge = m.sem("b_cv"), m.sem("b_v"), m.sem("b_gate"), m.sem("b_gate_exp")
    block_of = nc.Block()
    cols = [("w_kv", 0), ("w_kv", 256), ("w_kv", 512), ("w_kv", 1024)] + [("attn_w_in", 256 * i) for i in range(4)]

    def weight(name, c, n):
        w = a[name] if name == "w_kv" else a[name][0]
        return w.rearrange("(p k) c -> p k c", k=NK)[:, :, c:c + n]

    rotated = list(range(4, NF))
    with block_of as block:

        @block.sync
        def _(sp):
            with nc.allow_non_contiguous_dma(reason="small vectors"):
                sp.dma_start(gain[:, 0, :], a["norm_kv"].rearrange("(p k) -> p k", k=NK)).then_inc(s_gain, 16)
                sp.dma_start(gain[:, 1, :], a["norm_mix"][1].rearrange("(p k) -> p k", k=NK)).then_inc(s_gain, 16)
                for i in range(4):
                    sp.dma_start(freq[32 * i:32 * i + 32, :], a["inv_freq"].rearrange("(p a) -> p a", a=1)
                                 ).then_inc(s_pos, 16)
            sp.dma_start(posi[:], a["positions"].broadcast_to([P, S])).then_inc(s_pos, 16)
            for n, (name, c) in enumerate(cols):
                if n >= 2:
                    sp.wait_ge(s_feat, 2 * (n - 1))
                sp.dma_start(wk[:, n % 2, :, :], weight(name, c, 256)).then_inc(s_wk[n % 2], 16)
                if n == 3:
                    sp.dma_start(m.raw[:, 4:6, :].rearrange("p h (j n) -> p (h j) n", n=HID),
                                 a["cmp_w1_k"].rearrange("(j p) n -> p j n", p=P)).then_inc(m.w1_in, 16)
                if n == len(cols) - 1:
                    sp.wait_ge(s_tok, NT)
                    sp.dma_start(m.raw[:, 2:4, :].rearrange("p h (j n) -> p (h j) n", n=HID),
                                 a["cmp_w1_v"].rearrange("(j p) n -> p j n", p=P)).then_inc(m.w1_in, 16)
                if n == 1:
                    sp.dma_start(wv[:, 0, :, :], weight("w_kv", 768, 256)).then_inc(s_wv, 16)
                    sp.dma_start(wv[:, 1, :, :], weight("w_kv", 1280, 256)).then_inc(s_wv, 16)
                    sp.dma_start(wg[:], weight("attn_w_in", NH * HD, NH * NBR)).then_inc(s_wg, 16)

        @block.gpsimd
        def _(pool):
            for i in range(4):
                o = 32 * (i ^ 1)
                p = pool.tensor_copy(perm[:, 32 * i:32 * i + 32], m.ident[:, o:o + 32])
            p.then_inc(s_perm, 1)

        @block.scalar
        def _(act):
            nrm.scalar_root(act)
            act.wait_ge(s_gain, 32)
            nrm.evacuate(act, 0, [(hkv, gain[:, 0, :]), (hq, gain[:, 1, :])])
            act.wait_ge(s_ang, 1)
            act.activation(rope[:, 0, :], ang[:, 1, :], ACT.Sin).then_inc(s_sin, 1)
            act.activation(rope[:, 1, :], ang[:, 0, :], ACT.Sin).then_inc(s_sin, 1)
            for i in range(NF):
                act.wait_ge(s_feat, i + 1)
                if i < 4:
                    act.activation(cvT[:, i // 2, i % 2, :], m.ps[i % 4][:], ACT.Copy).then_inc(s_raw, 1)
                else:
                    if i >= 6 and i < 8:
                        act.wait_ge(s_rot, i - 5)
                    dst = raw[:, i % 2, :] if i < 8 else m.q[:, i - 8, :]
                    act.activation(dst, m.ps[i % 4][:], ACT.Copy).then_inc(s_raw, 1)
            for t in range(NT):
                act.wait_ge(s_g, t + 1)
            act.activation(gtmp[:], gtmp[:], ACT.Exp, scale=-1.0).then_inc(s_ge, 1)

        @block.vector
        def _(dve):
            own = Chain(dve, s_own)
            nrm.vector_stats(dve, small[:])
            nrm.vector_normed(dve, xn)
            dve.wait_ge(s_gain, 32)
            nrm.evacuate(dve, 1, [(hkv, gain[:, 0, :]), (hq, gain[:, 1, :])])
            dve.wait_ge(s_pos, 16 * 5)
            a0, a1, a2 = (ang[:, i, :] for i in range(3))
            own.step(dve.tensor_copy(a1, posi[:]))
            own.step(dve.tensor_scalar(a0, a1, freq[:, 0:1], None, ALU.mult))
            own.step(dve.tensor_scalar(a1, a0, 1.0 / (2 * PI), MAGIC, ALU.mult, ALU.add))
            own.step(dve.tensor_scalar(a1, a1, MAGIC, None, ALU.subtract))
            own.step(dve.scalar_tensor_tensor(out=a0, in0=a1, scalar=-TWO_PI[0], in1=a0, op0=ALU.mult, op1=ALU.add))
            own.step(dve.scalar_tensor_tensor(out=a0, in0=a1, scalar=-TWO_PI[1], in1=a0, op0=ALU.mult, op1=ALU.add))
            own.step(dve.scalar_tensor_tensor(out=a0, in0=a1, scalar=-TWO_PI[2], in1=a0, op0=ALU.mult, op1=ALU.add))
            own.step(dve.tensor_scalar(a0, a0, PI32, -PI32, ALU.min, ALU.max))
            own.step(dve.tensor_scalar(a2, a0, -1.0, None, ALU.mult))
            own.step(dve.tensor_tensor(a2, a2, a0, ALU.max))
            dve.tensor_scalar(a1, a2, -1.0, PI / 2, ALU.mult, ALU.add).then_inc(s_ang, 1)
            dve.wait_ge(s_sin, 2)
            for i in (0, 2):
                own.step(dve.tensor_scalar(rope[32 * i:32 * i + 32, 1, :], rope[32 * i:32 * i + 32, 1, :], -1.0, None,
                                           ALU.mult))
            for j, i in enumerate(rotated):
                src = raw[:, i % 2, :] if i < 8 else m.q[:, i - 8, :]
                dve.wait_ge(s_raw, i + 1)
                dve.tensor_tensor(prod[:, 0, :], src, rope[:, 0, :], ALU.mult).then_inc(s_v, 1)
                dve.wait_ge(s_swap, j + 1)
                own.step(dve.tensor_tensor(prod[:, 1, :], m.ps[4 + j % 2][:], rope[:, 1, :], ALU.mult))
                dve.wait_ge(s_v, j + 1)
                if i < 8:
                    br, g0 = (i - 4) // 2, 2 * (i % 2)
                    for g in range(2):
                        rows = slice(64 * g, 64 * g + 64)
                        for to in range(2):
                            r = dve.tensor_tensor(m.kT[64 * to:64 * to + 64, br, g0 + g, :], prod[rows, 0, :],
                                                  prod[rows, 1, :], ALU.add)
                else:
                    r = dve.tensor_tensor(m.qr[:, i - 8, :], prod[:, 0, :], prod[:, 1, :], ALU.add)
                r.then_inc(s_rot, 1)
                dve.wait_ge(s_rot, j + 1)
                if i == 6:
                    for t in range(NT):
                        dve.wait_ge(s_tok, t + 1)
                        v_hi, v_lo = m.v[:, t, :, :, 0, :], m.v[:, t, :, :, 1, :]
                        src = m.ps[6][:].rearrange("p (b g d) -> p b g d", b=2, g=NG)
                        dve.tensor_copy(v_hi, src).then_inc(s_cv, 1)
                        dve.wait_ge(s_cv, t + 1)
                        dve.tensor_tensor(v_lo, src, v_hi.bitcast(F32), ALU.subtract)
                        dve.tensor_copy(gtmp[:, t, :], m.ps[7][:, 0:NH * NBR]).then_inc(s_g, 1)
            dve.wait_ge(s_ge, 1)
            own.step(dve.tensor_scalar(gtmp[:], gtmp[:], 1.0, None, ALU.add))
            own.step(dve.reciprocal(m.gates[:].rearrange("p t h b -> p t (h b)"), gtmp[:]))

        @block.tensor
        def _(pe):
            nrm.tensor(pe, xn)
            nrm.wait_hT(pe)

            def swap(j):
                i = rotated[j]
                src = raw[:, i % 2, :] if i < 8 else m.q[:, i - 8, :]
                pe.wait_ge(s_raw, i + 1)
                if j == 0:
                    pe.wait_ge(s_perm, 1)
                if j >= 2:
                    pe.wait_ge(s_rot, j - 1)
                pe.matmul(m.ps[4 + j % 2][:], perm[:], src, start=True, stop=True).then_inc(s_swap, 1)

            def token_major():
                pe.wait_ge(s_wv, 32)
                pe.wait_ge(s_wg, 16)
                for t in range(NT):
                    if t:
                        pe.wait_ge(s_g, t)
                    for k in range(NK):
                        pe.matmul(m.ps[6][:].rearrange("p (b c) -> p b c", b=2), hkv[:, k, t * P:(t + 1) * P], wv[:, :, k, :],
                                  start=(k == 0), stop=(k == NK - 1))
                    for k in range(NK):
                        mm = pe.matmul(m.ps[7][:, 0:NH * NBR], hq[:, k, t * P:(t + 1) * P], wg[:, k, :],
                                       start=(k == 0), stop=(k == NK - 1))
                    mm.then_inc(s_tok, 1)

            for i in range(NF):
                n = i // 2
                pe.wait_ge(s_wk[n % 2], 16 * (n // 2 + 1))
                if i >= 4:
                    pe.wait_ge(s_raw, i - 3)
                h = hkv if i < 8 else hq
                for k in range(NK):
                    mm = pe.matmul(m.ps[i % 4][:], wk[:, n % 2, k, (i % 2) * P:(i % 2 + 1) * P], h[:, k, :],
                                   start=(k == 0), stop=(k == NK - 1))
                mm.then_inc(s_feat, 1)
                if i >= 5:
                    swap(i - 5)
                if i == 7:
                    token_major()
            swap(len(rotated) - 1)


def compress(nc, m, sb, cvT):
    a = m.a
    NJ = CMP // 2
    NB = NG * NCMP
    two = sb("two", [P, 2, NG, S])
    blk = sb("blk", [P, 2, NJ, NG, NCMP])
    pos = sb("pos", [P, 2, NJ])
    w1 = [m.raw[:, r:r + 2, :].rearrange("p h (j n) -> p (h j) n", n=HID) for r in (4, 2)]
    w2 = sb("w2", [P, 2, 2, HD])
    hid = sb("hid", [P, 2, HID])
    t1 = sb("t1", [P, 2, HID])
    hT = sb("hidT", [P, 2, 2, NB])
    s_in = [m.sem("z_w1_in"), m.sem("z_pos_in")]
    s_two, s_blk, s_hid, s_hs = m.sem("z_two"), m.sem("z_blocks"), m.sem("z_hidden"), m.sem("z_hid_sb")
    s_th, s_gelu, s_tr, s_hT, s_out = (m.sem(n) for n in ("z_tanh", "z_gelu", "z_tr", "z_hT", "z_out"))
    s_own, s_kc = m.sem("z_own"), m.sem("z_kc")
    with nc.Block() as block:

        @block.sync
        def _(sp):
            with nc.allow_non_contiguous_dma(reason="2,048 position embeddings"):
                for i, c in enumerate("kv"):
                    sp.dma_start(w2[:, i], a[f"cmp_w2_{c}"].rearrange("(k p) n -> p k n", p=P)).then_inc(s_in[0], 16)
                    sp.dma_start(pos[:, i], a[f"cmp_pos_{c}"].rearrange("(j two) d -> (two d) j", two=2)
                                 ).then_inc(s_in[1], 16)

        @block.vector
        def _(dve):
            own = Chain(dve, s_own)
            own.step(dve.memset(m.kc[:], 0.0))
            own.step(dve.memset(m.vc[:], 0.0))
            for i in range(2):
                for g in range(NG):
                    src = cvT[64 * (g % 2):64 * (g % 2) + 64, i, g // 2, :]
                    dve.tensor_copy(two[0:64, i, g, :], src)
                    c = dve.tensor_copy(two[64:P, i, g, 0:S - 1], src[:, 1:S])
                c.then_inc(s_two, 1)
            dve.wait_ge(s_in[1], 32)
            for i in range(2):
                dve.wait_ge(s_two, i + 1)
                for j in range(NJ):
                    src = two[:, i, :, 2 * j:2 * j + (NCMP - 1) * STRIDE + 1:STRIDE]
                    b = dve.tensor_scalar(blk[:, i, j], src, pos[:, i, j:j + 1], None, ALU.add)
                b.then_inc(s_blk, 1)
            for i in range(2):
                dve.wait_ge(s_hid, i + 1)
                h, t = hid[0:NB, i, :], t1[0:NB, i, :]
                own.step(dve.tensor_copy(h, m.ps[i][0:NB, 0:HID]))
                own.step(dve.tensor_tensor(t, h, h, ALU.mult))
                own.step(dve.tensor_scalar(t, t, 0.044715, 1.0, ALU.mult, ALU.add))
                dve.tensor_tensor(t, t, h, ALU.mult).then_inc(s_hs, 1)
            for i in range(2):
                h, t = hid[0:NB, i, :], t1[0:NB, i, :]
                dve.wait_ge(s_th, i + 1)
                own.step(dve.tensor_scalar(t, t, 1.0, 0.5, ALU.add, ALU.mult))
                dve.tensor_tensor(h, h, t, ALU.mult).then_inc(s_gelu, 1)
            for i in range(2):
                dve.wait_ge(s_tr, i + 1)
                dve.tensor_copy(hT[:, i], m.ps[2 + i][:, 0:2 * NB].rearrange("p (k n) -> p k n", k=2)).then_inc(s_hT, 1)
            dve.wait_ge(s_out, 1)
            for to in range(2):
                dve.tensor_copy(m.kc[64 * to:64 * to + 64, :, 0:NCMP],
                                m.ps[4][0:64, 0:NB].rearrange("p (g c) -> p g c", g=NG)).then_inc(s_kc, 1)
            dve.wait_ge(s_out, 2)
            for h in range(HPG):
                dve.tensor_copy(m.vc[NBLK * h:NBLK * h + NCMP, :, h // 2, (h % 2) * HD:(h % 2 + 1) * HD],
                                m.ps[5][0:NCMP, 0:NG * HD].rearrange("p (g d) -> p g d", g=NG)).then_inc(s_kc, 1)

        @block.scalar
        def _(act):
            for i in range(2):
                act.wait_ge(s_hs, i + 1)
                act.activation(t1[0:NB, i, :], t1[0:NB, i, :], ACT.Tanh, scale=(2 / PI) ** 0.5).then_inc(s_th, 1)

        @block.tensor
        def _(pe):
            pe.wait_ge(s_in[0], 32)
            pe.wait_ge(m.w1_in, 32)
            for i in range(2):
                pe.wait_ge(s_blk, i + 1)
                for j in range(NJ):
                    mm = pe.matmul(m.ps[i][0:NB, 0:HID], blk[:, i, j].rearrange("p g c -> p (g c)"), w1[i][:, j, :],
                                   start=(j == 0), stop=(j == NJ - 1))
                mm.then_inc(s_hid, 1)
            for i in range(2):
                pe.wait_ge(s_gelu, i + 1)
                for k in range(2):
                    tr = pe.transpose(m.ps[2 + i][:, k * NB:(k + 1) * NB], hid[0:NB, i, k * P:(k + 1) * P],
                                      m.ident[0:NB, 0:NB])
                tr.then_inc(s_tr, 1)
            pe.wait_ge(s_hT, 2)
            for k in range(2):
                mm = pe.matmul(m.ps[4][0:64, 0:NB], w2[:, 0, k, :], hT[:, 0, k, :], start=(k == 0), stop=(k == 1))
            mm.then_inc(s_out, 1)
            for g in range(NG):
                for k in range(2):
                    mm = pe.matmul(m.ps[5][0:NCMP, g * HD:(g + 1) * HD], hT[:, 1, k, g * NCMP:(g + 1) * NCMP],
                                   w2[:, 1, k, :], start=(k == 0), stop=(k == 1))
            mm.then_inc(s_out, 1)


def attention(nc, m):
    a = m.a
    with ExitStack() as ctx:
        def sb(name, shape, dt=F32):
            return ctx.enter_context(nc.sbuf_tensor("t_" + name, shape, dt))

        causal = sb("causal", [P, P], BF16)
        cmask = sb("cmask", [P, NT, NBLK])
        zero = sb("zero", [P, P])
        oT = m.q
        wout = m.raw[:, 0:4, :].rearrange("p q (j n) -> p (q j) n", n=D)
        pr = sb("pr", [P, 3, HPG, S])
        prT_hi = sb("prT_hi", [P, 2, NT, HPG * P], F32R)
        prT_lo = sb("prT_lo", [P, 2, NT, HPG * P], F32R)
        pc = sb("pc", [P, 2, NH, NBLK])
        pcT = sb("pcT", [P, 2, NG, P])
        cmx = sb("cmx", [P, 2, NH])
        csm = sb("csm", [P, 2, NH])
        mx = sb("mx", [P, 2, HPG])
        sm = sb("sm", [P, 3, HPG])
        s_wo, s_mask, s_z = m.sem("t_wout_in"), m.sem("t_masks"), m.sem("t_zero")
        s_csc, s_cmx, s_cex, s_cpn = (m.sem("t_cmp_" + n) for n in ("scores", "shifted", "exp", "scaled"))
        s_ctr, s_cT, s_cpv, s_co = (m.sem("t_cmp_" + n) for n in ("tr", "pT", "pv", "out"))
        s_sc, s_mx, s_ex, s_factor = m.sem("t_scores"), m.sem("t_max"), m.sem("t_exp"), m.sem("t_factor")
        s_scaled = [m.sem("t_scaled_dve"), m.sem("t_scaled_act")]
        BY_ACT = (1, 2, 3)
        s_tr, s_pv, s_oT = m.sem("t_tr"), m.sem("t_pv"), m.sem("t_oT")
        s_prT_hi, s_prT_lo = m.sem("t_prT_hi"), m.sem("t_prT_lo")
        s_own, s_o, s_res, s_sq = m.sem("t_own"), m.sem("t_out"), m.sem("t_res"), m.sem("t_squares")
        steps = [(t, g, b) for t in range(NT) for g in range(NG) for b in range(N_SHARED)]
        before = [sum(t + 1 for t, g, b in steps[:i]) for i in range(len(steps) + 1)]

        def half_of(i, half):
            n = steps[i][0] + 1
            return range((n + 1) // 2) if half == 0 else range((n + 1) // 2, n)

        block = ctx.enter_context(nc.Block())

        @block.sync
        def _(sp):
            sp.dma_start(wout[:], a["attn_w_out"][0].rearrange("(j p) n -> p j n", p=P)).then_inc(s_wo, 16)
            prefetch(sp, m, 1, (4, 5))
            sp.wait_ge(s_o, 2 * NT)
            prefetch(sp, m, 1, (0, 1, 2, 3))

        @block.gpsimd
        def _(pool):
            pool.memset(zero[:], 0.0).then_inc(s_z, 1)
            pool.wait_ge(s_z, 1)
            pool.affine_select(out=causal[:], in_=zero[:], compare_op=ALU.is_ge, fill=NEG, base=0,
                               pattern=[[-1, P]], channel_multiplier=1).then_inc(s_mask, 1)
            for t in range(NT):
                pool.affine_select(out=cmask[:, t, :], in_=zero[:, 0:NBLK], compare_op=ALU.is_ge, fill=NEG,
                                   base=t * P - (CMP - 1), pattern=[[-STRIDE, NBLK]],
                                   channel_multiplier=1).then_inc(s_mask, 1)

        @block.tensor
        def _(pe):
            def cmp_scores(t):
                if t >= 2:
                    pe.wait_ge(s_cmx, t - 1)
                for head in range(NH):
                    rows = slice(64 * (head % 2), 64 * (head % 2) + 64)
                    mm = pe.matmul(m.ps[2 * (t % 2) + head % 2][:, head // 2 * NBLK:(head // 2 + 1) * NBLK],
                                   m.q[rows, head // 2, t * P:(t + 1) * P], m.kc[rows, head // HPG, :],
                                   start=True, stop=True)
                    if head >= NH - 2:
                        mm.then_inc(s_csc, 1)

            def cmp_values(t):
                pe.wait_ge(s_cpn, t + 1)
                if t >= 2:
                    pe.wait_ge(s_cT, t - 1)
                for g in range(NG):
                    tr = pe.transpose(m.ps[4 + t % 2][:, g * P:(g + 1) * P],
                                      pc[:, t % 2, g * HPG:(g + 1) * HPG, :].rearrange("p h c -> p (h c)"), m.ident[:])
                tr.then_inc(s_ctr, 1)

            def cmp_product(t):
                pe.wait_ge(s_cT, t + 1)
                if t:
                    pe.wait_ge(s_co, t)
                for g in range(NG):
                    for pair in range(2):
                        i = 2 * g + pair
                        mm = pe.matmul(m.ps[6 + i // 4][:, (i % 4) * P:(i % 4 + 1) * P],
                                       m.vc[:, g, pair, :], pcT[:, t % 2, g, :], start=True, stop=True)
                mm.then_inc(s_cpv, 1)

            for t in range(NT + 2):
                if t < NT:
                    cmp_scores(t)
                if 1 <= t <= NT:
                    cmp_values(t - 1)
                if t >= 2:
                    cmp_product(t - 2)
            pe.wait_ge(s_mask, 1 + NT)

            def scores(i, pair):
                t, g, b = steps[i]
                n = (t + 1) * P
                if i:
                    pe.wait_ge(s_ex, HPG * (i - 1) + 2 * pair + 2)
                elif pair == 0:
                    pe.wait_ge(s_co, NT)
                for h in (2 * pair, 2 * pair + 1):
                    rows = slice(64 * (h % 2), 64 * (h % 2) + 64)
                    pe.matmul(m.ps[h][:, 0:n], m.qr[rows, (g * HPG + h) // 2, t * P:(t + 1) * P],
                              m.kT[rows, b, g, 0:n], start=True, stop=False)
                for h in (2 * pair, 2 * pair + 1):
                    pe.matmul(m.ps[h][:, t * P:n], m.identb[:], causal[:], start=False, stop=True).then_inc(s_sc, 1)

            def values(i, half):
                for j in half_of(i, half):
                    n = before[i] + j
                    if n >= 2:
                        pe.wait_ge(s_prT_lo, n - 1)
                    for h in range(HPG):
                        if j == 0:
                            same = [x for x in range(HPG) if (x in BY_ACT) == (h in BY_ACT)]
                            pe.wait_ge(s_scaled[h in BY_ACT], len(same) * i + same.index(h) + 1)
                        tr = pe.transpose(m.ps[4 + n % 2][:, h * P:(h + 1) * P], pr[:, i % 3, h, j * P:(j + 1) * P],
                                          m.ident[:])
                    tr.then_inc(s_tr, 1)

            def product(i, half):
                t, g, b = steps[i]
                o = i // N_SHARED
                if b == 0 and o >= 2 and half == 0:
                    pe.wait_ge(s_oT, o - 1)
                for j in half_of(i, half):
                    n = before[i] + j
                    pe.wait_ge(s_prT_lo, n + 1)
                    for p in (prT_hi, prT_lo):
                        mm = pe.matmul(m.ps[6 + o % 2][:], m.v[:, j, b, g, :, :].rearrange("p h d -> p (h d)"),
                                       p[:, i % 2, j, :], start=(b == 0 and j == 0 and p is prT_hi),
                                       stop=(b == N_SHARED - 1 and j == t and p is prT_lo))
                    if j == t:
                        mm.then_inc(s_pv, 1)

            for i in range(len(steps) + 3):
                for half in range(2):
                    if i < len(steps):
                        scores(i, half)
                    if 2 <= i < len(steps) + 2:
                        values(i - 2, half)
                    if i >= 3:
                        product(i - 3, half)
            pe.wait_ge(s_wo, 16)
            pe.wait_ge(s_oT, len(steps) // N_SHARED)
            project_out(pe, m, oT, wout, s_o)

        @block.vector
        def _(dve):
            own = Chain(dve, s_own)
            dve.wait_ge(s_mask, 1 + NT)

            def per_head(x):
                return x.unsqueeze(2).broadcast_to([P, NH, NBLK])

            def cmp_shift(t):
                dve.wait_ge(s_csc, 2 * t + 2)
                if t >= 2:
                    dve.wait_ge(s_ctr, t - 1)
                p, mxs = pc[:, t % 2, :, :], cmx[:, t % 2, :]
                for odd in range(2):
                    own.step(dve.tensor_tensor(
                        p[:, odd::2, :], m.ps[2 * (t % 2) + odd][:, 0:NH // 2 * NBLK].rearrange("p (h c) -> p h c", c=NBLK),
                        cmask[:, t, :].unsqueeze(1).broadcast_to([P, NH // 2, NBLK]), ALU.add))
                own.step(dve.tensor_reduce(mxs, p, AX.X, ALU.max))
                own.step(dve.tensor_scalar(mxs, mxs, 0.1 * NEG, None, ALU.max))
                dve.tensor_tensor(p, p, per_head(mxs), ALU.subtract).then_inc(s_cmx, 1)

            def cmp_scale(t):
                dve.wait_ge(s_cex, t + 1)
                p, sums = pc[:, t % 2, :, :], csm[:, t % 2, :]
                own.step(dve.tensor_reduce(sums, p, AX.X, ALU.add))
                own.step(dve.tensor_scalar(sums, sums, 1e-30, None, ALU.max))
                own.step(dve.reciprocal(sums, sums))
                own.step(dve.tensor_tensor(sums, sums, m.gates[:, t, :, 0], ALU.mult))
                dve.tensor_tensor(p, p, per_head(sums), ALU.mult).then_inc(s_cpn, 1)

            for t in range(NT + 1):
                if t:
                    cmp_scale(t - 1)
                if t < NT:
                    cmp_shift(t)

            def maxima(i, pair):
                t, g, b = steps[i]
                for h in (2 * pair, 2 * pair + 1):
                    dve.wait_ge(s_sc, HPG * i + h + 1)
                    top = dve.tensor_reduce(mx[:, i % 2, h:h + 1], m.ps[h][:, 0:(t + 1) * P], AX.X, ALU.max)
                own.step(top)
                pair_mx = mx[:, i % 2, 2 * pair:2 * pair + 2]
                dve.tensor_scalar(pair_mx, pair_mx, -SCALE, None, ALU.mult).then_inc(s_mx, 1)

            def scale(i):
                t, g, b = steps[i]
                dve.wait_ge(s_ex, HPG * (i + 1))
                own.step(dve.tensor_scalar(sm[:, i % 3, :], sm[:, i % 3, :], 1e-30, None, ALU.max))
                own.step(dve.reciprocal(sm[:, i % 3, :], sm[:, i % 3, :]))
                dve.tensor_tensor(sm[:, i % 3, :], sm[:, i % 3, :], m.gates[:, t, g * HPG:(g + 1) * HPG, 1 + b],
                                  ALU.mult).then_inc(s_factor, 1)
                dve.wait_ge(s_factor, i + 1)
                for h in range(HPG):
                    if h not in BY_ACT:
                        p = pr[:, i % 3, h, 0:(t + 1) * P]
                        dve.tensor_scalar(p, p, sm[:, i % 3, h:h + 1], None, ALU.mult).then_inc(s_scaled[0], 1)

            def low_parts(i, half):
                for j in half_of(i, half):
                    n = before[i] + j
                    dve.wait_ge(s_prT_hi, n + 1)
                    dve.tensor_tensor(prT_lo[:, i % 2, j, :], m.ps[4 + n % 2][:], prT_hi[:, i % 2, j, :].bitcast(F32),
                                      ALU.subtract).then_inc(s_prT_lo, 1)

            def out(o):
                t, g = o // NG, o % NG
                dve.wait_ge(s_pv, N_SHARED * (o + 1))
                dve.wait_ge(s_co, t + 1)
                for part in range(2):
                    src = m.ps[6 + o % 2][HD * part:HD * part + HD, :].rearrange("p (j two q) -> p j two q", j=2, two=2)
                    for odd in range(2):
                        dst = oT[64 * odd:64 * odd + 64, 2 * g:2 * g + 2, t * P:(t + 1) * P]
                        c = dve.tensor_tensor(dst, src[:, :, odd, :], dst, ALU.add)
                    if part == 0:
                        own.step(c)
                c.then_inc(s_oT, 1)

            for i in range(len(steps) + 3):
                for half in range(2):
                    if i < len(steps):
                        maxima(i, half)
                    if 2 <= i < len(steps) + 2:
                        low_parts(i - 2, half)
                    if half == 0 and 1 <= i <= len(steps):
                        scale(i - 1)
                if i >= 4 and (i - 4) % N_SHARED == 0:
                    out((i - 4) // N_SHARED)
            add_residual(dve, m, s_o, s_res)

        @block.scalar
        def _(act):
            def cmp_exp(t):
                act.wait_ge(s_cmx, t + 1)
                act.activation(pc[:, t % 2, :, :], pc[:, t % 2, :, :], ACT.Exp, scale=SCALE).then_inc(s_cex, 1)

            def cmp_transposed(t):
                act.wait_ge(s_ctr, t + 1)
                if t >= 2:
                    act.wait_ge(s_cpv, t - 1)
                act.activation(pcT[:, t % 2, :, :].rearrange("p g q -> p (g q)"), m.ps[4 + t % 2][:],
                               ACT.Copy).then_inc(s_cT, 1)

            def cmp_out(t):
                act.wait_ge(s_cpv, t + 1)
                for i in range(2):
                    c = act.activation(oT[:, 4 * i:4 * i + 4, t * P:(t + 1) * P],
                                       m.ps[6 + i][:].rearrange("p (j q) -> p j q", j=4), ACT.Copy)
                c.then_inc(s_co, 1)

            for t in range(NT + 2):
                if t < NT:
                    cmp_exp(t)
                if 1 <= t <= NT:
                    cmp_transposed(t - 1)
                if t >= 2:
                    cmp_out(t - 2)

            def exps(i, pair):
                t, g, b = steps[i]
                if i >= 3 and pair == 0:
                    act.wait_ge(s_tr, before[i - 2])
                n = (t + 1) * P
                act.wait_ge(s_mx, 2 * i + pair + 1)
                for h in (2 * pair, 2 * pair + 1):
                    act.activation(pr[:, i % 3, h, 0:n], m.ps[h][:, 0:n], ACT.Exp, bias=mx[:, i % 2, h:h + 1],
                                   scale=SCALE, accum_out=sm[:, i % 3, h:h + 1]).then_inc(s_ex, 1)

            def scale_by_act(i):
                act.wait_ge(s_factor, i + 1)
                for h in BY_ACT:
                    p = pr[:, i % 3, h, 0:(steps[i][0] + 1) * P]
                    act.activation(p, p, ACT.Copy, scale=sm[:, i % 3, h:h + 1]).then_inc(s_scaled[1], 1)

            def high_parts(i, half):
                if i >= 2 and half == 0:
                    act.wait_ge(s_pv, i - 1)
                for j in half_of(i, half):
                    n = before[i] + j
                    act.wait_ge(s_tr, n + 1)
                    act.activation(prT_hi[:, i % 2, j, :], m.ps[4 + n % 2][:], ACT.Copy).then_inc(s_prT_hi, 1)

            for i in range(len(steps) + 2):
                for half in range(2):
                    if i >= 2:
                        high_parts(i - 2, half)
                    if half == 1 and 1 <= i <= len(steps):
                        scale_by_act(i - 1)
                    if i < len(steps):
                        exps(i, half)
            sum_squares(act, m, s_sq, pc[:].rearrange("p b h c -> p (b h c)"), lambda t: act.wait_ge(s_res, 2 * t + 2))


_INS = ["x", "positions", "norm_mix", "norm_ffn", "conv_w_in", "conv_w", "conv_w_out", "norm_kv", "w_kv",
        "cmp_pos_k", "cmp_w1_k", "cmp_w2_k", "cmp_pos_v", "cmp_w1_v", "cmp_w2_v", "attn_w_in", "attn_w_out",
        "router_group_w", "router_group_b", "router_expert_w", "router_expert_b",
        "expert_w_gate", "expert_w_up", "expert_w_down", "norm_final"]


def kernel(**inputs):
    import numpy as np
    import concourse.bacc as bacc
    from concourse.bass_utils import run_bass_kernel_spmd

    nc = bacc.Bacc("TRN2", target_bir_lowering=False, num_devices=1)
    arrays = {f"in_{name}": np.ascontiguousarray(inputs[name]) for name in _INS}
    half = HD // 2
    arrays["in_inv_freq"] = (np.float32(10000.0) ** (-np.arange(half, dtype=np.float32) / np.float32(half)))
    a = {name[3:]: nc.dram_tensor(name, v.shape, mybir.dt.from_np(v.dtype), kind="ExternalInput").ap()
         for name, v in arrays.items()}
    out = nc.dram_tensor("out_0", (1, S, D), F32, kind="ExternalOutput").ap()
    program(nc, a, out)
    r = run_bass_kernel_spmd(nc, [arrays], core_ids=[0])
    return r.results[0]["out_0"]
```

```python
from contextlib import ExitStack

import concourse.bass as bass
from concourse import mybir

ALU = mybir.AluOpType
ACT = mybir.ActivationFunctionType
AX = mybir.AxisListType
F32 = mybir.dt.float32
F32R = mybir.dt.float32r
BF16 = mybir.dt.bfloat16
I32 = mybir.dt.int32
U32 = mybir.dt.uint32

P = 128
S = 512
D = 1024
NT = S // P
NK = D // P
EPS = 1e-6
NEG = -1e30

HD = 64
NH = 16
NG = 4
HPG = NH // NG
NBR = 3
CMP = 32
STRIDE = 16
NCMP = (S - CMP) // STRIDE + 1
NBLK = 32
HID = 256
NJ = CMP // 2
SCALE = HD ** -0.5
MAGIC = 12582912.0
PI = 3.141592653589793
PI32 = 3.1415925
TWO_PI = (6.28125, 0.0019354820251464844, -1.7484556025237907e-07)

G = 4
EPG = 8
E = G * EPG
F = D // 2
C = 64
N_OVF = 2 * S // C
ROWS = (E + N_OVF) * C
NPIECE = 6
PIECE = 2048


class Chain:

    def __init__(self, eng, sem, base=0):
        self.eng, self.sem, self.n, self.base = eng, sem, 0, base

    def step(self, ins):
        self.n += 1
        ins.then_inc(self.sem, 1)
        self.eng.wait_ge(self.sem, self.base + self.n)


class Mem:
    pass


def program(nc, a, out):
    with ExitStack() as ctx:
        m = Mem()
        m.a, m.out = a, out

        def sb(name, shape, dt=F32):
            return ctx.enter_context(nc.sbuf_tensor(name, shape, dt))

        def sem(name):
            return ctx.enter_context(nc.semaphore(name))

        m.stage_sems = []

        def stage_sem(name):
            m.stage_sems.append(nc.alloc_semaphore(name=name))
            return m.stage_sems[-1]

        m.sem = stage_sem
        m.x = sb("x_res", [P, NT, D])
        m.raw = sb("raw", [P, NPIECE, PIECE])
        m.ident = sb("ident", [P, P])
        m.identb = sb("identb", [P, P], BF16)
        m.before = sb("before", [P, P], BF16)
        m.ones = sb("ones", [P, P], BF16)
        m.iota = sb("iota", [P, P])
        m.ss = sb("ss", [P, 8])
        m.rstd = sb("rstd", [P, 5, NT])
        m.idx = sb("idx", [P, NT, 2], U32)
        m.wts = sb("wts", [P, NT, 2])
        m.novf = sb("novf", [1, 1], I32)
        m.ovf_e = sb("ovf_e", [1, N_OVF + 1], I32)
        m.ps = [ctx.enter_context(nc.psum_tensor(f"ps{i}", [P, 512], F32)) for i in range(8)]
        m.slots_y = nc.dram_tensor("slots_y", (ROWS, D), F32, kind="Internal").ap()
        m.ready = sem("constants_ready")
        m.load = [[sem(f"load{L}_{q}") for q in range(NPIECE)] for L in range(2)]

        setup(nc, m)
        conv_mixer(nc, m)
        moe(nc, m, 0)
        combine(nc, m, 0)
        recycle_semaphores(nc, m)
        with ExitStack() as kvctx:
            shared_kv(nc, m, kvctx)
            attention(nc, m)
        moe(nc, m, 1)
        combine(nc, m, 1)
        final_norm(nc, m)


def moe(nc, m, L):
    with ExitStack() as ctx:
        w = Weights(nc, m, L, ctx)
        m.xn = ctx.enter_context(nc.sbuf_tensor(f"m{L}_xn", [P, NT, D], F32))
        m.slot = ctx.enter_context(nc.sbuf_tensor(f"m{L}_slot", [P, NT, 2], F32))
        router(nc, m, L, w)
        experts(nc, m, L, w)


def recycle_semaphores(nc, m):
    nc.clear_and_free_semaphores(m.stage_sems)
    m.stage_sems = []
    nc.all_engine_barrier()


def setup(nc, m):
    filled = m.sem("const_filled")
    m.x_in = [m.sem(f"x_in{t}") for t in range(NT)]
    with nc.Block() as block:

        @block.sync
        def _(sp):
            for t in range(NT):
                sp.dma_start(m.x[:, t, :], m.a["x"][0, t * P:(t + 1) * P, :]).then_inc(m.x_in[t], 16)

        @block.gpsimd
        def _(pool):
            pool.memset(m.ident[:], 0.0).then_inc(filled, 1)
            pool.memset(m.ones[:], 1.0).then_inc(filled, 1)
            pool.iota(m.iota[:], [[1, P]], base=0, channel_multiplier=0,
                      allow_small_or_imprecise_dtypes=True).then_inc(filled, 1)
            pool.wait_ge(filled, 3)
            pool.affine_select(out=m.ident[:], in_=m.ident[:], compare_op=ALU.not_equal, fill=1.0, base=0,
                               pattern=[[-1, P]], channel_multiplier=1).then_inc(filled, 1)
            pool.affine_select(out=m.before[:], in_=m.ones[:], compare_op=ALU.is_gt, fill=0.0, base=0,
                               pattern=[[1, P]], channel_multiplier=-1).then_inc(filled, 1)
            pool.wait_ge(filled, 5)
            pool.tensor_copy(m.identb[:], m.ident[:]).then_inc(m.ready, 1)
            pool.wait_ge(m.ready, 1)


def sum_squares(act, m, sq, junk, wait_tile):
    for t in range(NT):
        wait_tile(t)
        if t:
            act.wait_ge(sq, t)
        act.activation(junk, m.x[:, t, :], ACT.Square, accum_out=m.ss[:, t:t + 1]).then_inc(sq, 1)


class Norm:

    def __init__(self, m, name, n):
        self.m, self.n = m, n
        self.ms, self.rt = m.sem(name + "_mean"), m.sem(name + "_root")
        self.own, self.xn = m.sem(name + "_own"), m.sem(name + "_normed")
        self.tr, self.ev = m.sem(name + "_transposed"), [m.sem(name + "_hT_act"), m.sem(name + "_hT_dve")]

    def scalar_root(self, act):
        m = self.m
        act.wait_ge(self.ms, 1)
        act.activation(m.rstd[:, self.n, :], m.ss[:, 4:8], ACT.Sqrt).then_inc(self.rt, 1)

    def vector_stats(self, dve, tmp):
        m, own = self.m, Chain(dve, self.own)
        dve.tensor_scalar(m.ss[:, 4:8], m.ss[:, 0:4], 1.0 / D, EPS, ALU.mult, ALU.add).then_inc(self.ms, 1)
        dve.wait_ge(self.rt, 1)
        r = m.rstd[:, self.n, :]
        own.step(dve.reciprocal(r, r))
        own.step(dve.tensor_tensor(tmp, r, r, ALU.mult))
        own.step(dve.tensor_tensor(tmp, tmp, m.ss[:, 4:8], ALU.mult))
        own.step(dve.tensor_scalar(tmp, tmp, -0.5, 1.5, ALU.mult, ALU.add))
        own.step(dve.tensor_tensor(r, r, tmp, ALU.mult))

    def vector_normed(self, dve, xn):
        for t in range(NT):
            dve.tensor_scalar(xn[:, t, :], self.m.x[:, t, :], self.m.rstd[:, self.n, t:t + 1], None,
                              ALU.mult).then_inc(self.xn, 1)

    def tensor(self, pe, xn):
        for t in range(NT):
            pe.wait_ge(self.xn, t + 1)
            for k in range(NK):
                tr = pe.transpose(self.m.ps[k][:, t * P:(t + 1) * P], xn[:, t, k::NK], self.m.ident[:])
                if t == NT - 1:
                    tr.then_inc(self.tr, 1)

    def evacuate(self, eng, dve, outs):
        for k in range(dve, NK, 2):
            eng.wait_ge(self.tr, k + 1)
            for hT, gain in outs:
                src, g = self.m.ps[k][:], None if gain is None else gain[:, k:k + 1]
                if dve:
                    i = eng.tensor_copy(hT[:, k, :], src) if g is None else \
                        eng.tensor_scalar(hT[:, k, :], src, g, None, ALU.mult)
                else:
                    i = eng.activation(hT[:, k, :], src, ACT.Copy, scale=1.0 if g is None else g)
            i.then_inc(self.ev[dve], 1)

    def wait_hT(self, pe):
        pe.wait_ge(self.ev[0], NK // 2)
        pe.wait_ge(self.ev[1], NK // 2)


def conv_mixer(nc, m):
    a = m.a
    CW = 256
    NCH = D // CW
    with ExitStack() as ctx:
        def sb(name, shape, dt=F32):
            return ctx.enter_context(nc.sbuf_tensor(name, shape, dt))

        hT = sb("c_hT", [P, NK, S])
        gain = sb("c_gain", [P, NK])
        cw = sb("c_cw", [P, 3, NK])
        win = sb("c_win", [P, 2, NK, 3, CW])
        wout = sb("c_wout", [P, NK, D])
        gated = sb("c_gated", [P, NK, S])
        xn = gated.rearrange("p k s -> p (k s)").rearrange("p (t d) -> p t d", t=NT)
        u = sb("c_u", [P, 2, S + 2])
        csb = sb("c_csb", [P, 2, S])
        y = sb("c_y", [P, 2, S])
        tmp = sb("c_tmp", [P, NT])
        zero = sb("c_zero", [P, D])
        s_zero, s_blank = m.sem("c_zero_set"), m.sem("c_blank_rows")
        nrm = Norm(m, "c", 0)
        s_gain, s_cw, s_wout = m.sem("c_gain_in"), m.sem("c_cw_in"), m.sem("c_wout_in")
        s_win = [m.sem(f"c_win{i}") for i in range(2)]
        s_proj, s_copied, s_own = m.sem("c_projected"), m.sem("c_copied"), m.sem("c_own2")
        s_sq, s_sq2 = m.sem("c_squares"), m.sem("c_squares_after")
        s_u, s_gated, s_o, s_res = m.sem("c_u_done"), m.sem("c_gated_done"), m.sem("c_out"), m.sem("c_res")
        block = ctx.enter_context(nc.Block())
        w_in = a["conv_w_in"][0].rearrange("(p k) (c n w) -> n c p k w", k=NK, c=3, w=CW)

        @block.sync
        def _(sp):
            with nc.allow_non_contiguous_dma(reason="small vectors"):
                sp.dma_start(gain[:], a["norm_mix"][0].rearrange("(p k) -> p k", k=NK)).then_inc(s_gain, 16)
                sp.dma_start(cw[:], a["conv_w"][0].rearrange("w (j p) -> p w j", p=P)).then_inc(s_cw, 16)
            for n in range(NCH):
                if n >= 2:
                    sp.wait_ge(s_proj, 6 * (n - 1))
                for c in range(3):
                    sp.dma_start(win[:, n % 2, :, c, :], w_in[n, c]).then_inc(s_win[n % 2], 16)
            sp.dma_start(wout[:], a["conv_w_out"][0].rearrange("(j p) n -> p j n", p=P)).then_inc(s_wout, 16)
            prefetch(sp, m, 0)
            sp.wait_ge(s_zero, 1)
            blank = [m.slots_y[i * P:(i + 1) * P, :] for i in range(E * C // P, ROWS // P)]
            for rows in blank:
                sp.dma_start(rows, zero[:]).then_inc(s_blank, 16)
            sp.wait_ge(s_blank, 16 * len(blank))

        @block.scalar
        def _(act):
            junk = y[:].rearrange("p b s -> p (b s)")
            sum_squares(act, m, s_sq, junk, lambda t: act.wait_ge(m.x_in[t], 16))
            nrm.scalar_root(act)
            act.wait_ge(s_gain, 16)
            nrm.evacuate(act, 0, [(hT, gain)])
            for j in range(NK):
                act.wait_ge(s_proj, 3 * j + 1)
                if j >= 2:
                    act.wait_ge(s_u, j - 1)
                act.activation(csb[:, j % 2, :], m.ps[3 * (j % 2)][:], ACT.Copy).then_inc(s_copied, 1)
            sum_squares(act, m, s_sq2, junk, lambda t: act.wait_ge(s_res, 2 * t + 2))

        @block.vector
        def _(dve):
            own = Chain(dve, s_own)
            dve.memset(zero[:], 0.0).then_inc(s_zero, 1)
            for b in range(2):
                own.step(dve.memset(u[:, b, 0:2], 0.0))
            dve.wait_ge(s_sq, NT)
            nrm.vector_stats(dve, tmp[:])
            nrm.vector_normed(dve, xn)
            dve.wait_ge(s_gain, 16)
            nrm.evacuate(dve, 1, [(hT, gain)])
            dve.wait_ge(s_cw, 16)
            for j in range(NK):
                b = j % 2
                dve.wait_ge(s_copied, j + 1)
                dve.wait_ge(s_proj, 3 * j + 2)
                dve.tensor_tensor(u[:, b, 2:], csb[:, b, :], m.ps[3 * b + 1][:], ALU.mult).then_inc(s_u, 1)
                dve.wait_ge(s_u, j + 1)
                own.step(dve.tensor_scalar(y[:, b, :], u[:, b, 0:S], cw[:, 0, j:j + 1], None, ALU.mult))
                for w in (1, 2):
                    own.step(dve.scalar_tensor_tensor(out=y[:, b, :], in0=u[:, b, w:w + S],
                                                      scalar=cw[:, w, j:j + 1], in1=y[:, b, :],
                                                      op0=ALU.mult, op1=ALU.add))
                dve.wait_ge(s_proj, 3 * j + 3)
                dve.tensor_tensor(gated[:, j, :], y[:, b, :], m.ps[3 * b + 2][:], ALU.mult).then_inc(s_gated, 1)
            add_residual(dve, m, s_o, s_res)

        @block.tensor
        def _(pe):
            nrm.tensor(pe, xn)
            nrm.wait_hT(pe)
            for j in range(NK):
                n = j // 2
                pe.wait_ge(s_win[n % 2], 48 * (n // 2 + 1))
                if j >= 2:
                    pe.wait_ge(s_gated, j - 1)
                for i, c in enumerate((1, 2, 0)):
                    for k in range(NK):
                        mm = pe.matmul(m.ps[3 * (j % 2) + i][:],
                                       win[:, n % 2, k, c, (j % 2) * P:(j % 2 + 1) * P], hT[:, k, :],
                                       start=(k == 0), stop=(k == NK - 1))
                    mm.then_inc(s_proj, 1)
            pe.wait_ge(s_wout, 16)
            pe.wait_ge(s_gated, NK)
            project_out(pe, m, gated, wout, s_o)


def project_out(pe, m, feats, w, s_o):
    for t in range(NT):
        for h in range(2):
            for k in range(NK):
                mm = pe.matmul(m.ps[2 * t + h][:], feats[:, k, t * P:(t + 1) * P], w[:, k, h * 512:(h + 1) * 512],
                               start=(k == 0), stop=(k == NK - 1))
            mm.then_inc(s_o, 1)


def add_residual(dve, m, s_o, s_res):
    for i in range(2 * NT):
        dve.wait_ge(s_o, i + 1)
        x = m.x[:, i // 2, (i % 2) * 512:(i % 2 + 1) * 512]
        dve.tensor_tensor(x, x, m.ps[i][:], ALU.add).then_inc(s_res, 1)


def piece_src(m, L, q, e):
    name = ("expert_w_gate", "expert_w_up", "expert_w_down")[q // 2]
    w = m.a[name][L]
    if q < 4:
        w = w.rearrange("e (p h k) n -> h e p (k n)", p=P, h=2)[q % 2]
    else:
        w = w.rearrange("e (h p k) n -> h e p (k n)", h=2, p=P)[q % 2]
    return w[e] if isinstance(e, int) else w[bass.ds(e, 1)].rearrange("e p n -> (e p) n")


def prefetch(sp, m, L, slots=(0, 1, 4, 5, 2, 3)):
    piece = {0: 0, 1: 1, 4: 2, 5: 3, 2: 4, 3: 5}
    for slot in slots:
        q = piece[slot]
        sp.dma_start(m.raw[:, slot, :], piece_src(m, L, q, 0)).then_inc(m.load[L][slot], 16)


def router(nc, m, L, w):
    a = m.a
    with ExitStack() as ctx:
        def sb(name, shape, dt=F32):
            return ctx.enter_context(nc.sbuf_tensor(f"r{L}_{name}", shape, dt))

        def sem(name):
            return m.sem(f"r{L}_{name}")

        NL = G + E
        xn, slotf = m.xn, m.slot
        hT = sb("hT", [P, NK, S])
        gb = sb("gb", [P, D])
        wr = sb("wr", [P, NK, NL])
        bias = sb("bias", [P, NL])
        lg = sb("lg", [P, NT, NL])
        g_work, g_exp, g_onehot = (sb(n, [P, NT, G]) for n in ("g_work", "g_exp", "g_onehot"))
        el = sb("el", [P, NT, E])
        work = sb("work", [P, NT, E])
        oh = [sb(f"oh{i}", [P, NT, E]) for i in range(2)]
        both = sb("both", [P, NT, E], BF16)
        top1, top2, gap, gap_exp, denom, place = (
            sb(n, [P, NT]) for n in ("top1", "top2", "gap", "gap_exp", "denom", "place"))
        slot = sb("slot", [P, NT, E])
        late = sb("late", [P, NT, E])
        falling = sb("falling", [P, E])
        more = sb("more", [P, E, 8])
        ovn = sb("ovn", [P, E])
        inc = sb("inc", [P, E])
        onef = sb("onef", [P, E])
        base = sb("base", [P, 2, E])
        tab = sb("tab", [1, N_OVF, E])
        tabf = sb("tabf", [1, N_OVF + 1])
        tmp = sb("tmp", [P, NT])
        nrm = Norm(m, f"r{L}", 1 + 2 * L)
        s_w, s_gb = sem("weights_in"), sem("gain_in")
        s_lg, s_one, s_rank = sem("logits"), sem("onehot"), sem("ranks")
        s_ge, s_e, s_own = sem("exp_ready"), sem("exp_done"), sem("own2")
        s_slots = sem("slots_ready")
        block = ctx.enter_context(nc.Block())

        @block.sync
        def _(sp):
            sp.dma_start(gb[:], a["norm_ffn"][L:L + 1, :].broadcast_to([P, D])).then_inc(s_gb, 16)
            with nc.allow_non_contiguous_dma(reason="router weights are 1% of the bytes"):
                sp.dma_start(wr[:, :, 0:G], a["router_group_w"][L].rearrange("(p k) g -> p k g", k=NK)).then_inc(s_w, 16)
                sp.dma_start(wr[:, :, G:], a["router_expert_w"][L].rearrange("(p k) g -> p k g", k=NK)).then_inc(s_w, 16)
                sp.dma_start(bias[:, 0:G], a["router_group_b"][L:L + 1, :].broadcast_to([P, G])).then_inc(s_w, 16)
                sp.dma_start(bias[:, G:], a["router_expert_b"][L:L + 1, :].broadcast_to([P, E])).then_inc(s_w, 16)

            w.load_second(sp)

        @block.scalar
        def _(act):
            nrm.scalar_root(act)
            nrm.evacuate(act, 0, [(hT, None)])
            w.split_first(act, "act")
            act.wait_ge(s_ge, 1)
            act.activation(g_exp[:], g_work[:], ACT.Exp).then_inc(s_e, 1)
            act.wait_ge(s_ge, 2)
            act.activation(gap_exp[:], gap[:], ACT.Exp).then_inc(s_e, 1)

        @block.tensor
        def _(pe):
            nrm.tensor(pe, xn)
            nrm.wait_hT(pe)
            pe.wait_ge(s_w, 64)
            for t in range(NT):
                for k in range(NK):
                    mm = pe.matmul(m.ps[0][:, t * NL:(t + 1) * NL], hT[:, k, t * P:(t + 1) * P], wr[:, k, :],
                                   start=(k == 0), stop=(k == NK - 1))
            mm.then_inc(s_lg, 1)
            pe.wait_ge(s_one, 1)
            for t in range(NT):
                for t2 in range(t + 1):
                    mm = pe.matmul(m.ps[1][:, t * E:(t + 1) * E], (m.before if t2 == t else m.ones)[:],
                                   both[:, t2, :], start=(t2 == 0), stop=(t2 == t))
            for t in range(NT):
                mm = pe.matmul(m.ps[1][:, NT * E:(NT + 1) * E], m.ones[:], both[:, t, :],
                               start=(t == 0), stop=(t == NT - 1))
            mm.then_inc(s_rank, 1)

        @block.vector
        def _(dve):
            own = Chain(dve, s_own)
            nrm.vector_stats(dve, tmp[:])
            dve.wait_ge(s_gb, 16)
            for t in range(NT):
                dve.scalar_tensor_tensor(out=xn[:, t, :], in0=m.x[:, t, :], scalar=m.rstd[:, nrm.n, t:t + 1],
                                         in1=gb[:], op0=ALU.mult, op1=ALU.mult).then_inc(nrm.xn, 1)
            nrm.evacuate(dve, 1, [(hT, None)])
            own.step(dve.tensor_scalar(falling[:], m.iota[:, 0:E], -1.0, 64.0, ALU.mult, ALU.add))
            own.step(dve.tensor_scalar(more[:], m.iota[:, 0:8].unsqueeze(1).broadcast_to([P, E, 8]),
                                       1.0, float(C), ALU.add, ALU.mult))
            own.step(dve.memset(onef[:], 1.0))
            own.step(dve.tensor_scalar(base[:, 0, :], m.iota[:, 0:E], float(C), None, ALU.mult))
            w.split_first(dve, "dve")
            dve.wait_ge(s_w, 64)
            dve.wait_ge(s_lg, 1)

            def bc(x, n):
                return x.unsqueeze(2).broadcast_to([P, NT, n])

            own.step(dve.tensor_tensor(lg[:], m.ps[0][:, 0:NT * NL].rearrange("p (t n) -> p t n", t=NT),
                                       bias[:].unsqueeze(1).broadcast_to([P, NT, NL]), ALU.add))

            def first_max(vals, n, top, onehot, scratch):
                own.step(dve.tensor_reduce(top, vals, AX.X, ALU.max))
                own.step(dve.tensor_tensor(scratch, vals, bc(top, n), ALU.is_equal))
                own.step(dve.tensor_tensor(scratch, scratch, down(n), ALU.mult))
                own.step(dve.tensor_reduce(place[:], scratch, AX.X, ALU.max))
                own.step(dve.tensor_tensor(onehot, scratch, bc(place[:], n), ALU.is_equal))

            def down(n):
                return falling[:, 0:n].unsqueeze(1).broadcast_to([P, NT, n])

            gl = lg[:, :, 0:G]
            first_max(gl, G, top1[:], g_onehot[:], g_work[:])
            dve.tensor_tensor(g_work[:], gl, bc(top1[:], G), ALU.subtract).then_inc(s_ge, 1)
            elv = el[:].rearrange("p t (g e) -> p t g e", g=G)
            gsel = g_onehot[:].unsqueeze(3).broadcast_to([P, NT, G, EPG])
            own.step(dve.tensor_tensor(elv, lg[:, :, G:].rearrange("p t (g e) -> p t g e", g=G), gsel, ALU.mult))
            own.step(dve.tensor_scalar(g_onehot[:], g_onehot[:], -1.0, -NEG, ALU.add, ALU.mult))
            own.step(dve.tensor_tensor(elv, elv, gsel, ALU.add))
            first_max(el[:], E, top1[:], oh[0][:], work[:])
            own.step(dve.scalar_tensor_tensor(out=el[:], in0=oh[0][:], scalar=NEG, in1=el[:],
                                              op0=ALU.mult, op1=ALU.add))
            first_max(el[:], E, top2[:], oh[1][:], work[:])
            dve.tensor_tensor(both[:], oh[0][:], oh[1][:], ALU.add).then_inc(s_one, 1)
            dve.tensor_tensor(gap[:], top2[:], top1[:], ALU.subtract).then_inc(s_ge, 1)
            dve.wait_ge(s_rank, 1)
            rank = m.ps[1][:, 0:NT * E].rearrange("p (t e) -> p t e", t=NT)
            cnt = m.ps[1][:, NT * E:(NT + 1) * E]
            own.step(dve.tensor_tensor(more[:], cnt.unsqueeze(2).broadcast_to([P, E, 8]), more[:], ALU.is_gt))
            own.step(dve.tensor_reduce(ovn[:], more[:], AX.X, ALU.add))
            own.step(dve.tensor_tensor_scan(inc[:], onef[:], ovn[:], 0.0, ALU.mult, ALU.add))
            own.step(dve.tensor_tensor(base[:, 1, :], inc[:], ovn[:], ALU.subtract))
            own.step(dve.tensor_scalar(base[:, 1, :], base[:, 1, :], float(C), float(C * E - C), ALU.mult, ALU.add))
            own.step(dve.tensor_tensor(base[:, 1, :], base[:, 1, :], base[:, 0, :], ALU.subtract))
            own.step(dve.tensor_scalar(late[:], rank, float(C) - 0.5, None, ALU.is_gt))
            own.step(dve.tensor_tensor(late[:], late[:], base[:, 1, :].unsqueeze(1).broadcast_to([P, NT, E]), ALU.mult))
            own.step(dve.tensor_tensor(slot[:], rank, base[:, 0, :].unsqueeze(1).broadcast_to([P, NT, E]), ALU.add))
            own.step(dve.tensor_tensor(slot[:], slot[:], late[:], ALU.add))
            for k in range(2):
                own.step(dve.tensor_tensor(work[:], slot[:], oh[k][:], ALU.mult))
                own.step(dve.tensor_reduce(slotf[:, :, k], work[:], AX.X, ALU.add))
            dve.tensor_copy(m.idx[:], slotf[:]).then_inc(s_slots, 1)
            dve.wait_ge(s_e, 1)
            own.step(dve.tensor_reduce(denom[:], g_exp[:], AX.X, ALU.add))
            dve.wait_ge(s_e, 2)
            own.step(dve.tensor_scalar(place[:], gap_exp[:], 1.0, None, ALU.add))
            own.step(dve.tensor_tensor(denom[:], denom[:], place[:], ALU.mult))
            own.step(dve.reciprocal(m.wts[:, :, 0], denom[:]))
            own.step(dve.tensor_tensor(m.wts[:, :, 1], m.wts[:, :, 0], gap_exp[:], ALU.mult))
            own.step(dve.tensor_tensor(tab[:], inc[0:1, :].unsqueeze(1).broadcast_to([1, N_OVF, E]),
                                       m.iota[0:1, 0:N_OVF].unsqueeze(2).broadcast_to([1, N_OVF, E]), ALU.is_le))
            own.step(dve.memset(tabf[:, 0:1], float(E - 1)))
            own.step(dve.tensor_reduce(tabf[:, 1:], tab[:], AX.X, ALU.add))
            own.step(dve.tensor_scalar(tabf[:], tabf[:], float(E - 1), None, ALU.min))
            own.step(dve.tensor_copy(m.ovf_e[:], tabf[:]))
            own.step(dve.tensor_copy(m.novf[:], inc[0:1, E - 1:E]))

        @block.gpsimd
        def _(pool):
            w.split_first(pool, "pool")


def may_wait(eng, s, v):
    if not isinstance(v, int) or v > 0:
        eng.wait_ge(s, v)


GATE, DOWN, UP = (0, 1), (2, 3), (4, 5)
HI = ("act", "act", "dve", "act", "dve", "act")
LO = ("dve", "pool", "dve", "pool", "dve", "dve")


class Weights:

    def __init__(self, nc, m, L, ctx):
        self.m, self.L, self.parts = m, L, {}
        self.s_hi = {"act": m.sem(f"w{L}_hi_act"), "dve": m.sem(f"w{L}_hi_dve")}
        self.s_lo = {"dve": m.sem(f"w{L}_lo_dve"), "pool": m.sem(f"w{L}_lo_pool")}
        self.s_used = m.sem(f"w{L}_used")
        self.make_room(nc, ctx, "gate_up", GATE + UP)

    def make_room(self, nc, ctx, name, pieces):
        hi, lo = (ctx.enter_context(nc.sbuf_tensor(f"w{self.L}_{name}_{part}", [P, len(pieces), PIECE], F32R))
                  for part in ("hi", "lo"))
        for n, k in enumerate(pieces):
            self.parts[k] = (hi[:, n, :], lo[:, n, :])

    def made(self, eng, table, c, k, last=False):
        who, first_step = table[k], isinstance(c, int) and c == 0
        down = sum(table[q] == who for q in DOWN)
        before = [q for q in range(k) if not (last and q in GATE) and not (first_step and q in DOWN)]
        first = 0 if first_step else c * table.count(who) - down
        may_wait(eng, (self.s_hi if table is HI else self.s_lo)[who],
                 first + sum(table[q] == who for q in before) + 1)

    def used(self, eng, c, k, last=False):
        if isinstance(c, int) and c < 0 or isinstance(c, int) and c == 0 and k in DOWN:
            return
        if isinstance(c, int) and c == 0:
            eng.wait_ge(self.s_used, {0: 1, 1: 2, 4: 3, 5: 4}[k])
        else:
            eng.wait_ge(self.s_used, c * NPIECE - 2 + k + 1 - (2 if last else 0))

    def split(self, eng, who, c, k, last=False):
        raw, (hi, lo) = self.m.raw[:, k, :], self.parts[k]
        if HI[k] == who:
            may_wait(eng, self.m.load[self.L][k], (c if k in DOWN else c + 1) * 16)
            self.used(eng, c - 1, k)
            h = eng.activation(hi, raw, ACT.Copy) if who == "act" else eng.tensor_copy(hi, raw)
            h.then_inc(self.s_hi[who], 1)
        if LO[k] == who:
            self.made(eng, HI, c, k, last)
            self.used(eng, c - 1, k)
            eng.tensor_tensor(lo, raw, hi.bitcast(F32), ALU.subtract).then_inc(self.s_lo[who], 1)

    def load(self, sp, c, k, q, e):
        self.made(sp, LO, c - 1, k)
        sp.dma_start(self.m.raw[:, k, :], piece_src(self.m, self.L, q, e)).then_inc(self.m.load[self.L][k], 16)

    def split_first(self, eng, who):
        for k in GATE + UP:
            self.split(eng, who, 0, k)

    def load_second(self, sp):
        for k, q in zip(GATE + UP, range(4)):
            self.load(sp, 1, k, q, 1)


def experts(nc, m, L, w):
    with ExitStack() as ctx:
        def sb(name, shape, dt=F32):
            return ctx.enter_context(nc.sbuf_tensor(f"e{L}_{name}", shape, dt))

        def sem(name):
            return m.sem(f"e{L}_{name}")

        H = 2 * C
        FH = F // 2
        pick = sb("pick", [P, NT, H])
        second = sb("second", [P, NT, H])
        xst = sb("xst", [P, 2, NK, H], F32R)
        w.make_room(nc, ctx, "down", DOWN)
        part = sb("part", [P, 2, FH])
        gate = sb("gate", [P, FH])
        up = sb("up", [P, FH])
        act_g = sb("act_g", [P, FH])
        hid = sb("hid", [P, FH])
        hst = sb("hst", [P, 2, 2, H], F32R)
        ypart = sb("ypart", [C, D])
        yrow = sb("yrow", [C, D])
        s_st, s_eq, s_pick, s_moved = sem("y_out"), sem("slot_equal"), sem("picked"), sem("slot_moved")
        s_xt, s_xhi, s_xlo = sem("x_transposed"), sem("x_hi"), sem("x_lo")
        s_used = w.s_used
        s_part = [sem("gate_part"), sem("up_part")]
        s_sum = [sem("gate_sum"), sem("up_sum")]
        s_sg, s_h = sem("silu"), sem("hidden")
        s_ht, s_hhi, s_hlo = sem("h_transposed"), sem("h_hi"), sem("h_lo")
        s_yp, s_y = sem("y_part"), sem("y_sum")
        ps_x, ps_gu, ps_h, ps_y = m.ps[0:2], m.ps[2:4], m.ps[4], m.ps[5:7]
        wait, made, used = may_wait, w.made, w.used

        def pe_rows(pe, i, half):
            wait(pe, s_pick, i + 1)
            wait(pe, s_xlo, i * 2)
            for k in range(4 * half, 4 * half + 4):
                for t in range(NT):
                    mm = pe.matmul(ps_x[k // 4][:, (k % 4) * P:(k % 4 + 1) * P], m.xn[:, t, k::NK], pick[:, t, :],
                                   start=(t == 0), stop=(t == NT - 1))
            if half:
                mm.then_inc(s_xt, 1)

        def pe_gate_up(pe, c, u, i, pieces):
            wait(pe, s_xlo, c + 1)
            for b, k in enumerate(pieces):
                made(pe, LO, c, k)
                if b == 0:
                    wait(pe, s_sum[i], c)
                for kk in range(4):
                    for part in range(2):
                        mm = pe.matmul(ps_gu[i][:], xst[:, u, 4 * b + kk, :], w.parts[k][part][:, kk * F:(kk + 1) * F],
                                       start=(b == 0 and kk == 0 and part == 0),
                                       stop=(b == 1 and kk == 3 and part == 1))
                mm.then_inc(s_used, 1)

        def pe_down(pe, c, last=False):
            wait(pe, s_h, c)
            wait(pe, s_hlo, c - 1)
            for k in range(2):
                mm = pe.transpose(ps_h[:, k * P:(k + 1) * P], hid[:, k::2], m.ident[:])
            mm.then_inc(s_ht, 1)
            wait(pe, s_hlo, c)
            wait(pe, s_y, c - 1)
            for h, k in enumerate(DOWN):
                made(pe, LO, c, k, last)
                for kk in range(2):
                    for part in range(2):
                        for n in range(2):
                            mm = pe.matmul(ps_y[n][:], hst[:, kk, h, :],
                                           w.parts[k][part][:, kk * D + n * 512:kk * D + (n + 1) * 512],
                                           start=(h == 0 and kk == 0 and part == 0),
                                           stop=(h == 1 and kk == 1 and part == 1))
                mm.then_inc(s_used, 1)

        def pe_step(pe, c, u):
            start = isinstance(c, int) and c == 0
            if start:
                pe_rows(pe, 0, 0)
                pe_rows(pe, 0, 1)
            pe_gate_up(pe, c, u, 0, GATE)
            if u == 1:
                pe_rows(pe, (c + 1) // 2 if isinstance(c, int) else (c + 1) >> 1, 1)
            if not start:
                pe_down(pe, c)
            if u == 0:
                pe_rows(pe, 1 if start else (c >> 1) + 1, 0)
            pe_gate_up(pe, c, u, 1, UP)

        def act_hi(act, c, k, last=False):
            if HI[k] == "act":
                w.split(act, "act", c, k, last)

        def act_part(act, c, i, at, k):
            used(act, at, k)
            wait(act, s_sum[i], c)
            act.activation(part[0:C, i, :], ps_gu[i][C:H, 0:FH], ACT.Copy)
            act.activation(part[C:H, i, :], ps_gu[i][0:C, FH:F], ACT.Copy).then_inc(s_part[i], 1)

        def act_h_hi(act, c):
            wait(act, s_ht, c)
            used(act, c - 1, DOWN[1])
            act.activation(hst[:, :, :, 0:C], ps_h[:, 0:2 * P].rearrange("p (k h c) -> p k h c", k=2, h=2),
                           ACT.Copy).then_inc(s_hhi, 1)

        def act_y(act, c, last=False):
            used(act, c, DOWN[1], last)
            wait(act, s_y, c - 1)
            for n in range(2):
                act.activation(ypart[:, n * 512:(n + 1) * 512], ps_y[n][C:H, :], ACT.Copy).then_inc(s_yp, 1)
            wait(act, s_y, c)
            act.dma_start(m.slots_y[bass.ds(c * C - C, C), :], yrow[:]).then_inc(s_st, 16)

        def rows_view(u):
            return [(ps_x[b][:].rearrange("p (k u c) -> p k u c", k=4, u=2)[:, :, u, :],
                     xst[:, u, 4 * b:4 * b + 4, :]) for b in range(2)]

        def act_x_hi(act, c, u):
            wait(act, s_xt, (c // 2 if isinstance(c, int) else c >> 1) + 1)
            used(act, c - 2, UP[1])
            wait(act, s_xlo, c)
            for src, dst in rows_view(u):
                act.activation(dst[:, :, 0:C], src, ACT.Copy).then_inc(s_xhi, 1)

        def act_step(act, c, u):
            start = isinstance(c, int) and c == 0
            if start:
                act_x_hi(act, 0, 0)
                act_x_hi(act, 1, 1)
            else:
                act_hi(act, c, GATE[0])
                act_hi(act, c, GATE[1])
                act_part(act, c - 1, 1, c - 1, UP[1])
                if u == 0:
                    act_x_hi(act, c + 1, 1)
                if not (isinstance(c, int) and c == 1):
                    act_y(act, c - 1)
                act_hi(act, c, DOWN[1])
            act_part(act, c, 0, c, GATE[1])
            if not start:
                act_h_hi(act, c)
            wait(act, s_sum[0], c + 1)
            wait(act, s_h, c)
            act.activation(act_g[:], gate[:], ACT.Silu).then_inc(s_sg, 1)
            if not start:
                act_hi(act, c, UP[1])
            if u == 1:
                act_x_hi(act, c + 1, 0)

        def act_tail(act, c):
            act_part(act, c - 1, 1, c - 1, UP[1])
            for k in DOWN:
                act_hi(act, c, k, True)
            act_h_hi(act, c)
            act_y(act, c - 1)
            act_y(act, c, True)

        split = w.split

        def dve_sum(dve, c, i, dst):
            wait(dve, s_part[i], c + 1)
            wait(dve, (s_sg, s_h)[i], c)
            dve.tensor_tensor(dst[0:C, :], ps_gu[i][0:C, 0:FH], part[0:C, i, :], ALU.add)
            dve.tensor_tensor(dst[C:H, :], ps_gu[i][C:H, FH:F], part[C:H, i, :], ALU.add).then_inc(s_sum[i], 1)

        def dve_hidden(dve, c):
            dve_sum(dve, c - 1, 1, up)
            wait(dve, s_sum[1], c)
            wait(dve, s_sg, c)
            wait(dve, s_ht, c - 1)
            dve.tensor_tensor(hid[:], act_g[:], up[:], ALU.mult).then_inc(s_h, 1)

        def dve_h_lo(dve, c):
            wait(dve, s_hhi, c)
            dve.tensor_tensor(hst[:, :, :, C:H], ps_h[:, 0:2 * P].rearrange("p (k h c) -> p k h c", k=2, h=2),
                              hst[:, :, :, 0:C].bitcast(F32), ALU.subtract).then_inc(s_hlo, 1)

        def dve_y(dve, c):
            wait(dve, s_yp, 2 * c)
            wait(dve, s_st, 16 * c - 16)
            for n in range(2):
                o = dve.tensor_tensor(yrow[:, n * 512:(n + 1) * 512], ps_y[n][0:C, :],
                                      ypart[:, n * 512:(n + 1) * 512], ALU.add)
            o.then_inc(s_y, 1)

        def dve_pick(dve, i):
            wait(dve, s_xt, i)
            wait(dve, s_moved, i)
            slots = m.iota[:].unsqueeze(1).broadcast_to([P, NT, H])
            for k, dst in enumerate((pick, second)):
                e = dve.tensor_tensor(dst[:], slots, m.slot[:, :, k:k + 1].broadcast_to([P, NT, H]), ALU.is_equal)
            e.then_inc(s_eq, 1)

        def dve_x_lo(dve, c, u):
            wait(dve, s_xhi, c * 2 + 2)
            for src, dst in rows_view(u):
                o = dve.tensor_tensor(dst[:, :, C:H], src, dst[:, :, 0:C].bitcast(F32), ALU.subtract)
            o.then_inc(s_xlo, 1)

        def dve_step(dve, c, u):
            start = isinstance(c, int) and c == 0
            if start:
                dve_pick(dve, 0)
                dve_x_lo(dve, 0, 0)
                dve_x_lo(dve, 1, 1)
                dve_pick(dve, 1)
            else:
                if u == 0:
                    dve_pick(dve, (c >> 1) + 1)
                split(dve, "dve", c, GATE[0])
                dve_hidden(dve, c)
                if not (isinstance(c, int) and c == 1):
                    dve_y(dve, c - 1)
                if u == 0:
                    dve_x_lo(dve, c + 1, 1)
                split(dve, "dve", c, DOWN[0])
            dve_sum(dve, c, 0, gate)
            if not start:
                dve_h_lo(dve, c)
                split(dve, "dve", c, UP[0])
                split(dve, "dve", c, UP[1])
            if u == 1:
                dve_x_lo(dve, c + 1, 0)

        def dve_tail(dve, c):
            dve_hidden(dve, c)
            for k in DOWN:
                split(dve, "dve", c, k, True)
            dve_y(dve, c - 1)
            dve_h_lo(dve, c)
            dve_y(dve, c)

        def pool_pick(pool, i):
            wait(pool, s_eq, i + 1)
            pool.tensor_tensor(pick[:], pick[:], second[:], ALU.add).then_inc(s_pick, 1)
            pool.tensor_scalar(m.slot[:], m.slot[:], float(H), None, ALU.subtract).then_inc(s_moved, 1)

        def pool_step(pool, c, u):
            if isinstance(c, int) and c == 0:
                pool_pick(pool, 0)
                pool_pick(pool, 1)
            elif u == 0:
                pool_pick(pool, (c >> 1) + 1)
            if not (isinstance(c, int) and c == 0):
                for k in range(NPIECE):
                    split(pool, "pool", c, k)

        def pool_tail(pool, c):
            for k in DOWN:
                split(pool, "pool", c, k, True)
            pool.wait_ge(s_st, c * 16)

        sp_load = w.load

        def sp_step(sp, c, e, before):
            for k, q in ((0, 0), (1, 1)):
                sp_load(sp, c, k, q, e)
            for k, q in ((2, 4), (3, 5)):
                sp_load(sp, c, k, q, before)
            for k, q in ((4, 2), (5, 3)):
                sp_load(sp, c, k, q, e)

        def pipeline(eng, step, tail):
            step(eng, 0, 0)
            step(eng, 1, 1)
            with eng.Fori(1, E // 2) as i:
                step(eng, i * 2, 0)
                step(eng, i * 2 + 1, 1)
            n = eng.value_load(m.novf[0:1, 0:1], min_val=0, max_val=N_OVF)
            with eng.If(0 < n):
                with eng.Fori(0, N_OVF // 4) as quad:
                    with eng.If(quad * 4 < n):
                        with eng.Fori(0, 2) as pair:
                            j = quad * 4 + pair * 2
                            with eng.If(j < n):
                                step(eng, j + E, 0)
                            with eng.If(j + 1 < n):
                                step(eng, j + (E + 1), 1)
            tail(eng, n + E)

        block = ctx.enter_context(nc.Block())

        @block.sync
        def _(sp):
            def expert(i):
                return sp.value_load(m.ovf_e[0:1, bass.ds(i, 1)], min_val=0, max_val=E - 1)

            sp_step(sp, 2, 2, 1)
            with sp.Fori(3, E) as c:
                sp_step(sp, c, c, c - 1)
            n = sp.value_load(m.novf[0:1, 0:1], min_val=0, max_val=N_OVF)
            with sp.If(0 < n):
                with sp.Fori(0, N_OVF // 4) as quad:
                    with sp.If(quad * 4 < n):
                        with sp.Fori(0, 4) as i:
                            j = quad * 4 + i
                            with sp.If(j < n):
                                sp_step(sp, j + E, expert(j + 1), expert(j))
            e = expert(n)
            for k, q in ((2, 4), (3, 5)):
                sp_load(sp, n + E, k, q, e)

        @block.scalar
        def _(act):
            pipeline(act, act_step, act_tail)

        @block.vector
        def _(dve):
            pipeline(dve, dve_step, dve_tail)

        @block.gpsimd
        def _(pool):
            pipeline(pool, pool_step, pool_tail)

        @block.tensor
        def _(pe):
            pipeline(pe, pe_step, lambda eng, c: pe_down(eng, c, True))


def combine(nc, m, L):
    with ExitStack() as ctx:
        rows = ctx.enter_context(nc.sbuf_tensor(f"k{L}_rows", [P, NT, 2, D], F32))
        junk = ctx.enter_context(nc.sbuf_tensor(f"k{L}_junk", [P, D], F32))
        s_in = [m.sem(f"k{L}_in{t}") for t in range(NT)]
        s_add, s_sq = m.sem(f"k{L}_added"), m.sem(f"k{L}_squares")
        block = ctx.enter_context(nc.Block())

        @block.scalar
        def _(act):
            sum_squares(act, m, s_sq, junk[:], lambda t: act.wait_ge(s_add, 2 * t + 2))

        @block.gpsimd
        def _(pool):
            for t in range(NT):
                for k in range(2):
                    pool.indirect_dma_start(out=rows[:, t, k, :], out_offset=None, in_=m.slots_y[:, :],
                                            in_offset=bass.IndirectOffsetOnAxis(ap=m.idx[:, t, k:k + 1], axis=0)
                                            ).then_inc(s_in[t], 16)

        @block.vector
        def _(dve):
            for t in range(NT):
                dve.wait_ge(s_in[t], 32)
                for k in range(2):
                    dve.scalar_tensor_tensor(out=m.x[:, t, :], in0=rows[:, t, k, :], scalar=m.wts[:, t, k:k + 1],
                                             in1=m.x[:, t, :], op0=ALU.mult, op1=ALU.add).then_inc(s_add, 1)
                    dve.wait_ge(s_add, 2 * t + k + 1)


def final_norm(nc, m):
    with ExitStack() as ctx:
        gb = ctx.enter_context(nc.sbuf_tensor("f_gb", [P, D], F32))
        y = ctx.enter_context(nc.sbuf_tensor("f_y", [P, NT, D], F32))
        tmp = ctx.enter_context(nc.sbuf_tensor("f_tmp", [P, NT], F32))
        nrm = Norm(m, "f", 4)
        s_gb, s_out = m.sem("f_gain_in"), m.sem("f_out")
        block = ctx.enter_context(nc.Block())
        out = m.out.rearrange("b (t p) d -> t p (b d)", p=P)

        @block.sync
        def _(sp):
            sp.dma_start(gb[:], m.a["norm_final"].rearrange("(a d) -> a d", a=1).broadcast_to([P, D])).then_inc(s_gb, 16)
            for t in range(NT):
                sp.wait_ge(nrm.xn, t + 1)
                sp.dma_start(out[t], y[:, t, :]).then_inc(s_out, 16)
            sp.wait_ge(s_out, 16 * NT)

        @block.scalar
        def _(act):
            nrm.scalar_root(act)

        @block.vector
        def _(dve):
            nrm.vector_stats(dve, tmp[:])
            dve.wait_ge(s_gb, 16)
            for t in range(NT):
                dve.scalar_tensor_tensor(out=y[:, t, :], in0=m.x[:, t, :], scalar=m.rstd[:, 4, t:t + 1], in1=gb[:],
                                         op0=ALU.mult, op1=ALU.mult).then_inc(nrm.xn, 1)


N_SHARED = 2


def shared_kv(nc, m, ctx):

    def keep(name, shape, dt=F32):
        return ctx.enter_context(nc.sbuf_tensor("a_" + name, shape, dt))

    m.kT = keep("kT", [P, 2, NG, S])
    m.v = keep("v", [P, NT, 2, NG, 2, HD], F32R)
    m.q = keep("q", [P, NK, S])
    m.qr = keep("qr", [P, NK, S])
    m.gates = keep("gates", [P, NT, NH, NBR])
    m.kc = keep("kc", [P, NG, NBLK])
    m.vc = keep("vc", [P, NG, 2, 2 * HD])
    m.w1_in = m.sem("a_w1_in")
    with ExitStack() as both:
        def shared(name, shape):
            return both.enter_context(nc.sbuf_tensor("c2_" + name, shape, F32))

        z = Mem()
        z.cvT = shared("cvT", [P, 2, 2, S])
        z.pos = shared("pos", [P, 2, NJ])
        z.w2 = shared("w2", [P, 2, 2, HD])
        z.w1 = [m.raw[:, r:r + 2, :].rearrange("p h (j n) -> p (h j) n", n=HID) for r in (4, 2)]
        z.hkv = shared("hkv", [P, NK, S])
        z.blk = z.hkv[:].rearrange("p k s -> p (k s)")[:, 0:2 * NJ * NG * NCMP].rearrange(
            "p (i j g c) -> p i j g c", i=2, j=NJ, g=NG)
        for stage, letter in ((norm_and_project, "b_"), (compress, "z_")):
            with ExitStack() as tmp:
                def sb(name, shape, dt=F32):
                    return tmp.enter_context(nc.sbuf_tensor(letter + name, shape, dt))

                stage(nc, m, sb, z)


def norm_and_project(nc, m, sb, z):
    a = m.a
    NF = 4 + 4 + 8
    hkv, cvT = z.hkv, z.cvT
    two = sb("two", [P, NG, S])
    hq = sb("hq", [P, NK, S])
    gain = sb("gain", [P, 2, NK])
    wk = m.raw[:, 0:2, :].rearrange("p b (k n) -> p b k n", k=NK)
    wv = m.raw[:, 2:4, :].rearrange("p b (k n) -> p b k n", k=NK)
    wg = sb("wg", [P, NK, NH * NBR])
    rope = sb("rope", [P, 2, S])
    perm = sb("perm", [P, P])
    raw = sb("rawk", [P, 2, S])
    prod = sb("prod", [P, 2, S])
    xn = m.qr[:].rearrange("p k s -> p (k s)").rearrange("p (t d) -> p t d", t=NT)
    small = sb("tmp", [P, NT])
    posi = sb("posi", [P, S], I32)
    freq = sb("freq", [P, 1])
    ang = m.qr[:, 0:3, :]
    gtmp = sb("gtmp", [P, NT, NH * NBR])
    nrm = Norm(m, "b", 2)
    s_gain, s_wg, s_z, s_two, s_pos = m.sem("b_gain_in"), m.sem("b_gate_w_in"), m.sem("b_cmp_in"), m.sem("b_two"), m.sem("b_pos_in")
    s_wk = [m.sem(f"b_wk{i}") for i in range(2)]
    s_wv = m.sem("b_wv_in")
    s_feat, s_tok = m.sem("b_features"), m.sem("b_tokens")
    s_raw, s_swap, s_rot = m.sem("b_raw"), m.sem("b_swapped"), m.sem("b_rotated")
    s_own, s_sin, s_ang, s_perm = m.sem("b_own2"), m.sem("b_sin"), m.sem("b_angles"), m.sem("b_perm")
    s_cv, s_v, s_g, s_ge = m.sem("b_cv"), m.sem("b_v"), m.sem("b_gate"), m.sem("b_gate_exp")
    cols = [("w_kv", 0), ("w_kv", 256), ("w_kv", 512), ("w_kv", 1024)] + [("attn_w_in", 256 * i) for i in range(4)]

    def weight(name, c, n):
        w = a[name] if name == "w_kv" else a[name][0]
        return w.rearrange("(p k) c -> p k c", k=NK)[:, :, c:c + n]

    rotated = list(range(4, NF))
    with nc.Block() as block:

        @block.sync
        def _(sp):
            def feature_weights(n):
                name, c = cols[n]
                sp.dma_start(wk[:, n % 2, :, :], weight(name, c, 256)).then_inc(s_wk[n % 2], 16)

            with nc.allow_non_contiguous_dma(reason="small vectors"):
                sp.dma_start(gain[:, 0, :], a["norm_kv"].rearrange("(p k) -> p k", k=NK)).then_inc(s_gain, 16)
                sp.dma_start(gain[:, 1, :], a["norm_mix"][1].rearrange("(p k) -> p k", k=NK)).then_inc(s_gain, 16)
                feature_weights(0)
                feature_weights(1)
                sp.dma_start(posi[:], a["positions"].broadcast_to([P, S])).then_inc(s_pos, 16)
                for i in range(4):
                    sp.dma_start(freq[32 * i:32 * i + 32, :], a["inv_freq"].rearrange("(p a) -> p a", a=1)
                                 ).then_inc(s_pos, 16)
                sp.dma_start(wv[:, 0, :, :], weight("w_kv", 768, 256)).then_inc(s_wv, 16)
                sp.dma_start(wv[:, 1, :, :], weight("w_kv", 1280, 256)).then_inc(s_wv, 16)
                sp.dma_start(wg[:], weight("attn_w_in", NH * HD, NH * NBR)).then_inc(s_wg, 16)
                for i, c in enumerate("kv"):
                    sp.dma_start(z.w2[:, i], a[f"cmp_w2_{c}"].rearrange("(k p) n -> p k n", p=P)).then_inc(s_z, 16)
                    sp.dma_start(z.pos[:, i], a[f"cmp_pos_{c}"].rearrange("(j two) d -> (two d) j", two=2)
                                 ).then_inc(s_z, 16)
                sp.dma_start(m.raw[:, 4:6, :].rearrange("p h (j n) -> p (h j) n", n=HID),
                             a["cmp_w1_k"].rearrange("(j p) n -> p j n", p=P)).then_inc(m.w1_in, 16)
            for n in range(2, len(cols)):
                sp.wait_ge(s_feat, 2 * (n - 1))
                feature_weights(n)
            sp.wait_ge(s_tok, NT)
            sp.dma_start(m.raw[:, 2:4, :].rearrange("p h (j n) -> p (h j) n", n=HID),
                         a["cmp_w1_v"].rearrange("(j p) n -> p j n", p=P)).then_inc(m.w1_in, 16)

        @block.gpsimd
        def _(pool):
            for i in range(4):
                o = 32 * (i ^ 1)
                p = pool.tensor_copy(perm[:, 32 * i:32 * i + 32], m.ident[:, o:o + 32])
            p.then_inc(s_perm, 1)

        @block.scalar
        def _(act):
            nrm.scalar_root(act)
            act.wait_ge(s_gain, 32)
            nrm.evacuate(act, 0, [(hkv, gain[:, 0, :]), (hq, gain[:, 1, :])])
            act.wait_ge(s_ang, 1)
            act.activation(rope[:, 0, :], ang[:, 1, :], ACT.Sin).then_inc(s_sin, 1)
            act.activation(rope[:, 1, :], ang[:, 0, :], ACT.Sin).then_inc(s_sin, 1)
            for i in range(NF):
                act.wait_ge(s_feat, i + 1)
                if i < 4:
                    act.activation(cvT[:, i // 2, i % 2, :], m.ps[i % 4][:], ACT.Copy).then_inc(s_raw, 1)
                else:
                    if i >= 6 and i < 8:
                        act.wait_ge(s_rot, i - 5)
                    dst = raw[:, i % 2, :] if i < 8 else m.q[:, i - 8, :]
                    act.activation(dst, m.ps[i % 4][:], ACT.Copy).then_inc(s_raw, 1)
            for t in range(NT):
                act.wait_ge(s_g, t + 1)
            act.activation(gtmp[:], gtmp[:], ACT.Exp, scale=-1.0).then_inc(s_ge, 1)

        @block.vector
        def _(dve):
            own = Chain(dve, s_own)
            nrm.vector_stats(dve, small[:])
            nrm.vector_normed(dve, xn)
            dve.wait_ge(s_gain, 32)
            nrm.evacuate(dve, 1, [(hkv, gain[:, 0, :]), (hq, gain[:, 1, :])])
            dve.wait_ge(s_pos, 16 * 5)
            a0, a1, a2 = (ang[:, i, :] for i in range(3))
            own.step(dve.tensor_copy(a1, posi[:]))
            own.step(dve.tensor_scalar(a0, a1, freq[:, 0:1], None, ALU.mult))
            own.step(dve.tensor_scalar(a1, a0, 1.0 / (2 * PI), MAGIC, ALU.mult, ALU.add))
            own.step(dve.tensor_scalar(a1, a1, MAGIC, None, ALU.subtract))
            own.step(dve.scalar_tensor_tensor(out=a0, in0=a1, scalar=-TWO_PI[0], in1=a0, op0=ALU.mult, op1=ALU.add))
            own.step(dve.scalar_tensor_tensor(out=a0, in0=a1, scalar=-TWO_PI[1], in1=a0, op0=ALU.mult, op1=ALU.add))
            own.step(dve.scalar_tensor_tensor(out=a0, in0=a1, scalar=-TWO_PI[2], in1=a0, op0=ALU.mult, op1=ALU.add))
            own.step(dve.tensor_scalar(a0, a0, PI32, -PI32, ALU.min, ALU.max))
            own.step(dve.tensor_scalar(a2, a0, -1.0, None, ALU.mult))
            own.step(dve.tensor_tensor(a2, a2, a0, ALU.max))
            dve.tensor_scalar(a1, a2, -1.0, PI / 2, ALU.mult, ALU.add).then_inc(s_ang, 1)
            dve.wait_ge(s_sin, 2)
            for i in (0, 2):
                own.step(dve.tensor_scalar(rope[32 * i:32 * i + 32, 1, :], rope[32 * i:32 * i + 32, 1, :], -1.0, None,
                                           ALU.mult))
            def shift(kind):
                for g in range(NG):
                    src = cvT[64 * (g % 2):64 * (g % 2) + 64, kind, g // 2, :]
                    dve.tensor_copy(two[0:64, g, :], src)
                    c = dve.tensor_copy(two[64:P, g, 0:S - 1], src[:, 1:S])
                c.then_inc(s_two, 1)

            def blocks(kind):
                dve.wait_ge(s_tok, NT)
                dve.wait_ge(s_z, 64)
                dve.wait_ge(s_two, kind + 1)
                for j in range(NJ):
                    src = two[:, :, 2 * j:2 * j + (NCMP - 1) * STRIDE + 1:STRIDE]
                    dve.tensor_scalar(z.blk[:, kind, j], src, z.pos[:, kind, j:j + 1], None, ALU.add)

            for j, i in enumerate(rotated):
                src = raw[:, i % 2, :] if i < 8 else m.q[:, i - 8, :]
                dve.wait_ge(s_raw, i + 1)
                dve.tensor_tensor(prod[:, 0, :], src, rope[:, 0, :], ALU.mult).then_inc(s_v, 1)
                dve.wait_ge(s_swap, j + 1)
                own.step(dve.tensor_tensor(prod[:, 1, :], m.ps[4 + j % 2][:], rope[:, 1, :], ALU.mult))
                dve.wait_ge(s_v, j + 1)
                if i < 8:
                    br, g0 = (i - 4) // 2, 2 * (i % 2)
                    for g in range(2):
                        rows = slice(64 * g, 64 * g + 64)
                        for to in range(2):
                            r = dve.tensor_tensor(m.kT[64 * to:64 * to + 64, br, g0 + g, :], prod[rows, 0, :],
                                                  prod[rows, 1, :], ALU.add)
                else:
                    r = dve.tensor_tensor(m.qr[:, i - 8, :], prod[:, 0, :], prod[:, 1, :], ALU.add)
                r.then_inc(s_rot, 1)
                dve.wait_ge(s_rot, j + 1)
                if i in (7, 9):
                    shift((i - 7) // 2)
                if i in (8, 10):
                    blocks((i - 8) // 2)
                if i == 6:
                    for t in range(NT):
                        dve.wait_ge(s_tok, t + 1)
                        v_hi, v_lo = m.v[:, t, :, :, 0, :], m.v[:, t, :, :, 1, :]
                        src = m.ps[6][:].rearrange("p (b g d) -> p b g d", b=2, g=NG)
                        dve.tensor_copy(v_hi, src).then_inc(s_cv, 1)
                        dve.wait_ge(s_cv, t + 1)
                        dve.tensor_tensor(v_lo, src, v_hi.bitcast(F32), ALU.subtract)
                        dve.tensor_copy(gtmp[:, t, :], m.ps[7][:, 0:NH * NBR]).then_inc(s_g, 1)
            dve.wait_ge(s_ge, 1)
            own.step(dve.tensor_scalar(gtmp[:], gtmp[:], 1.0, None, ALU.add))
            own.step(dve.reciprocal(m.gates[:].rearrange("p t h b -> p t (h b)"), gtmp[:]))

        @block.tensor
        def _(pe):
            nrm.tensor(pe, xn)
            nrm.wait_hT(pe)

            def swap(j):
                i = rotated[j]
                src = raw[:, i % 2, :] if i < 8 else m.q[:, i - 8, :]
                pe.wait_ge(s_raw, i + 1)
                if j == 0:
                    pe.wait_ge(s_perm, 1)
                if j >= 2:
                    pe.wait_ge(s_rot, j - 1)
                pe.matmul(m.ps[4 + j % 2][:], perm[:], src, start=True, stop=True).then_inc(s_swap, 1)

            def token_major():
                pe.wait_ge(s_wv, 32)
                pe.wait_ge(s_wg, 16)
                for t in range(NT):
                    if t:
                        pe.wait_ge(s_g, t)
                    for k in range(NK):
                        pe.matmul(m.ps[6][:].rearrange("p (b c) -> p b c", b=2), hkv[:, k, t * P:(t + 1) * P], wv[:, :, k, :],
                                  start=(k == 0), stop=(k == NK - 1))
                    for k in range(NK):
                        mm = pe.matmul(m.ps[7][:, 0:NH * NBR], hq[:, k, t * P:(t + 1) * P], wg[:, k, :],
                                       start=(k == 0), stop=(k == NK - 1))
                    mm.then_inc(s_tok, 1)

            for i in range(NF):
                n = i // 2
                pe.wait_ge(s_wk[n % 2], 16 * (n // 2 + 1))
                if i >= 4:
                    pe.wait_ge(s_raw, i - 3)
                h = hkv if i < 8 else hq
                for k in range(NK):
                    mm = pe.matmul(m.ps[i % 4][:], wk[:, n % 2, k, (i % 2) * P:(i % 2 + 1) * P], h[:, k, :],
                                   start=(k == 0), stop=(k == NK - 1))
                mm.then_inc(s_feat, 1)
                if i >= 5:
                    swap(i - 5)
                if i == 7:
                    token_major()
            swap(len(rotated) - 1)


def compress(nc, m, sb, z):
    NB = NG * NCMP
    w1, w2, blk = z.w1, z.w2, z.blk
    hid = sb("hid", [P, 2, HID])
    t1 = sb("t1", [P, 2, HID])
    hT = sb("hidT", [P, 2, 2, NB])
    s_hid, s_hs = m.sem("z_hidden"), m.sem("z_hid_sb")
    s_th, s_gelu, s_tr, s_hT, s_out = (m.sem(n) for n in ("z_tanh", "z_gelu", "z_tr", "z_hT", "z_out"))
    s_own, s_kc = m.sem("z_own"), m.sem("z_kc")
    with nc.Block() as block:

        @block.vector
        def _(dve):
            own = Chain(dve, s_own)
            own.step(dve.memset(m.kc[:], 0.0))
            own.step(dve.memset(m.vc[:], 0.0))
            for i in range(2):
                dve.wait_ge(s_hid, i + 1)
                h, t = hid[0:NB, i, :], t1[0:NB, i, :]
                own.step(dve.tensor_copy(h, m.ps[i][0:NB, 0:HID]))
                own.step(dve.tensor_tensor(t, h, h, ALU.mult))
                own.step(dve.tensor_scalar(t, t, 0.044715, 1.0, ALU.mult, ALU.add))
                dve.tensor_tensor(t, t, h, ALU.mult).then_inc(s_hs, 1)
            for i in range(2):
                h, t = hid[0:NB, i, :], t1[0:NB, i, :]
                dve.wait_ge(s_th, i + 1)
                own.step(dve.tensor_scalar(t, t, 1.0, 0.5, ALU.add, ALU.mult))
                dve.tensor_tensor(h, h, t, ALU.mult).then_inc(s_gelu, 1)
            for i in range(2):
                dve.wait_ge(s_tr, i + 1)
                dve.tensor_copy(hT[:, i], m.ps[2 + i][:, 0:2 * NB].rearrange("p (k n) -> p k n", k=2)).then_inc(s_hT, 1)
            dve.wait_ge(s_out, 1)
            for to in range(2):
                dve.tensor_copy(m.kc[64 * to:64 * to + 64, :, 0:NCMP],
                                m.ps[4][0:64, 0:NB].rearrange("p (g c) -> p g c", g=NG)).then_inc(s_kc, 1)
            dve.wait_ge(s_out, 2)
            for h in range(HPG):
                dve.tensor_copy(m.vc[NBLK * h:NBLK * h + NCMP, :, h // 2, (h % 2) * HD:(h % 2 + 1) * HD],
                                m.ps[5][0:NCMP, 0:NG * HD].rearrange("p (g d) -> p g d", g=NG)).then_inc(s_kc, 1)

        @block.scalar
        def _(act):
            for i in range(2):
                act.wait_ge(s_hs, i + 1)
                act.activation(t1[0:NB, i, :], t1[0:NB, i, :], ACT.Tanh, scale=(2 / PI) ** 0.5).then_inc(s_th, 1)

        @block.tensor
        def _(pe):
            pe.wait_ge(m.w1_in, 32)
            for i in range(2):
                for j in range(NJ):
                    mm = pe.matmul(m.ps[i][0:NB, 0:HID], blk[:, i, j].rearrange("p g c -> p (g c)"), w1[i][:, j, :],
                                   start=(j == 0), stop=(j == NJ - 1))
                mm.then_inc(s_hid, 1)
            for i in range(2):
                pe.wait_ge(s_gelu, i + 1)
                for k in range(2):
                    tr = pe.transpose(m.ps[2 + i][:, k * NB:(k + 1) * NB], hid[0:NB, i, k * P:(k + 1) * P],
                                      m.ident[0:NB, 0:NB])
                tr.then_inc(s_tr, 1)
            pe.wait_ge(s_hT, 2)
            for k in range(2):
                mm = pe.matmul(m.ps[4][0:64, 0:NB], w2[:, 0, k, :], hT[:, 0, k, :], start=(k == 0), stop=(k == 1))
            mm.then_inc(s_out, 1)
            for g in range(NG):
                for k in range(2):
                    mm = pe.matmul(m.ps[5][0:NCMP, g * HD:(g + 1) * HD], hT[:, 1, k, g * NCMP:(g + 1) * NCMP],
                                   w2[:, 1, k, :], start=(k == 0), stop=(k == 1))
            mm.then_inc(s_out, 1)


def attention(nc, m):
    a = m.a
    with ExitStack() as ctx:
        def sb(name, shape, dt=F32):
            return ctx.enter_context(nc.sbuf_tensor("t_" + name, shape, dt))

        causal = sb("causal", [P, P], BF16)
        cmask = sb("cmask", [P, NT, NBLK])
        zero = sb("zero", [P, P])
        oT = m.q
        wout = m.raw[:, 0:4, :].rearrange("p q (j n) -> p (q j) n", n=D)
        pr = sb("pr", [P, 3, HPG, S])
        prT_hi = sb("prT_hi", [P, 2, NT, HPG * P], F32R)
        prT_lo = sb("prT_lo", [P, 2, NT, HPG * P], F32R)
        pc = sb("pc", [P, 2, NH, NBLK])
        pcT = sb("pcT", [P, 2, NG, P])
        cmx = sb("cmx", [P, 2, NH])
        csm = sb("csm", [P, 2, NH])
        mx = sb("mx", [P, 2, HPG])
        sm = sb("sm", [P, 3, HPG])
        s_wo, s_mask, s_z = m.sem("t_wout_in"), m.sem("t_masks"), m.sem("t_zero")
        s_csc, s_cmx, s_cex, s_cpn = (m.sem("t_cmp_" + n) for n in ("scores", "shifted", "exp", "scaled"))
        s_ctr, s_cT, s_cpv, s_co = (m.sem("t_cmp_" + n) for n in ("tr", "pT", "pv", "out"))
        s_sc, s_mx, s_ex, s_factor = m.sem("t_scores"), m.sem("t_max"), m.sem("t_exp"), m.sem("t_factor")
        s_scaled = [m.sem("t_scaled_dve"), m.sem("t_scaled_act")]
        BY_ACT = (1, 2, 3)
        s_tr, s_pv, s_oT = m.sem("t_tr"), m.sem("t_pv"), m.sem("t_oT")
        s_prT_hi, s_prT_lo = m.sem("t_prT_hi"), m.sem("t_prT_lo")
        s_own, s_o, s_res, s_sq = m.sem("t_own"), m.sem("t_out"), m.sem("t_res"), m.sem("t_squares")
        steps = [(t, g, b) for t in range(NT) for g in range(NG) for b in range(N_SHARED)]
        before = [sum(t + 1 for t, g, b in steps[:i]) for i in range(len(steps) + 1)]

        def half_of(i, half):
            n = steps[i][0] + 1
            return range((n + 1) // 2) if half == 0 else range((n + 1) // 2, n)

        block = ctx.enter_context(nc.Block())

        @block.sync
        def _(sp):
            sp.dma_start(wout[:], a["attn_w_out"][0].rearrange("(j p) n -> p j n", p=P)).then_inc(s_wo, 16)
            prefetch(sp, m, 1, (4, 5))
            sp.wait_ge(s_o, 2 * NT)
            prefetch(sp, m, 1, (0, 1, 2, 3))

        @block.gpsimd
        def _(pool):
            pool.memset(zero[:], 0.0).then_inc(s_z, 1)
            pool.wait_ge(s_z, 1)
            pool.affine_select(out=causal[:], in_=zero[:], compare_op=ALU.is_ge, fill=NEG, base=0,
                               pattern=[[-1, P]], channel_multiplier=1).then_inc(s_mask, 1)
            for t in range(NT):
                pool.affine_select(out=cmask[:, t, :], in_=zero[:, 0:NBLK], compare_op=ALU.is_ge, fill=NEG,
                                   base=t * P - (CMP - 1), pattern=[[-STRIDE, NBLK]],
                                   channel_multiplier=1).then_inc(s_mask, 1)

        @block.tensor
        def _(pe):
            def cmp_scores(t):
                if t >= 2:
                    pe.wait_ge(s_cmx, t - 1)
                for head in range(NH):
                    rows = slice(64 * (head % 2), 64 * (head % 2) + 64)
                    mm = pe.matmul(m.ps[2 * (t % 2) + head % 2][:, head // 2 * NBLK:(head // 2 + 1) * NBLK],
                                   m.q[rows, head // 2, t * P:(t + 1) * P], m.kc[rows, head // HPG, :],
                                   start=True, stop=True)
                    if head >= NH - 2:
                        mm.then_inc(s_csc, 1)

            def cmp_values(t):
                pe.wait_ge(s_cpn, t + 1)
                if t >= 2:
                    pe.wait_ge(s_cT, t - 1)
                for g in range(NG):
                    tr = pe.transpose(m.ps[4 + t % 2][:, g * P:(g + 1) * P],
                                      pc[:, t % 2, g * HPG:(g + 1) * HPG, :].rearrange("p h c -> p (h c)"), m.ident[:])
                tr.then_inc(s_ctr, 1)

            def cmp_product(t):
                pe.wait_ge(s_cT, t + 1)
                if t:
                    pe.wait_ge(s_co, t)
                for g in range(NG):
                    for pair in range(2):
                        i = 2 * g + pair
                        mm = pe.matmul(m.ps[6 + i // 4][:, (i % 4) * P:(i % 4 + 1) * P],
                                       m.vc[:, g, pair, :], pcT[:, t % 2, g, :], start=True, stop=True)
                mm.then_inc(s_cpv, 1)

            for t in range(NT + 2):
                if t < NT:
                    cmp_scores(t)
                if 1 <= t <= NT:
                    cmp_values(t - 1)
                if t >= 2:
                    cmp_product(t - 2)
            pe.wait_ge(s_mask, 1 + NT)

            def scores(i, pair):
                t, g, b = steps[i]
                n = (t + 1) * P
                if i:
                    pe.wait_ge(s_ex, HPG * (i - 1) + 2 * pair + 2)
                elif pair == 0:
                    pe.wait_ge(s_co, NT)
                for h in (2 * pair, 2 * pair + 1):
                    rows = slice(64 * (h % 2), 64 * (h % 2) + 64)
                    pe.matmul(m.ps[h][:, 0:n], m.qr[rows, (g * HPG + h) // 2, t * P:(t + 1) * P],
                              m.kT[rows, b, g, 0:n], start=True, stop=False)
                for h in (2 * pair, 2 * pair + 1):
                    pe.matmul(m.ps[h][:, t * P:n], m.identb[:], causal[:], start=False, stop=True).then_inc(s_sc, 1)

            def values(i, half):
                for j in half_of(i, half):
                    n = before[i] + j
                    if n >= 2:
                        pe.wait_ge(s_prT_lo, n - 1)
                    for h in range(HPG):
                        if j == 0:
                            same = [x for x in range(HPG) if (x in BY_ACT) == (h in BY_ACT)]
                            pe.wait_ge(s_scaled[h in BY_ACT], len(same) * i + same.index(h) + 1)
                        tr = pe.transpose(m.ps[4 + n % 2][:, h * P:(h + 1) * P], pr[:, i % 3, h, j * P:(j + 1) * P],
                                          m.ident[:])
                    tr.then_inc(s_tr, 1)

            def product(i, half):
                t, g, b = steps[i]
                o = i // N_SHARED
                if b == 0 and o >= 2 and half == 0:
                    pe.wait_ge(s_oT, o - 1)
                for j in half_of(i, half):
                    n = before[i] + j
                    pe.wait_ge(s_prT_lo, n + 1)
                    for p in (prT_hi, prT_lo):
                        mm = pe.matmul(m.ps[6 + o % 2][:], m.v[:, j, b, g, :, :].rearrange("p h d -> p (h d)"),
                                       p[:, i % 2, j, :], start=(b == 0 and j == 0 and p is prT_hi),
                                       stop=(b == N_SHARED - 1 and j == t and p is prT_lo))
                    if j == t:
                        mm.then_inc(s_pv, 1)

            for i in range(len(steps) + 3):
                for half in range(2):
                    if i < len(steps):
                        scores(i, half)
                    if 2 <= i < len(steps) + 2:
                        values(i - 2, half)
                    if i >= 3:
                        product(i - 3, half)
            pe.wait_ge(s_wo, 16)
            pe.wait_ge(s_oT, len(steps) // N_SHARED)
            project_out(pe, m, oT, wout, s_o)

        @block.vector
        def _(dve):
            own = Chain(dve, s_own)
            dve.wait_ge(s_mask, 1 + NT)

            def per_head(x):
                return x.unsqueeze(2).broadcast_to([P, NH, NBLK])

            def cmp_shift(t):
                dve.wait_ge(s_csc, 2 * t + 2)
                if t >= 2:
                    dve.wait_ge(s_ctr, t - 1)
                p, mxs = pc[:, t % 2, :, :], cmx[:, t % 2, :]
                for odd in range(2):
                    own.step(dve.tensor_tensor(
                        p[:, odd::2, :], m.ps[2 * (t % 2) + odd][:, 0:NH // 2 * NBLK].rearrange("p (h c) -> p h c", c=NBLK),
                        cmask[:, t, :].unsqueeze(1).broadcast_to([P, NH // 2, NBLK]), ALU.add))
                own.step(dve.tensor_reduce(mxs, p, AX.X, ALU.max))
                own.step(dve.tensor_scalar(mxs, mxs, 0.1 * NEG, None, ALU.max))
                dve.tensor_tensor(p, p, per_head(mxs), ALU.subtract).then_inc(s_cmx, 1)

            def cmp_scale(t):
                dve.wait_ge(s_cex, t + 1)
                p, sums = pc[:, t % 2, :, :], csm[:, t % 2, :]
                own.step(dve.tensor_reduce(sums, p, AX.X, ALU.add))
                own.step(dve.tensor_scalar(sums, sums, 1e-30, None, ALU.max))
                own.step(dve.reciprocal(sums, sums))
                own.step(dve.tensor_tensor(sums, sums, m.gates[:, t, :, 0], ALU.mult))
                dve.tensor_tensor(p, p, per_head(sums), ALU.mult).then_inc(s_cpn, 1)

            for t in range(NT + 1):
                if t:
                    cmp_scale(t - 1)
                if t < NT:
                    cmp_shift(t)

            def maxima(i, pair):
                t, g, b = steps[i]
                for h in (2 * pair, 2 * pair + 1):
                    dve.wait_ge(s_sc, HPG * i + h + 1)
                    top = dve.tensor_reduce(mx[:, i % 2, h:h + 1], m.ps[h][:, 0:(t + 1) * P], AX.X, ALU.max)
                own.step(top)
                pair_mx = mx[:, i % 2, 2 * pair:2 * pair + 2]
                dve.tensor_scalar(pair_mx, pair_mx, -SCALE, None, ALU.mult).then_inc(s_mx, 1)

            def scale(i):
                t, g, b = steps[i]
                dve.wait_ge(s_ex, HPG * (i + 1))
                own.step(dve.tensor_scalar(sm[:, i % 3, :], sm[:, i % 3, :], 1e-30, None, ALU.max))
                own.step(dve.reciprocal(sm[:, i % 3, :], sm[:, i % 3, :]))
                dve.tensor_tensor(sm[:, i % 3, :], sm[:, i % 3, :], m.gates[:, t, g * HPG:(g + 1) * HPG, 1 + b],
                                  ALU.mult).then_inc(s_factor, 1)
                dve.wait_ge(s_factor, i + 1)
                for h in range(HPG):
                    if h not in BY_ACT:
                        p = pr[:, i % 3, h, 0:(t + 1) * P]
                        dve.tensor_scalar(p, p, sm[:, i % 3, h:h + 1], None, ALU.mult).then_inc(s_scaled[0], 1)

            def low_parts(i, half):
                for j in half_of(i, half):
                    n = before[i] + j
                    dve.wait_ge(s_prT_hi, n + 1)
                    dve.tensor_tensor(prT_lo[:, i % 2, j, :], m.ps[4 + n % 2][:], prT_hi[:, i % 2, j, :].bitcast(F32),
                                      ALU.subtract).then_inc(s_prT_lo, 1)

            def out(o):
                t, g = o // NG, o % NG
                dve.wait_ge(s_pv, N_SHARED * (o + 1))
                dve.wait_ge(s_co, t + 1)
                for part in range(2):
                    src = m.ps[6 + o % 2][HD * part:HD * part + HD, :].rearrange("p (j two q) -> p j two q", j=2, two=2)
                    for odd in range(2):
                        dst = oT[64 * odd:64 * odd + 64, 2 * g:2 * g + 2, t * P:(t + 1) * P]
                        c = dve.tensor_tensor(dst, src[:, :, odd, :], dst, ALU.add)
                    if part == 0:
                        own.step(c)
                c.then_inc(s_oT, 1)

            for i in range(len(steps) + 3):
                for half in range(2):
                    if i < len(steps):
                        maxima(i, half)
                    if half == 0 and 1 <= i <= len(steps):
                        scale(i - 1)
                    if 2 <= i < len(steps) + 2:
                        low_parts(i - 2, half)
                if i >= 4 and (i - 4) % N_SHARED == 0:
                    out((i - 4) // N_SHARED)
            add_residual(dve, m, s_o, s_res)

        @block.scalar
        def _(act):
            def cmp_exp(t):
                act.wait_ge(s_cmx, t + 1)
                act.activation(pc[:, t % 2, :, :], pc[:, t % 2, :, :], ACT.Exp, scale=SCALE).then_inc(s_cex, 1)

            def cmp_transposed(t):
                act.wait_ge(s_ctr, t + 1)
                if t >= 2:
                    act.wait_ge(s_cpv, t - 1)
                act.activation(pcT[:, t % 2, :, :].rearrange("p g q -> p (g q)"), m.ps[4 + t % 2][:],
                               ACT.Copy).then_inc(s_cT, 1)

            def cmp_out(t):
                act.wait_ge(s_cpv, t + 1)
                for i in range(2):
                    c = act.activation(oT[:, 4 * i:4 * i + 4, t * P:(t + 1) * P],
                                       m.ps[6 + i][:].rearrange("p (j q) -> p j q", j=4), ACT.Copy)
                c.then_inc(s_co, 1)

            for t in range(NT + 2):
                if t < NT:
                    cmp_exp(t)
                if 1 <= t <= NT:
                    cmp_transposed(t - 1)
                if t >= 2:
                    cmp_out(t - 2)

            def exps(i, pair):
                t, g, b = steps[i]
                if i >= 3 and pair == 0:
                    act.wait_ge(s_tr, before[i - 2])
                n = (t + 1) * P
                act.wait_ge(s_mx, 2 * i + pair + 1)
                for h in (2 * pair, 2 * pair + 1):
                    act.activation(pr[:, i % 3, h, 0:n], m.ps[h][:, 0:n], ACT.Exp, bias=mx[:, i % 2, h:h + 1],
                                   scale=SCALE, accum_out=sm[:, i % 3, h:h + 1]).then_inc(s_ex, 1)

            def scale_by_act(i):
                act.wait_ge(s_factor, i + 1)
                for h in BY_ACT:
                    p = pr[:, i % 3, h, 0:(steps[i][0] + 1) * P]
                    act.activation(p, p, ACT.Copy, scale=sm[:, i % 3, h:h + 1]).then_inc(s_scaled[1], 1)

            def high_parts(i, half):
                if i >= 2 and half == 0:
                    act.wait_ge(s_pv, i - 1)
                for j in half_of(i, half):
                    n = before[i] + j
                    act.wait_ge(s_tr, n + 1)
                    act.activation(prT_hi[:, i % 2, j, :], m.ps[4 + n % 2][:], ACT.Copy).then_inc(s_prT_hi, 1)

            for i in range(len(steps) + 2):
                for half in range(2):
                    if i >= 2:
                        high_parts(i - 2, half)
                    if half == 1 and 1 <= i <= len(steps):
                        scale_by_act(i - 1)
                    if i < len(steps):
                        exps(i, half)
            sum_squares(act, m, s_sq, pc[:].rearrange("p b h c -> p (b h c)"), lambda t: act.wait_ge(s_res, 2 * t + 2))


_INS = ["x", "positions", "norm_mix", "norm_ffn", "conv_w_in", "conv_w", "conv_w_out", "norm_kv", "w_kv",
        "cmp_pos_k", "cmp_w1_k", "cmp_w2_k", "cmp_pos_v", "cmp_w1_v", "cmp_w2_v", "attn_w_in", "attn_w_out",
        "router_group_w", "router_group_b", "router_expert_w", "router_expert_b",
        "expert_w_gate", "expert_w_up", "expert_w_down", "norm_final"]


def kernel(**inputs):
    import numpy as np
    import concourse.bacc as bacc
    from concourse.bass_utils import run_bass_kernel_spmd

    nc = bacc.Bacc("TRN2", target_bir_lowering=False, num_devices=1)
    arrays = {f"in_{name}": np.ascontiguousarray(inputs[name]) for name in _INS}
    half = HD // 2
    arrays["in_inv_freq"] = (np.float32(10000.0) ** (-np.arange(half, dtype=np.float32) / np.float32(half)))
    a = {name[3:]: nc.dram_tensor(name, v.shape, mybir.dt.from_np(v.dtype), kind="ExternalInput").ap()
         for name, v in arrays.items()}
    out = nc.dram_tensor("out_0", (1, S, D), F32, kind="ExternalOutput").ap()
    program(nc, a, out)
    r = run_bass_kernel_spmd(nc, [arrays], core_ids=[0])
    return r.results[0]["out_0"]
```
